# Optimizing a Trainium2 kernel written in Bass

```python
import jax, jax.numpy as jnp
from jax import lax
import numpy as np

D_MODEL = 1024
BATCH = 1
SEQ = 1024
DEPTH = 1

D_MIX = D_MODEL
RET_HEADS = 8
RET_HEAD_DIM = 64
RET_WIDTH = RET_HEADS * RET_HEAD_DIM
RET_CHUNK = 128
ROPE_BASE = 10000.0
DSA_HEADS = 8
DSA_HEAD_DIM = 64
DSA_WIDTH = DSA_HEADS * DSA_HEAD_DIM
DSA_LATENT = 128
IDX_HEADS = 8
IDX_DIM = 64
IDX_TOPK_MAX = 256
Q_BLOCK = 128
PLE_DIM = 256
D_FF = -(-8 * D_MODEL // (3 * 256)) * 256
EPS = 1e-6
IN_COLS = 4 * RET_WIDTH + DSA_WIDTH + DSA_LATENT + IDX_HEADS * IDX_DIM + IDX_DIM + IDX_HEADS

kernel_name = "hymba_style_retention_dsa_hybrid"

def rms_norm(x, g):
    xf = x.astype(jnp.float32)
    y = xf * lax.rsqrt(jnp.mean(xf * xf, axis=-1, keepdims=True) + EPS)
    return (y * g.astype(jnp.float32)).astype(x.dtype)

def layer_norm(x, g, b):
    xf = x.astype(jnp.float32)
    mu = jnp.mean(xf, axis=-1, keepdims=True)
    var = jnp.mean(jnp.square(xf - mu), axis=-1, keepdims=True)
    y = (xf - mu) * lax.rsqrt(var + EPS)
    return (y * g.astype(jnp.float32) + b.astype(jnp.float32)).astype(x.dtype)

def rotate(x, positions):
    d = x.shape[-1]
    inv_freq = 1.0 / (ROPE_BASE ** (jnp.arange(0, d, 2, dtype=jnp.float32) / d))
    ang = positions.astype(jnp.float32)[:, :, None] * inv_freq
    cos = jnp.cos(ang)[:, :, None, :]
    sin = jnp.sin(ang)[:, :, None, :]
    xf = x.astype(jnp.float32)
    x1, x2 = xf[..., : d // 2], xf[..., d // 2:]
    return jnp.concatenate([x1 * cos - x2 * sin, x1 * sin + x2 * cos], axis=-1)

def retention_chunkwise(q, k, v):
    B, S, H, d = q.shape
    C = RET_CHUNK
    N = S // C
    log_g = jnp.log1p(-jnp.power(2.0, -5.0 - jnp.arange(H, dtype=jnp.float32)))
    q = q.astype(jnp.float32).reshape(B, N, C, H, d)
    k = (k.astype(jnp.float32) * (d ** -0.5)).reshape(B, N, C, H, d)
    v = v.astype(jnp.float32).reshape(B, N, C, H, d)
    i = jnp.arange(C, dtype=jnp.float32)
    diff = i[:, None] - i[None, :]
    decay = jnp.where(diff >= 0, jnp.exp(log_g[:, None, None] * jnp.maximum(diff, 0.0)), 0.0)
    scores = jnp.einsum('bnihd,bnjhd->bnhij', q, k) * decay
    intra = jnp.einsum('bnhij,bnjhe->bnihe', scores, v)
    zeta = jnp.exp(log_g[None, :] * (C - 1 - i)[:, None])
    kv = jnp.einsum('bnjhd,bnjhe->bnhde', k * zeta[None, None, :, :, None], v)
    chunk_decay = jnp.exp(log_g * C)[None, :, None, None]

    def step(R, kv_n):
        return chunk_decay * R + kv_n, R

    _, R_prev = lax.scan(step, jnp.zeros((B, H, d, d), jnp.float32), jnp.moveaxis(kv, 1, 0))
    R_prev = jnp.moveaxis(R_prev, 0, 1)
    xi = jnp.exp(log_g[None, :] * (i + 1.0)[:, None])
    cross = jnp.einsum('bnihd,bnhde->bnihe', q * xi[None, None, :, :, None], R_prev)
    return (intra + cross).reshape(B, S, H, d)

def dsa_sparse_attention(q_lat, c_kv, qi, ki, wi):
    B, S, H, C = q_lat.shape
    NB = S // Q_BLOCK
    topk = min(IDX_TOPK_MAX, S // 4)
    s_idx = jnp.arange(S)
    b_idx = jnp.arange(B)[:, None, None]

    def to_blocks(a):
        return jnp.moveaxis(a.reshape((B, NB, Q_BLOCK) + a.shape[2:]), 1, 0)

    def block(args):
        ql_b, qi_b, wi_b, start = args
        t = start + jnp.arange(Q_BLOCK)
        rel = jax.nn.relu(jnp.einsum('bthd,bsd->bths', qi_b, ki).astype(jnp.float32))
        iscore = jnp.einsum('bths,bth->bts', rel, wi_b.astype(jnp.float32))
        causal = s_idx[None, :] <= t[:, None]
        iscore = jnp.where(causal[None], iscore, -jnp.inf)
        _, sel = lax.top_k(iscore, topk)
        valid = sel <= t[None, :, None]
        kv_sel = c_kv[b_idx, sel]
        logits = jnp.einsum('bthc,btkc->bthk', ql_b, kv_sel).astype(jnp.float32)
        logits = jnp.where(valid[:, :, None, :], logits, -jnp.inf)
        probs = jax.nn.softmax(logits, axis=-1).astype(kv_sel.dtype)
        return jnp.einsum('bthk,btkc->bthc', probs, kv_sel)

    starts = jnp.arange(NB, dtype=jnp.int32) * Q_BLOCK
    o = lax.map(block, (to_blocks(q_lat), to_blocks(qi), to_blocks(wi), starts))
    return jnp.moveaxis(o, 0, 1).reshape(B, S, H, C)

def split_cols(proj):
    sizes = (RET_WIDTH,) * 4 + (DSA_WIDTH, DSA_LATENT, IDX_HEADS * IDX_DIM, IDX_DIM, IDX_HEADS)
    out, o = [], 0
    for sz in sizes:
        out.append(proj[..., o:o + sz])
        o += sz
    return out

def setup_inputs(seed: int = 0) -> dict:
    key = jax.random.key(seed)
    ks = jax.random.split(key, 24)
    f32 = jnp.float32

    def nrm(k, shape, fan_in):
        return jax.random.normal(k, shape, f32) * (fan_in ** -0.5)

    def gain(k, shape):
        return 1.0 + 0.02 * jax.random.normal(k, shape, f32)

    def bias(k, shape):
        return 0.02 * jax.random.normal(k, shape, f32)

    L = DEPTH
    x = jax.random.normal(ks[0], (BATCH, SEQ, D_MODEL), f32)
    p = jax.random.normal(ks[1], (DEPTH, BATCH, SEQ, PLE_DIM), f32)
    offsets = jax.random.randint(ks[2], (BATCH, 1), 0, 1024, dtype=jnp.int32)
    positions = offsets + jnp.arange(SEQ, dtype=jnp.int32)[None, :]
    return {
        "x": x,
        "p": p,
        "positions": positions,
        "pre_mix_g": gain(ks[3], (L, D_MODEL)),
        "w_in": nrm(ks[4], (L, D_MODEL, IN_COLS), D_MODEL),
        "ret_norm_g": gain(ks[5], (L, RET_HEADS, RET_HEAD_DIM)),
        "ret_norm_b": bias(ks[6], (L, RET_HEADS, RET_HEAD_DIM)),
        "kv_norm_g": gain(ks[7], (L, DSA_LATENT)),
        "idx_k_norm_g": gain(ks[8], (L, IDX_DIM)),
        "idx_k_norm_b": bias(ks[9], (L, IDX_DIM)),
        "w_uk": nrm(ks[10], (L, DSA_HEADS, DSA_HEAD_DIM, DSA_LATENT), DSA_HEAD_DIM),
        "w_uv": nrm(ks[11], (L, DSA_HEADS, DSA_LATENT, DSA_HEAD_DIM), DSA_LATENT),
        "w_out": nrm(ks[12], (L, D_MIX, D_MODEL), D_MIX),
        "post_mix_g": gain(ks[13], (L, D_MODEL)),
        "pre_ffn_g": gain(ks[14], (L, D_MODEL)),
        "w_ffn_gate": nrm(ks[15], (L, D_MODEL, D_FF), D_MODEL),
        "w_ffn_up": nrm(ks[16], (L, D_MODEL, D_FF), D_MODEL),
        "w_ffn_down": nrm(ks[17], (L, D_FF, D_MODEL), D_FF),
        "post_ffn_g": gain(ks[18], (L, D_MODEL)),
        "w_ple_up": nrm(ks[19], (L, PLE_DIM, D_MODEL), PLE_DIM),
        "w_ple_gate": nrm(ks[20], (L, D_MODEL, D_MODEL), D_MODEL),
        "ple_norm_g": gain(ks[21], (L, D_MODEL)),
    }

def reference(x, p, positions, pre_mix_g, w_in, ret_norm_g, ret_norm_b, kv_norm_g,
              idx_k_norm_g, idx_k_norm_b, w_uk, w_uv, w_out, post_mix_g, pre_ffn_g,
              w_ffn_gate, w_ffn_up, w_ffn_down, post_ffn_g, w_ple_up, w_ple_gate, ple_norm_g):
    B, S, _ = x.shape
    for i in range(DEPTH):
        h = rms_norm(x, pre_mix_g[i])
        proj = h @ w_in[i]
        r_q, r_k, r_v, r_g, a_q, a_c, i_q, i_k, i_w = split_cols(proj)

        rq = rotate(r_q.reshape(B, S, RET_HEADS, RET_HEAD_DIM), positions)
        rk = rotate(r_k.reshape(B, S, RET_HEADS, RET_HEAD_DIM), positions)
        rv = r_v.reshape(B, S, RET_HEADS, RET_HEAD_DIM)
        ry = retention_chunkwise(rq, rk, rv).astype(x.dtype)
        ry = layer_norm(ry, ret_norm_g[i], ret_norm_b[i]).reshape(B, S, RET_WIDTH)
        y_ret = jax.nn.silu(r_g) * ry

        aq = a_q.reshape(B, S, DSA_HEADS, DSA_HEAD_DIM)
        c_kv = rms_norm(a_c, kv_norm_g[i])
        q_lat = jnp.einsum('bshd,hdc->bshc', aq, w_uk[i]) * (DSA_HEAD_DIM ** -0.5)
        qi = i_q.reshape(B, S, IDX_HEADS, IDX_DIM)
        ki = layer_norm(i_k, idx_k_norm_g[i], idx_k_norm_b[i])
        wi = i_w * ((IDX_HEADS ** -0.5) * (IDX_DIM ** -0.5))
        o_lat = dsa_sparse_attention(q_lat, c_kv, qi, ki, wi)
        y_dsa = jnp.einsum('bshc,hcd->bshd', o_lat, w_uv[i]).reshape(B, S, DSA_WIDTH)

        mix = jnp.concatenate([y_ret, y_dsa], axis=-1) @ w_out[i]
        x = x + rms_norm(mix, post_mix_g[i])

        f = rms_norm(x, pre_ffn_g[i])
        f = (jax.nn.silu(f @ w_ffn_gate[i]) * (f @ w_ffn_up[i])) @ w_ffn_down[i]
        x = x + rms_norm(f, post_ffn_g[i])

        e = p[i] @ w_ple_up[i]
        gate = jax.nn.sigmoid(x @ w_ple_gate[i])
        x = x + rms_norm(gate * e, ple_norm_g[i])
    return x


_drawn_inputs = setup_inputs


def setup_inputs(seed=0):
    import zlib

    import numpy as np

    out = dict(_drawn_inputs(seed))
    spreads = {}
    factors = {'ret_norm_g': 20.082,
     'ret_norm_b': 19.814,
     'kv_norm_g': 5.943,
     'idx_k_norm_g': 3.347,
     'idx_k_norm_b': 3.91,
     'post_mix_g': 3.679,
     'pre_ffn_g': 3.819,
     'post_ffn_g': 19.524,
     'ple_norm_g': 23.85}
    for name, (base, spread) in spreads.items():
        noise = np.random.default_rng([zlib.crc32(name.encode()), seed]).standard_normal(out[name].shape)
        drawn = base * np.exp(spread * noise) if base else spread * noise
        out[name] = __import__('jax').numpy.asarray(drawn.astype(out[name].dtype))
    for name, factor in factors.items():
        out[name] = (out[name] * factor).astype(out[name].dtype)
    return out
```

```python
from contextlib import ExitStack

import numpy as np

import concourse.bass as bass
from concourse import mybir

F32 = mybir.dt.float32
F32R = mybir.dt.float32r
I32 = mybir.dt.int32
ALU = mybir.AluOpType
ACT = mybir.ActivationFunctionType
AX = mybir.AxisListType

P = 128
S = 1024
D = 1024
RT = S // P
KT = D // P
H = 8
HD = 64
NP = H // 2
FF = 2816
FT = FF // P
PLE = 256
TOPK = 256
B0 = TOPK // P
C_RET, C_AQ, C_AC, C_IQ, C_IK, C_IW = 0, 2048, 2560, 2688, 3200, 3264
SMALL = P + HD + H
EPS = 1e-6
NONCAUSAL = -3.0e38
PICKED = -3.4e38
MASKED = -1.0e30
ROUNDS = TOPK // 8
UNROLL = 8
TWO_PI = 2.0 * np.pi
MAGIC = 12582912.0
PI_CAP = 3.1415925


def shape_tables():
    inv_freq = (1.0 / (10000.0 ** (np.arange(0, HD, 2, dtype=np.float64) / HD))).astype(np.float32)
    g = 1.0 - 2.0 ** (-5.0 - np.arange(H, dtype=np.float64))
    i = np.arange(P, dtype=np.float64)[:, None]
    q_scale = g[None, :] ** (i + 1.0)
    k_scale = g[None, :] ** (-(i + 1.0)) * HD ** -0.5
    small = np.concatenate([q_scale, k_scale, np.eye(P)], axis=1).astype(np.float32)
    same_head = np.kron(np.eye(2), np.ones((HD, HD)))
    chunk_decay = same_head[:, None, :] * np.repeat((g ** P).reshape(NP, 2), HD, axis=1)[None]
    return np.tile(inv_freq, (P, 1)), small, chunk_decay.astype(np.float32)


def cody_waite():
    c1 = 6.28125
    c2 = float(np.float32(TWO_PI - c1))
    c2 = float(np.float32(np.round(c2 * 2.0 ** 20) / 2.0 ** 20))
    return c1, c2, float(np.float32(TWO_PI - c1 - c2))


def build(nc, x, p, positions, pre_mix_g, w_in, ret_norm_g, ret_norm_b, kv_norm_g, idx_k_norm_g,
          idx_k_norm_b, w_uk, w_uv, w_out, post_mix_g, pre_ffn_g, w_ffn_gate, w_ffn_up, w_ffn_down,
          post_ffn_g, w_ple_up, w_ple_gate, ple_norm_g, inv_freq, small_tab, decay_tab, out, x1_dram, ret_dram):
    ctx = ExitStack()
    base = 16512
    kb = 1024

    def sb(name, shape, at, dt=F32):
        return nc.alloc_sbuf_tensor_at(name, shape, dt, offset=base + int(at * kb))

    def sem(name):
        return nc.alloc_semaphore(name)

    TAB = sb("tab", [P, 2 * H + P], 0)
    QSC, KSC, ID = TAB[:, 0:H], TAB[:, H:2 * H], TAB[:, 2 * H:]
    SML = sb("sml", [P, 256], 0.75)
    KVG = sb("kvg", [P, P], 1.75)
    IKG = sb("ikg", [P, HD], 2.25)
    IKB = sb("ikb", [P, HD], 2.5)
    INV = sb("inv", [P, 32], 2.75)
    COS = sb("cos", [P, RT, 32], 3)
    SIN = sb("sin", [P, RT, 32], 4)
    NSIN = sb("nsin", [P, RT, 32], 5)
    TRI = sb("tri", [P, 2 * P], 6)
    WUK = sb("wuk", [P, NP, P], 7)
    WUV = sb("wuv", [P, H, HD], 9)
    WI = sb("wi", [P, RT, H], 11)
    M8 = sb("m8", [P, 8], 11.25)
    POSI = sb("posi", [P, RT], 11.3125, I32)

    cols = {}
    at = 0
    for name, n in (("ss0", 8), ("v0", 8), ("rs0", 8), ("half", 16), ("ssn", 16), ("vn", 16), ("rsn", 16),
                    ("mu", 8), ("pos", 8), ("sum", 16), ("rsum", 16), ("nmax", 4), ("ssm", 8), ("vm", 8),
                    ("rsm", 8), ("ssf", 8), ("vf", 8), ("rsf", 8), ("cap", 1)):
        cols[name] = SML[:, at:at + n]
        at += n
    assert at <= 256

    XTH = sb("xth", [P, KT, S], 12, F32R)
    XTL = sb("xtl", [P, KT, S], 44, F32R)
    WBH = [sb(f"wbh{i}", [P, KT, 512], 76 + 32 * i, F32R) for i in range(2)]
    WBL = [sb(f"wbl{i}", [P, KT, 512], 92 + 32 * i, F32R) for i in range(2)]
    XN = sb("xn", [P, RT, D], 108)
    RAW = [sb(f"raw{i}", [P, 512], 140 + 2 * i) for i in range(4)]
    QI = sb("qi", [P, NP, S], 148)
    AQ = sb("aq", [P, NP, S], 148)
    CKV = sb("ckv", [P, RT, P], 164)
    CKVT = sb("ckvt", [P, S], 168)
    sc_off = [sum(range(B0 + 1, b + 1)) * P for b in range(B0, RT)]
    SC = [sb(f"sc{b}", [P, (b + 1) * P], 172 + sc_off[b - B0] * 4 / kb) for b in range(B0, RT)]
    NTMP = sb("ntmp", [P, RT, P], 172)
    NXM = sb("nxm", [P, RT, HD], 176)
    GIN = sb("gin", [P, D], 188.5)
    RL = [sb(f"rl{i}", [P, S], 188.5 + 4 * i) for i in range(2)]
    KN = sb("kn", [P, RT, P], 192.5)
    KIT = sb("kit", [P, S], 196.5)
    AC = sb("ac", [P, RT, SMALL], 200.5)
    STG = [sb(f"stg{i}", [P, 512], 200.5 + 2 * i) for i in range(2)]
    RT1 = sb("rt1", [P, 256], 204.5)
    RT2 = sb("rt2", [P, 256], 205.5)
    ANG = sb("ang", [P, RT, 32], 188.5 + 4)
    ANK = sb("ank", [P, RT, 32], 188.5 + 5)
    ANR = sb("anr", [P, RT, 32], 188.5 + 6)

    RP = [sb(f"rp{i}", [P, RT, 512], 108 + 16 * i) for i in range(2)]
    QKT = [sb(f"qkt{i}", [P, RT, 384], 12 + 12 * i) for i in range(2)]
    ST = [sb(f"st{i}", [P, 256], 36 + i) for i in range(2)]
    RST = [sb(f"rst{i}", [P, RT, P], 66 + 4 * i) for i in range(2)]
    CD = sb("cd", [P, NP, P], 38)
    O = [sb(f"o{i}", [P, RT, P], 42 + 4 * i) for i in range(2)]
    SGR = sb("sgr", [P, RT, P], 50)
    PT1 = sb("pt1", [P, RT, P], 54)
    Y = sb("y", [P, RT, P], 58)
    RG = sb("rg", [P, 512], 62)
    RB = sb("rb", [P, 512], 64)
    YRT = sb("yrt", [P, NP, S], 188.75)

    WO = sb("wo", [P, KT, D], 76)
    FTR = sb("ftr", [P, KT, S], 12)
    XR = [sb(f"xr{i}", [P, D], 44 + 4 * i) for i in range(2)]
    GPO = sb("gpo", [P, D], 52)
    GPF = sb("gpf", [P, D], 56)
    QL = [sb("ql0", [P, H, P], 108), sb("ql1", [P, H, P], 60)]
    LM = [sb(f"lm{i}", [P, S], 112 + 4 * i) for i in range(2)]
    PT = [sb(f"pt{i}", [P, S], 120 + 4 * i) for i in range(2)]
    OTS = [sb(f"ots{i}", [P, 512], 128 + 2 * i) for i in range(2)]
    YD = sb("yd", [P, 512], 132)
    YDT = sb("ydt", [P, NP, P], 134)
    MXS = sb("mxs", [P, D], 136)
    FN = sb("fn", [P, D], 140)
    JK = sb("jk", [P, D], 144)

    FTH = sb("fth", [P, KT, S], 44, F32R)
    FTL = sb("ftl", [P, KT, S], 12, F32R)
    HT = sb("ht", [P, FT, S], 76)
    WR = [sb("wr0", [P, 2, KT, P], 2), sb("wr1", [P, 2, KT, P], 164)]
    WH = [sb(f"wh{i}", [P, 2, KT, P], 172 + 16 * i, F32R) for i in range(2)]
    WL = [sb(f"wl{i}", [P, 2, KT, P], 180 + 16 * i, F32R) for i in range(2)]
    SG = [sb("sg0", [P, 512], 204), sb("sg1", [P, 512], 10)]
    HTH = [sb(f"hth{i}", [P, S], 164 + 8 * i, F32R) for i in range(2)]
    HTL = [sb(f"htl{i}", [P, S], 168 + 8 * i, F32R) for i in range(2)]
    DR = [sb(f"dr{i}", [P, 512], 180 + 2 * i) for i in range(2)]
    DH = [sb(f"dh{i}", [P, 512], 188 + 4 * i, F32R) for i in range(2)]
    DL = [sb(f"dl{i}", [P, 512], 190 + 4 * i, F32R) for i in range(2)]
    FO0 = sb("fo0", [P, RT, 512], 28)
    FO1 = sb("fo1", [P, RT, 512], 12)

    WGH = sb("wgh", [P, KT, D], 76, F32R)
    WGL = sb("wgl", [P, KT, D], 108, F32R)
    WUH = sb("wuh", [P, 2, D], 140, F32R)
    WUL = sb("wul", [P, 2, D], 148, F32R)
    PTH = sb("pth", [P, 2, S], 156, F32R)
    PTL = sb("ptl", [P, 2, S], 164, F32R)
    X2 = [sb(f"x2{i}", [P, D], 172 + 4 * i) for i in range(3)]
    X2H = [sb(f"x2h{i}", [P, KT, P], 44 + 8 * i, F32R) for i in range(2)]
    X2L = [sb(f"x2l{i}", [P, KT, P], 48 + 8 * i, F32R) for i in range(2)]
    GPF2 = sb("gpf2", [P, D], 60)
    GPL = sb("gpl", [P, D], 64)
    SGG = sb("sgg", [P, D], 68)
    UU = [sb("uu0", [P, D], 72), sb("uu1", [P, D], 184)]
    JF = sb("jf", [P, D], 188)
    PN = sb("pn", [P, RT, PLE], 192)
    WGR = [sb(f"wgr{i}", [P, 512], 200 + 2 * i) for i in range(3)]
    SMF = sb("smf", [P, 64], 206.25)

    PS = ctx.enter_context(nc.psum_tensor("ps", [P, 8 * 512], F32))

    def bank(i, n=512):
        return PS[:, 512 * i:512 * i + n]

    names = """a_sq v_var p_rs v_xn t_xt a_xh v_xl p_half v_ang a_trig v_nsin a_whi p_wlo t_unit a_ev
        v_link p_link v_nrm p_nrs v_kn v_ckv v_wi v_ac t_nt a_nt t_ix a_rl v_acc p_caus v_mask p_tri p_rot
        t_rb a_rb p_rst t_sc a_st p_st t_ro a_o a_silu p_zero v_lnv p_lnr v_y t_yr a_yrt
        t_lg v_lm a_ex t_tp a_tp t_pv a_ots t_ms a_ms v_ms a_mss v_mv p_mr v_x1 a_fss v_fv p_fr v_fn
        a_fth v_ftl a_gh v_gl t_gu a_sg v_ht a_dwh v_dwl a_dhh v_dhl t_dn t_acc a_fo v_fo
        a_wgh v_wgl t_pt a_pth v_ptl a_css v_wv p_wr v_x2 t_x2 a_x2h v_x2l t_gt t_em a_sig v_u a_uss v_uv p_ur
        v_out load_const load_gin load_gain load_wuk load_wo load_retg load_pn load_gain2 st_x1""".split()
    s = {n: sem(n) for n in names}
    load_x = [sem(f"load_x{i}") for i in range(RT)]
    load_raw = [sem(f"load_raw{i}") for i in range(4)]
    st_ret = [sem(f"st_ret{i}") for i in range(2)]
    st_out = [sem(f"st_out{i}") for i in range(2)]
    load_rp = [sem(f"load_rp{i}") for i in range(2)]
    load_xr = [sem(f"load_xr{i}") for i in range(2)]
    load_wr = [sem(f"load_wr{i}") for i in range(2)]
    load_dr = [sem(f"load_dr{i}") for i in range(2)]
    load_wg = [sem(f"load_wg{i}") for i in range(3)]
    load_x2 = [sem(f"load_x2{i}") for i in range(3)]

    NCH = 7
    block = ctx.enter_context(nc.Block())


    def pair(j, n=1024):
        return PS[:, 1024 * j:1024 * j + n]

    def raw_count(n):
        return 16 * sum(2 if m // KT == 1 else 1 for m in range(n % 4, n + 1, 4))

    def width(c):
        return SMALL if c == 1 else 512

    LAST = NCH * KT
    STEPS = RT * H
    TAIL = 11

    def at_block(t, lag):
        b, h = divmod(t - lag, H)
        return b if h == H - 1 and 0 <= b < RT else None

    def at_half(t, lag):
        g, h = divmod(t - lag, 4)
        return g if h == 3 and 0 <= g < 2 * RT else None

    def ql_due(t):
        b, h = divmod(t + 4, H)
        return (b, h) if h < 2 and 1 <= b < RT else None

    tp_use, ms_use = [], [("ql", 0, 0), ("ql", 0, 1)]
    for t in range(STEPS + TAIL):
        if 1 <= t <= STEPS:
            tp_use.append(("tr", t - 1))
        if at_block(t, 5) is not None:
            tp_use.append(("mx", at_block(t, 5)))
        if at_block(t, 10) is not None:
            tp_use.append(("ft", at_block(t, 10)))
        if ql_due(t) is not None:
            ms_use.append(("ql", *ql_due(t)))
        if at_half(t, 3) is not None:
            ms_use.append(("y", at_half(t, 3)))
        if at_block(t, 4) is not None:
            ms_use.append(("yt", at_block(t, 4)))
    tp_at = {u: n for n, u in enumerate(tp_use)}
    ms_at = {u: n for n, u in enumerate(ms_use)}

    def ms_read(n):
        v = sum(u[0] == "y" for u in ms_use[:n])
        return n - v, v

    @block.sync
    def _(sp):
        x_t = x.rearrange("b (r p) d -> p (b r) d", p=P)

        def row_gain(dst, g, sm):
            sp.dma_start(dst[:, :], g[0:1, :].to_broadcast([P, g.shape[1]])).then_inc(s[sm], 16)

        def proj_weights(n):
            c, k = divmod(n, KT)
            if n >= 4:
                sp.wait_ge(s["a_whi"], n - 3)
                sp.wait_ge(s["p_wlo"], n - 3)
            dst, sm = RAW[n % 4], load_raw[n % 4]
            w = w_in[0, k * P:(k + 1) * P, :]
            if c == 0:
                sp.dma_start(dst[:, :], w[:, C_IQ:C_IQ + 512]).then_inc(sm, 16)
            elif c == 1:
                sp.dma_start(dst[:, 0:P], w[:, C_AC:C_AC + P]).then_inc(sm, 16)
                sp.dma_start(dst[:, P:SMALL], w[:, C_IK:C_IK + HD + H]).then_inc(sm, 16)
            elif c == 6:
                sp.dma_start(dst[:, :], w[:, C_AQ:C_AQ + 512]).then_inc(sm, 16)
            else:
                src = w[:, 0:4 * 512].rearrange("p (g c) -> p g c", g=4)[:, :, (c - 2) * P:(c - 1) * P]
                sp.dma_start(dst[:, :].rearrange("p (g c) -> p g c", g=4), src).then_inc(sm, 16)

        def store_retention(n):
            hp, r = divmod(n, RT)
            sp.wait_ge(s["p_rot"], n + 1)
            sp.dma_start(ret_dram[hp, r * P:(r + 1) * P, :], STG[n % 2][:, :]).then_inc(st_ret[n % 2], 16)

        sp.dma_start(XN[:, 0, :], x_t[:, 0, :]).then_inc(load_x[0], 16)
        row_gain(GIN, pre_mix_g, "load_gin")
        sp.dma_start(TAB[:, :], small_tab).then_inc(s["load_const"], 16)
        for r in range(1, 4):
            sp.dma_start(XN[:, r, :], x_t[:, r, :]).then_inc(load_x[r], 16)
        for n in range(4):
            proj_weights(n)
        for r in range(4, RT):
            sp.dma_start(XN[:, r, :], x_t[:, r, :]).then_inc(load_x[r], 16)
        with nc.allow_non_contiguous_dma(reason="1024 positions, once"):
            sp.dma_start(POSI[:, :], positions[0].rearrange("(r p) -> p r", p=P)).then_inc(s["load_const"], 16)
        sp.dma_start(INV[:, :], inv_freq).then_inc(s["load_const"], 16)
        row_gain(KVG, kv_norm_g, "load_const")
        row_gain(IKG, idx_k_norm_g, "load_const")
        row_gain(IKB, idx_k_norm_b, "load_const")
        for h in range(H):
            j = HD * (h % 2)
            sp.dma_start(WUK[j:j + HD, h // 2, :], w_uk[0, h]).then_inc(s["load_wuk"], 16)
        sp.dma_start(WUV[:, :, :], w_uv[0].rearrange("h c d -> c h d")).then_inc(s["load_wuk"], 16)
        for g in range(-8, LAST):
            if 4 <= g + 12 < LAST:
                proj_weights(g + 12)
            if 0 <= g - 17 < NP * RT:
                store_retention(g - 17)
        sp.wait_ge(s["t_unit"], 6 * RT)
        for hp in range(NP):
            for i in range(2):
                sp.wait_ge(st_ret[i], 16 * 4 * (hp + 1))
            if hp >= 2:
                sp.wait_ge(s["t_ro"], RT * (hp - 1))
                sp.wait_ge(s["a_silu"], hp - 1)
            sp.dma_start(RP[hp % 2][:, :, :], ret_dram[hp].rearrange("(r p) c -> p r c", p=P))\
              .then_inc(load_rp[hp % 2], 16)
            if hp == 1:
                sp.wait_ge(s["t_unit"], LAST)
                for dst, g in ((RG, ret_norm_g), (RB, ret_norm_b)):
                    sp.dma_start(dst[:, :], g[0:1].rearrange("a h d -> a (h d)").to_broadcast([P, 512]))\
                      .then_inc(s["load_retg"], 16)
                sp.dma_start(CD[:, :, :], decay_tab).then_inc(s["load_retg"], 16)
                sp.dma_start(WO[:, :, :], w_out[0].rearrange("(k p) d -> p k d", p=P)).then_inc(s["load_wo"], 16)
        sp.wait_ge(s["v_y"], NP)
        sp.wait_ge(s["t_yr"], NP)
        row_gain(GPO, post_mix_g, "load_gain")
        row_gain(GPF, pre_ffn_g, "load_gain")
        for b in range(2):
            sp.dma_start(XR[b][:, :], x_t[:, b, :]).then_inc(load_xr[b], 16)
        for b in range(RT):
            sp.wait_ge(s["v_x1"], b + 1)
            sp.dma_start(x1_dram[b * P:(b + 1) * P, :], XR[b % 2][:, :]).then_inc(s["st_x1"], 16)
            if b + 2 < RT:
                sp.wait_ge(s["st_x1"], 16 * (b + 1))
                sp.wait_ge(s["a_fss"], b + 1)
                sp.wait_ge(s["v_fn"], b + 1)
                sp.dma_start(XR[b % 2][:, :], x_t[:, b + 2, :]).then_inc(load_xr[b % 2], 16)

        def gate_up(slot, f):
            for j, w in enumerate((w_ffn_gate, w_ffn_up)):
                src = w[0].rearrange("(k p) f -> p k f", p=P)[:, :, bass.ds(f * P, P)]
                sp.dma_start(WR[slot][:, j, :, :], src).then_inc(load_wr[slot], 16)

        sp.wait_ge(s["t_ms"], len(ms_use))
        sp.wait_ge(s["v_lm"], STEPS)
        sp.wait_ge(s["t_pv"], STEPS)
        gate_up(0, 0)
        gate_up(1, 1)
        with sp.Fori(1, FT // 2) as i:
            for t in range(2):
                sp.wait_ge(s["v_gl"], i * 2 + (t - 1))
                gate_up(t, i * 2 + t)

        def down(slot, f, dh):
            src = w_ffn_down[0, bass.ds(f * P, P), dh * 512:(dh + 1) * 512]
            sp.dma_start(DR[slot][:, :], src).then_inc(load_dr[slot], 16)

        sp.wait_ge(s["t_gu"], 2 * FT)
        for t in range(2):
            down(t, t, 0)
        with sp.Fori(1, FT // 2) as i:
            for t in range(2):
                sp.wait_ge(s["v_dwl"], i * 2 + (t - 1))
                down(t, i * 2 + t, 0)
        with sp.Fori(0, FT // 2) as i:
            for t in range(2):
                sp.wait_ge(s["v_dwl"], i * 2 + (FT + t - 1))
                down(t, i * 2 + t, 1)
        sp.wait_ge(s["t_dn"], 2 * FT)
        sp.dma_start(PN[:, :, :], p[0, 0].rearrange("(r q) c -> q r c", q=P)).then_inc(s["load_pn"], 16)
        row_gain(GPF2, post_ffn_g, "load_gain2")
        sp.wait_ge(s["st_x1"], 16 * RT)
        for r in range(3):
            sp.dma_start(X2[r][:, :], x1_dram[r * P:(r + 1) * P, :]).then_inc(load_x2[r], 16)
        row_gain(GPL, ple_norm_g, "load_gain2")
        for n in range(2 * (2 + KT)):
            k, dh = divmod(n if n < 4 else n - 4, 2)
            src = w_ple_up[0] if n < 4 else w_ple_gate[0]
            if n >= 3:
                sp.wait_ge(s["v_wgl"], n - 2)
            sp.dma_start(WGR[n % 3][:, :], src[k * P:(k + 1) * P, dh * 512:(dh + 1) * 512])\
              .then_inc(load_wg[n % 3], 16)
        for r in range(RT):
            sp.wait_ge(s["v_out"], r + 1)
            sp.dma_start(out[0, r * P:(r + 1) * P, :], UU[r % 2][:, :]).then_inc(st_out[r % 2], 16)
            if r + 3 < RT:
                sp.dma_start(X2[r % 3][:, :], x1_dram[(r + 3) * P:(r + 4) * P, :]).then_inc(load_x2[r % 3], 16)
        for i in range(2):
            sp.wait_ge(st_out[i], 16 * RT // 2)

    @block.tensor
    def _(pe):
        def mm3(o, ah, al, wh, wl, start, stop):
            pe.matmul(o, ah, wh, start=start, stop=False)
            pe.matmul(o, ah, wl, start=False, stop=False)
            return pe.matmul(o, al, wh, start=False, stop=stop)

        pe.wait_ge(s["load_const"], 16)
        for r in range(RT):
            pe.wait_ge(s["v_xn"], r + 1)
            if r >= 2:
                pe.wait_ge(s["v_xl"], r - 1)
            for k in range(KT):
                m = pe.transpose(pair(1 + r % 2)[:, k * P:(k + 1) * P], XN[:, r, k * P:(k + 1) * P], ID)
            m.then_inc(s["t_xt"], 1)

        def unit(g):
            c, u = divmod(g, KT)
            if g >= 2:
                pe.wait_ge(s["a_ev"], g - 1)
            if c == 0 and u % 4 == 0:
                pe.wait_ge(s["v_xl"], u + 4)
            if c == 1 and u == 0:
                pe.wait_ge(s["v_xl"], RT)
            o = bank(g % 2, width(c))
            hi, lo = WBH[c % 2], WBL[c % 2]
            for k in range(KT):
                if u == 0:
                    pe.wait_ge(s["p_wlo"], c * KT + k + 1)
                if c in (0, 6):
                    m, half = u % 4, u // 4
                    cs, rs = slice(m * P, (m + 1) * P), slice(half * 512, (half + 1) * 512)
                    last = mm3(o, hi[:, k, cs], lo[:, k, cs], XTH[:, k, rs], XTL[:, k, rs], k == 0, k == KT - 1)
                else:
                    rs = slice(u * P, (u + 1) * P)
                    last = mm3(o, XTH[:, k, rs], XTL[:, k, rs], hi[:, k, 0:width(c)], lo[:, k, 0:width(c)],
                               k == 0, k == KT - 1)
            last.then_inc(s["t_unit"], 1)

        for g in range(2 * KT):
            unit(g)
        pe.wait_ge(s["v_kn"], 1)
        pe.wait_ge(s["a_ev"], 1)
        for r in range(RT):
            m = pe.transpose(pair(1)[:, r * P:(r + 1) * P], KN[:, r, :], ID)
        m.then_inc(s["t_nt"], 1)
        pe.wait_ge(s["v_ckv"], 1)
        for r in range(RT):
            m = pe.transpose(pair(2)[:, r * P:(r + 1) * P], CKV[:, r, :], ID)
        m.then_inc(s["t_nt"], 1)

        pe.wait_ge(s["a_nt"], 2)
        for n in range((RT - B0) * H):
            b, h = B0 + n // H, n % H
            if n >= 2:
                pe.wait_ge(s["a_rl"], n - 1)
            j = slice(HD * (h % 2), HD * (h % 2) + HD)
            keys = (b + 1) * P
            for k0 in range(0, keys, 512):
                k1 = min(k0 + 512, keys)
                m = pe.matmul(pair(1 + n % 2)[:, k0:k1], QI[j, h // 2, b * P:(b + 1) * P], KIT[j, k0:k1],
                              start=True, stop=True)
            m.then_inc(s["t_ix"], 1)
        for g in range(2 * KT, LAST):
            unit(g)

        def pair_bank(n):
            hp, r = divmod(n, RT)
            if r == 0:
                pe.wait_ge(load_rp[hp % 2], 16 * (hp // 2 + 1))
            if n == 0:
                pe.wait_ge(s["a_ev"], LAST)
            if n >= 2:
                pe.wait_ge(s["a_rb"], n - 1)
            if r == 0 and hp >= 3:
                pe.wait_ge(s["a_yrt"], hp - 2)
            rp, o = RP[hp % 2], bank(n % 2)
            pe.transpose(o[:, 0:P], rp[:, r, 0:P], ID)
            m = pe.transpose(o[:, P:2 * P], rp[:, r, P:2 * P], ID)
            if r < RT - 1:
                m = pe.matmul(o[:, 2 * P:3 * P], rp[:, r, P:2 * P], rp[:, r, 2 * P:3 * P], start=True, stop=True)
            m.then_inc(s["t_rb"], 1)

        def scores(n):
            hp, r = divmod(n, RT)
            pe.wait_ge(s["a_rb"], n + 1)
            if n >= 2:
                pe.wait_ge(s["a_st"], n - 1)
            for h in range(2):
                j = slice(HD * h, HD * h + HD)
                qk = QKT[hp % 2]
                m = pe.matmul(bank(2 + 2 * (n % 2) + h, P), qk[j, r, P:2 * P], qk[j, r, 0:P],
                              start=True, stop=True)
            m.then_inc(s["t_sc"], 1)

        def ret_out(n):
            hp, r = divmod(n, RT)
            pe.wait_ge(s["p_st"], n + 1)
            if r > 0:
                pe.wait_ge(s["p_rst"], hp * (RT - 1) + r)
            else:
                pe.wait_ge(s["p_zero"], 2)
            if n >= 2:
                pe.wait_ge(s["a_o"], n - 1)
            o = bank(6 + n % 2, P)
            pe.matmul(o, QKT[hp % 2][:, r, 0:P], RST[hp % 2][:, r, :], start=True, stop=False)
            for h in range(2):
                m = pe.matmul(o[:, h * HD:(h + 1) * HD], ST[n % 2][:, h * P:(h + 1) * P],
                              RP[hp % 2][:, r, 2 * P + h * HD:2 * P + (h + 1) * HD], start=False, stop=(h == 1))
            m.then_inc(s["t_ro"], 1)

        def ret_transpose(hp):
            pe.wait_ge(s["v_y"], hp + 1)
            pe.wait_ge(s["a_rb"], min(hp + 3, NP) * RT)
            for r in range(RT):
                m = pe.transpose(pair(0)[:, r * P:(r + 1) * P], Y[:, r, :], ID)
            m.then_inc(s["t_yr"], 1)

        for r in range(RT):
            pair_bank(r)
        for hp in range(NP):
            for r in range(RT + 1):
                if r < RT and hp + 1 < NP:
                    pair_bank((hp + 1) * RT + r)
                if r < RT:
                    scores(hp * RT + r)
                if r >= 1:
                    ret_out(hp * RT + r - 1)
            if hp >= 1:
                ret_transpose(hp - 1)
        pe.wait_ge(s["a_yrt"], NP - 1)
        ret_transpose(NP - 1)

        def tp_free(use):
            if tp_at[use] >= 1:
                pe.wait_ge(s["a_tp"], tp_at[use])

        def ms_free(use):
            a, v = ms_read(ms_at[use])
            if a:
                pe.wait_ge(s["a_ms"], a)
            if v:
                pe.wait_ge(s["v_ms"], v)

        def latent_queries(b, half):
            ms_free(("ql", b, half))
            for hh in range(4):
                h = 2 * hh + half
                j = slice(HD * (h % 2), HD * (h % 2) + HD)
                m = pe.matmul(bank(7)[:, hh * P:(hh + 1) * P], WUK[j, h // 2, :], AQ[j, h // 2, b * P:(b + 1) * P],
                              start=True, stop=True)
            m.then_inc(s["t_ms"], 1)

        def logits(t):
            b, h = divmod(t, H)
            if h == 0:
                pe.wait_ge(s["a_ms"], ms_read(ms_at[("ql", b, 1)])[0] + 1)
            if t >= 2:
                pe.wait_ge(s["v_lm"], t - 1)
            keys = (b + 1) * P
            for k0 in range(0, keys, 512):
                k1 = min(k0 + 512, keys)
                m = pe.matmul(pair(t % 2)[:, k0:k1], QL[b % 2][:, h, :], CKVT[:, k0:k1], start=True, stop=True)
            m.then_inc(s["t_lg"], 1)

        def prob_transposes(t):
            b = t // H
            tp_free(("tr", t))
            pe.wait_ge(s["a_ex"], t + 1)
            for j in range(b + 1):
                m = pe.transpose(pair(2)[:, j * P:(j + 1) * P], LM[t % 2][:, j * P:(j + 1) * P], ID)
            m.then_inc(s["t_tp"], 1)

        def prob_values(t):
            b, h = divmod(t, H)
            pe.wait_ge(s["a_tp"], tp_at[("tr", t)] + 1)
            if t % 4 == 0 and t >= 4:
                pe.wait_ge(s["a_ots"], t // 4)
            for j in range(b + 1):
                m = pe.matmul(bank(6)[:, (h % 4) * P:(h % 4 + 1) * P], CKV[:, j, :], PT[t % 2][:, j * P:(j + 1) * P],
                              start=(j == 0), stop=(j == b))
            m.then_inc(s["t_pv"], 1)

        def head_values(g):
            pe.wait_ge(s["a_ots"], g + 1)
            ms_free(("y", g))
            for hh in range(4):
                m = pe.matmul(bank(7)[:, hh * HD:(hh + 1) * HD], OTS[g % 2][:, hh * P:(hh + 1) * P],
                              WUV[:, 4 * (g % 2) + hh, :], start=True, stop=True)
            m.then_inc(s["t_ms"], 1)

        def y_transposes(b):
            ms_free(("yt", b))
            for k in range(NP):
                m = pe.transpose(bank(7)[:, k * P:(k + 1) * P], YD[:, k * P:(k + 1) * P], ID)
            m.then_inc(s["t_ms"], 1)

        def out_projection(b):
            tp_free(("mx", b))
            for k in range(KT):
                if k == NP:
                    pe.wait_ge(s["a_ms"], ms_read(ms_at[("yt", b)])[0] + 1)
                src = YRT[:, k, b * P:(b + 1) * P] if k < NP else YDT[:, k - NP, :]
                for dh in range(2):
                    m = pe.matmul(pair(2)[:, dh * 512:(dh + 1) * 512], src, WO[:, k, dh * 512:(dh + 1) * 512],
                                  start=(k == 0), stop=(k == KT - 1))
            m.then_inc(s["t_tp"], 1)

        def ffn_transposes(b):
            pe.wait_ge(s["v_fn"], b + 1)
            tp_free(("ft", b))
            for k in range(KT):
                m = pe.transpose(pair(2)[:, k * P:(k + 1) * P], FN[:, k * P:(k + 1) * P], ID)
            m.then_inc(s["t_tp"], 1)

        pe.wait_ge(s["load_wuk"], 16 * (H + 1))
        pe.wait_ge(s["load_wo"], 16)
        pe.wait_ge(s["a_yrt"], NP)
        latent_queries(0, 0)
        latent_queries(0, 1)
        for t in range(STEPS + TAIL):
            if t < STEPS:
                logits(t)
            if 1 <= t <= STEPS:
                prob_transposes(t - 1)
            if 2 <= t <= STEPS + 1:
                prob_values(t - 2)
            if ql_due(t) is not None:
                latent_queries(*ql_due(t))
            if at_half(t, 3) is not None:
                head_values(at_half(t, 3))
            if at_block(t, 4) is not None:
                y_transposes(at_block(t, 4))
            if at_block(t, 5) is not None:
                out_projection(at_block(t, 5))
            if at_block(t, 10) is not None:
                ffn_transposes(at_block(t, 10))

        def gate_up(slot, f, first):
            pe.wait_ge(s["v_gl"], f + 1)
            for half in range(2):
                if not first:
                    pe.wait_ge(s["v_ht"], f * 2 + (half - 3))
                rs = slice(half * 512, (half + 1) * 512)
                for j in range(2):
                    o = bank(4 * slot + 2 * half + j)
                    for k in range(KT):
                        if first and slot == 0 and half == 0 and j == 0:
                            pe.wait_ge(s["v_ftl"], k + 1)
                        m = mm3(o, WH[slot][:, j, k, :], WL[slot][:, j, k, :], FTH[:, k, rs], FTL[:, k, rs],
                                k == 0, k == KT - 1)
                m.then_inc(s["t_gu"], 1)

        pe.wait_ge(s["a_tp"], len(tp_use))
        for t in range(2):
            gate_up(t, t, True)
        with pe.Fori(1, FT // 2) as i:
            for t in range(2):
                gate_up(t, i * 2 + t, False)

        def down(slot, n, start, stop, fresh=None):
            pe.wait_ge(s["v_dwl"], n + 1)
            pe.wait_ge(s["v_dhl"], n + 1)
            for r in range(RT):
                rs = slice(r * P, (r + 1) * P)
                if fresh is not None:
                    fresh(r)
                m = mm3(bank(r), HTH[slot][:, rs], HTL[slot][:, rs], DH[slot][:, :], DL[slot][:, :], start, stop)
                if stop:
                    m.then_inc(s["t_acc"], 1)
            if stop:
                pe.wait_ge(s["t_acc"], (n + 1) // FT * RT)
                pe.sem_inc(s["t_dn"], 1)
            else:
                m.then_inc(s["t_dn"], 1)

        def after_gate_up(r):
            if r == 0:
                pe.wait_ge(s["v_ht"], 2 * FT)

        def after_first_half(r):
            pe.wait_ge(s["a_fo" if r % 2 == 0 else "v_fo"], r // 2 + 1)

        for dh, fresh in enumerate((after_gate_up, after_first_half)):
            n0 = dh * FT
            down(0, n0, True, False, fresh)
            down(1, n0 + 1, False, False)
            with pe.Fori(1, FT // 2 - 1) as i:
                for t in range(2):
                    down(t, i * 2 + (n0 + t), False, False)
            down(0, n0 + FT - 2, False, False)
            down(1, n0 + FT - 1, False, True)

        pe.wait_ge(s["load_pn"], 16)
        for k in range(2):
            pe.wait_ge(s["a_fo"], 2 * RT // 2)
            pe.wait_ge(s["v_fo"], 2 * RT // 2)
            for r in range(RT):
                m = pe.transpose(pair(k)[:, r * P:(r + 1) * P], PN[:, r, k * P:(k + 1) * P], ID)
            m.then_inc(s["t_pt"], 1)

        def x2_transposes(r):
            pe.wait_ge(s["v_x2"], r + 1)
            if r < 2:
                pe.wait_ge(s["v_ptl"], r + 1)
            else:
                pe.wait_ge(s["v_x2l"], r - 1)
            for k in range(KT):
                m = pe.transpose(pair(r % 2)[:, k * P:(k + 1) * P], X2[r % 3][:, k * P:(k + 1) * P], ID)
            m.then_inc(s["t_x2"], 1)

        def gate(r):
            pe.wait_ge(s["v_x2l"], r + 1)
            if r >= 1:
                pe.wait_ge(s["a_sig"], r)
            for dh in range(2):
                ds = slice(dh * 512, (dh + 1) * 512)
                for k in range(KT):
                    if r == 0 and dh == 0:
                        pe.wait_ge(s["v_wgl"], 4 + 2 * (k + 1))
                    m = mm3(pair(2)[:, ds], X2H[r % 2][:, k, :], X2L[r % 2][:, k, :], WGH[:, k, ds], WGL[:, k, ds],
                            k == 0, k == KT - 1)
            m.then_inc(s["t_gt"], 1)

        def embed(r):
            if r == 0:
                pe.wait_ge(s["v_ptl"], 2)
                pe.wait_ge(s["v_wgl"], 4)
            if r >= 1:
                pe.wait_ge(s["v_u"], r)
            rs = slice(r * P, (r + 1) * P)
            for dh in range(2):
                ds = slice(dh * 512, (dh + 1) * 512)
                for k in range(2):
                    m = mm3(pair(3)[:, ds], PTH[:, k, rs], PTL[:, k, rs], WUH[:, k, ds], WUL[:, k, ds], k == 0, k == 1)
            m.then_inc(s["t_em"], 1)

        x2_transposes(0)
        for r in range(RT):
            embed(r)
            gate(r)
            if r + 1 < RT:
                x2_transposes(r + 1)

    @block.scalar
    def _(act):
        sc = nc.scalar

        def square(r):
            act.wait_ge(load_x[r], 16)
            if r:
                act.wait_ge(s["a_sq"], r)
            sc.activation(pair(3), XN[:, r, :], ACT.Square, accum_out=cols["ss0"][:, r:r + 1]).then_inc(s["a_sq"], 1)

        def x_hi(r):
            act.wait_ge(s["t_xt"], r + 1)
            sc.copy(XTH[:, :, r * P:(r + 1) * P], pair(1 + r % 2).rearrange("p (k c) -> p k c", k=KT))\
              .then_inc(s["a_xh"], 1)

        def w_hi(n):
            c, k = divmod(n, KT)
            act.wait_ge(load_raw[n % 4], raw_count(n))
            if k == 0 and c == 1:
                act.wait_ge(s["t_xt"], RT)
            if k == 0 and c >= 2:
                act.wait_ge(s["t_unit"], KT * (c - 1))
            w = width(c)
            sc.copy(WBH[c % 2][:, k, 0:w], RAW[n % 4][:, 0:w]).then_inc(s["a_whi"], 1)

        def evacuate(g):
            c, u = divmod(g, KT)
            act.wait_ge(s["t_unit"], g + 1)
            o = bank(g % 2)
            if c in (0, 6):
                m, half = u % 4, u // 4
                ins = sc.copy((QI if c == 0 else AQ)[:, m, half * 512:(half + 1) * 512], o)
            elif c == 1:
                ins = sc.copy(AC[:, u, :], o[:, 0:SMALL])
            else:
                n, hp = g - 2 * KT, c - 2
                if n == 0:
                    act.wait_ge(s["v_ac"], 1)
                if n >= 2:
                    act.wait_ge(st_ret[n % 2], 16 * (n // 2))
                for j in range(4):
                    col = (QSC if j < 2 else KSC)[:, 2 * hp + j % 2:2 * hp + j % 2 + 1]
                    sc.activation(STG[n % 2][:, j * HD:(j + 1) * HD], o[:, j * HD:(j + 1) * HD], ACT.Copy, scale=col)
                ins = sc.copy(STG[n % 2][:, 256:512], o[:, 256:512])
            ins.then_inc(s["a_ev"], 1)

        for r in range(RT + 2):
            if r < RT:
                square(r)
            if r >= 2:
                x_hi(r - 2)
                w_hi(r - 2)
        act.wait_ge(s["v_ang"], 1)
        sc.activation(SIN[:, :, :], ANR[:, :, :], ACT.Sin).then_inc(s["a_trig"], 1)
        sc.activation(COS[:, :, :], ANK[:, :, :], ACT.Sin).then_inc(s["a_trig"], 1)
        for g in range(2 * KT):
            w_hi(g + KT)
            evacuate(g)
        for j, dst in enumerate((KIT[:, :], CKVT[:, :])):
            act.wait_ge(s["t_nt"], j + 1)
            sc.copy(dst, pair(1 + j)).then_inc(s["a_nt"], 1)
        for n in range((RT - B0) * H):
            keys = (B0 + n // H + 1) * P
            act.wait_ge(s["t_ix"], n + 1)
            if n >= 2:
                act.wait_ge(s["v_acc"], n - 1)
            sc.activation(RL[n % 2][:, 0:keys], pair(1 + n % 2, keys), ACT.Relu).then_inc(s["a_rl"], 1)
        for g in range(2 * KT, LAST):
            if g + KT < LAST:
                w_hi(g + KT)
            evacuate(g)

        def read_pair_bank(n):
            hp, r = divmod(n, RT)
            act.wait_ge(s["t_rb"], n + 1)
            w = 3 * P if r < RT - 1 else 2 * P
            sc.copy(QKT[hp % 2][:, r, 0:w], bank(n % 2, w)).then_inc(s["a_rb"], 1)

        def read_scores(n):
            act.wait_ge(s["t_sc"], n + 1)
            if n >= 2:
                act.wait_ge(s["t_ro"], n - 1)
            b0 = 1024 * (1 + n % 2)
            src = PS[:, b0:b0 + 1024].rearrange("p (h i) -> p h i", h=2)[:, :, 0:P]
            sc.copy(ST[n % 2][:, :].rearrange("p (h i) -> p h i", h=2), src).then_inc(s["a_st"], 1)

        def read_out(n):
            hp, r = divmod(n, RT)
            if r == 0 and hp >= 2:
                act.wait_ge(s["v_y"], hp - 1)
            act.wait_ge(s["t_ro"], n + 1)
            sc.copy(O[hp % 2][:, r, :], bank(6 + n % 2, P)).then_inc(s["a_o"], 1)

        def ret_gate(hp):
            act.wait_ge(load_rp[hp % 2], 16 * (hp // 2 + 1))
            if hp >= 1:
                act.wait_ge(s["v_y"], hp)
            sc.activation(SGR[:, :, :], RP[hp % 2][:, :, 3 * P:4 * P], ACT.Silu).then_inc(s["a_silu"], 1)

        def read_ret(hp):
            if hp == 0:
                for i in range(2):
                    act.wait_ge(st_ret[i], 16 * 4 * NP)
            act.wait_ge(s["t_yr"], hp + 1)
            sc.copy(YRT[:, hp, :], pair(0)).then_inc(s["a_yrt"], 1)

        for r in range(RT):
            read_pair_bank(r)
        for hp in range(NP):
            for r in range(RT + 1):
                if r < RT and hp + 1 < NP:
                    read_pair_bank((hp + 1) * RT + r)
                if r < RT:
                    read_scores(hp * RT + r)
                if r >= 1:
                    read_out(hp * RT + r - 1)
            if hp >= 1:
                ret_gate(hp)
                read_ret(hp - 1)
            else:
                ret_gate(0)
        read_ret(NP - 1)

        def read_queries(b, half):
            n = ms_at[("ql", b, half)]
            act.wait_ge(s["t_ms"], n + 1)
            if b >= 2:
                act.wait_ge(s["t_lg"], H * (b - 1))
            sc.mul(QL[b % 2][:, half:H:2, :], bank(7).rearrange("p (h c) -> p h c", h=4), HD ** -0.5)\
              .then_inc(s["a_ms"], 1)

        def exponent(t):
            b, h = divmod(t, H)
            keys = (b + 1) * P
            act.wait_ge(s["v_lm"], t + 1)
            if h == 0 and b >= 2:
                act.wait_ge(s["v_ms"], 2 * (b - 1))
            c = (b % 2) * H + h
            sc.activation(LM[t % 2][:, 0:keys], LM[t % 2][:, 0:keys], ACT.Exp, scale=-1.0,
                          bias=cols["nmax"][:, t % 4:t % 4 + 1], accum_out=cols["sum"][:, c:c + 1])\
              .then_inc(s["a_ex"], 1)

        def read_probs(t):
            keys = (t // H + 1) * P
            act.wait_ge(s["t_tp"], tp_at[("tr", t)] + 1)
            if t >= 2:
                act.wait_ge(s["t_pv"], t - 1)
            sc.copy(PT[t % 2][:, 0:keys], pair(2, keys)).then_inc(s["a_tp"], 1)

        def read_latent(g):
            act.wait_ge(s["t_pv"], 4 * (g + 1))
            if g >= 2:
                act.wait_ge(s["t_ms"], ms_at[("y", g - 2)] + 1)
            sc.copy(OTS[g % 2][:, :], bank(6)).then_inc(s["a_ots"], 1)

        def read_y(b):
            act.wait_ge(s["t_ms"], ms_at[("yt", b)] + 1)
            if b >= 1:
                act.wait_ge(s["t_tp"], tp_at[("mx", b - 1)] + 1)
            sc.copy(YDT[:, :, :], bank(7).rearrange("p (k c) -> p k c", k=NP)).then_inc(s["a_ms"], 1)

        def read_mix(b):
            act.wait_ge(s["t_tp"], tp_at[("mx", b)] + 1)
            if b >= 1:
                act.wait_ge(s["v_x1"], b)
            sc.copy(MXS[:, :], pair(2)).then_inc(s["a_tp"], 1)
            act.wait_ge(s["a_tp"], tp_at[("mx", b)] + 1)
            if b >= 1:
                act.wait_ge(s["a_fss"], b)
            sc.activation(JK[:, :], MXS[:, :], ACT.Square, accum_out=cols["ssm"][:, b:b + 1]).then_inc(s["a_mss"], 1)

        def ffn_square(b):
            act.wait_ge(s["v_x1"], b + 1)
            act.wait_ge(s["a_mss"], b + 1)
            sc.activation(JK[:, :], XR[b % 2][:, :], ACT.Square, accum_out=cols["ssf"][:, b:b + 1])\
              .then_inc(s["a_fss"], 1)

        def read_ffn_rows(b):
            act.wait_ge(s["t_tp"], tp_at[("ft", b)] + 1)
            sc.copy(FTR[:, :, b * P:(b + 1) * P], pair(2).rearrange("p (k c) -> p k c", k=KT)).then_inc(s["a_tp"], 1)

        read_queries(0, 0)
        read_queries(0, 1)
        for t in range(STEPS + TAIL):
            if t < STEPS:
                exponent(t)
            if 1 <= t <= STEPS:
                read_probs(t - 1)
            if at_half(t, 2) is not None:
                read_latent(at_half(t, 2))
            if ql_due(t) is not None:
                read_queries(*ql_due(t))
            if at_block(t, 4) is not None:
                read_y(at_block(t, 4))
            if at_block(t, 5) is not None:
                read_mix(at_block(t, 5))
            if at_block(t, 8) is not None:
                ffn_square(at_block(t, 8))
            if at_block(t, 10) is not None:
                read_ffn_rows(at_block(t, 10))

        for k in range(KT):
            if k == 0:
                act.wait_ge(s["a_tp"], len(tp_use))
                act.wait_ge(s["st_x1"], 16 * RT)
            sc.copy(FTH[:, k, :], FTR[:, k, :]).then_inc(s["a_fth"], 1)
            if k == 0:
                act.wait_ge(load_wr[0], 32)
                sc.copy(WH[0][:, :, :, :], WR[0][:, :, :, :]).then_inc(s["a_gh"], 1)

        def gate_hi(slot, f, first=False):
            act.wait_ge(load_wr[slot], (f - slot) * 16 + 32)
            if not first:
                act.wait_ge(s["t_gu"], f * 2 - 2)
            sc.copy(WH[slot][:, :, :, :], WR[slot][:, :, :, :]).then_inc(s["a_gh"], 1)

        def silu_gate(slot, f, half, first=False):
            act.wait_ge(s["t_gu"], f * 2 + (half + 1))
            if not first:
                act.wait_ge(s["v_ht"], f * 2 + (half - 1))
            sc.activation(SG[half][:, :], bank(4 * slot + 2 * half), ACT.Silu).then_inc(s["a_sg"], 1)

        gate_hi(1, 1, True)
        silu_gate(0, 0, 0, True)
        silu_gate(0, 0, 1, True)
        with act.Fori(1, FT // 2) as i:
            gate_hi(0, i * 2)
            for half in range(2):
                silu_gate(1, i * 2 - 1, half)
            gate_hi(1, i * 2 + 1)
            for half in range(2):
                silu_gate(0, i * 2, half)
        for half in range(2):
            silu_gate(1, FT - 1, half)

        def down_hi(slot, n, f, first=False):
            act.wait_ge(load_dr[slot], (n - slot) * 8 + 16)
            if not first:
                act.wait_ge(s["t_dn"], n - 1)
            sc.copy(DH[slot][:, :], DR[slot][:, :]).then_inc(s["a_dwh"], 1)
            sc.copy(HTH[slot][:, :], HT[:, bass.ds(f, 1), :]).then_inc(s["a_dhh"], 1)

        act.wait_ge(s["t_gu"], 2 * FT)
        act.wait_ge(s["v_ht"], 2 * FT)
        for t in range(2):
            down_hi(t, t, t, True)
        with act.Fori(1, FT // 2) as i:
            for t in range(2):
                down_hi(t, i * 2 + t, i * 2 + t)
        for t in range(2):
            down_hi(t, FT + t, t)
        for r in range(0, RT, 2):
            act.wait_ge(s["t_acc"], r + 1)
            sc.copy(FO0[:, r, :], bank(r)).then_inc(s["a_fo"], 1)
        with act.Fori(1, FT // 2) as i:
            for t in range(2):
                down_hi(t, i * 2 + (FT + t), i * 2 + t)
        for r in range(0, RT, 2):
            act.wait_ge(s["t_acc"], RT + r + 1)
            sc.copy(FO1[:, r, :], bank(r)).then_inc(s["a_fo"], 1)

        def ffn_out_square(r):
            if r == 0:
                act.wait_ge(s["a_fo"], RT)
                act.wait_ge(s["v_fo"], RT)
            else:
                act.wait_ge(s["a_css"], 2 * r)
            if r >= 4:
                act.wait_ge(s["a_uss"], r - 3)
            for dh, fo in enumerate((FO0, FO1)):
                sc.activation(JF[:, 512 * dh:512 * (dh + 1)], fo[:, r, :], ACT.Square,
                              accum_out=SMF[:, 2 * r + dh:2 * r + dh + 1]).then_inc(s["a_css"], 1)

        def ple_hi(n):
            act.wait_ge(load_wg[n % 3], 16 * (n // 3 + 1))
            k, dh = divmod(n if n < 4 else n - 4, 2)
            dst = WUH if n < 4 else WGH
            sc.copy(dst[:, k, dh * 512:(dh + 1) * 512], WGR[n % 3][:, :]).then_inc(s["a_wgh"], 1)

        def x2_hi(r):
            act.wait_ge(s["t_x2"], r + 1)
            if r >= 2:
                act.wait_ge(s["t_gt"], r - 1)
            sc.copy(X2H[r % 2][:, :, :], pair(r % 2).rearrange("p (k c) -> p k c", k=KT)).then_inc(s["a_x2h"], 1)

        ffn_out_square(0)
        for n in range(4):
            ple_hi(n)
        for k in range(2):
            act.wait_ge(s["t_pt"], k + 1)
            sc.copy(PTH[:, k, :], pair(k)).then_inc(s["a_pth"], 1)
        for n in range(4, 20):
            ple_hi(n)
            if n == 8:
                x2_hi(0)
            if n in (5, 11, 17):
                ffn_out_square((n + 1) // 6)
        for r in range(RT):
            if r + 1 < RT:
                x2_hi(r + 1)
            act.wait_ge(s["t_gt"], r + 1)
            if r >= 1:
                act.wait_ge(s["v_u"], r)
            sc.activation(SGG[:, :], pair(2), ACT.Sigmoid).then_inc(s["a_sig"], 1)
            act.wait_ge(s["v_u"], r + 1)
            act.wait_ge(s["a_css"], 2 * min(r + 4, RT))
            if r:
                act.wait_ge(s["a_uss"], r)
            sc.activation(JF[:, :], UU[r % 2][:, :], ACT.Square, accum_out=SMF[:, 32 + r:33 + r])\
              .then_inc(s["a_uss"], 1)
            if r + 4 < RT:
                ffn_out_square(r + 4)

    @block.vector
    def _(dve):
        v = nc.vector
        made = [0]

        def link(ins):
            made[0] += 1
            ins.then_inc(s["v_link"], 1)
            dve.wait_ge(s["v_link"], made[0])

        def norm_x(r):
            if r == 0:
                dve.wait_ge(s["load_gin"], 16)
            dve.wait_ge(s["p_rs"], r + 1)
            v.scalar_tensor_tensor(XN[:, r, :], XN[:, r, :], cols["rs0"][:, r:r + 1], GIN[:, :], ALU.mult, ALU.mult)\
             .then_inc(s["v_xn"], 1)

        def x_lo(r):
            dve.wait_ge(s["a_xh"], r + 1)
            rs = slice(r * P, (r + 1) * P)
            v.tensor_tensor(XTL[:, :, rs], pair(1 + r % 2).rearrange("p (k c) -> p k c", k=KT),
                            XTH[:, :, rs].bitcast(F32), ALU.subtract).then_inc(s["v_xl"], 1)

        for r in range(RT + 2):
            if r < RT:
                dve.wait_ge(s["a_sq"], r + 1)
                v.tensor_scalar(cols["v0"][:, r:r + 1], cols["ss0"][:, r:r + 1], 1.0 / D, EPS, ALU.mult, ALU.add)\
                 .then_inc(s["v_var"], 1)
            if 1 <= r <= RT:
                norm_x(r - 1)
            if r >= 2:
                x_lo(r - 2)
        c1, c2, c3 = cody_waite()
        dve.wait_ge(s["load_const"], 16 * 6)
        dve.wait_ge(s["v_xn"], RT)
        link(v.tensor_copy(cols["pos"], POSI[:, :]))
        inv_b = INV[:, :].unsqueeze(1).to_broadcast([P, RT, 32])
        link(v.tensor_tensor(ANG[:, :, :], cols["pos"].unsqueeze(2).to_broadcast([P, RT, 32]), inv_b, ALU.mult))
        link(v.tensor_scalar(ANK[:, :, :], ANG[:, :, :], 1.0 / TWO_PI, MAGIC, ALU.mult, ALU.add))
        link(v.tensor_scalar(ANK[:, :, :], ANK[:, :, :], MAGIC, None, ALU.subtract))
        flat = [a[:, :, :].rearrange("p r c -> p (r c)") for a in (ANG, ANK, ANR)]
        link(v.scalar_tensor_tensor(flat[2], flat[1], -c1, flat[0], ALU.mult, ALU.add))
        link(v.scalar_tensor_tensor(flat[2], flat[1], -c2, flat[2], ALU.mult, ALU.add))
        link(v.scalar_tensor_tensor(flat[2], flat[1], -c3, flat[2], ALU.mult, ALU.add))
        link(v.tensor_scalar(flat[0], flat[2], np.pi / 2, None, ALU.add))
        link(v.tensor_scalar(flat[1], flat[0], np.pi, TWO_PI, ALU.is_gt, ALU.mult))
        link(v.tensor_tensor(flat[1], flat[0], flat[1], ALU.subtract))
        link(v.tensor_scalar(flat[1], flat[1], PI_CAP, -PI_CAP, ALU.min, ALU.max))
        v.tensor_scalar(flat[2], flat[2], PI_CAP, -PI_CAP, ALU.min, ALU.max).then_inc(s["v_ang"], 1)
        dve.wait_ge(s["a_trig"], 1)
        v.tensor_scalar(NSIN[:, :, :], SIN[:, :, :], -1.0, None, ALU.mult).then_inc(s["v_nsin"], 1)

        def over(col, n):
            return col.unsqueeze(2).to_broadcast([P, RT, n])

        def rows(g, n):
            return g[:, :].unsqueeze(1).to_broadcast([P, RT, n])

        dve.wait_ge(s["a_ev"], 2 * KT)
        dve.wait_ge(s["a_trig"], 2)
        ac, ak = AC[:, :, 0:P], AC[:, :, P:P + HD]
        link(v.tensor_tensor(NTMP[:, :, :], ac, ac, ALU.mult))
        link(v.tensor_reduce(cols["ssn"][:, 0:8], NTMP[:, :, :], AX.X, ALU.add))
        link(v.tensor_reduce(cols["mu"], ak, AX.X, ALU.add))
        link(v.tensor_scalar(cols["mu"], cols["mu"], 1.0 / HD, None, ALU.mult))
        link(v.tensor_tensor(NXM[:, :, :], ak, over(cols["mu"], HD), ALU.subtract))
        link(v.tensor_tensor(NTMP[:, :, 0:HD], NXM[:, :, :], NXM[:, :, :], ALU.mult))
        link(v.tensor_reduce(cols["ssn"][:, 8:16], NTMP[:, :, 0:HD], AX.X, ALU.add))
        v.tensor_scalar(cols["vn"][:, 0:8], cols["ssn"][:, 0:8], 1.0 / P, EPS, ALU.mult, ALU.add)
        v.tensor_scalar(cols["vn"][:, 8:16], cols["ssn"][:, 8:16], 1.0 / HD, EPS, ALU.mult, ALU.add)\
         .then_inc(s["v_nrm"], 1)
        dve.wait_ge(s["p_nrs"], 1)
        link(v.tensor_tensor(NXM[:, :, :], NXM[:, :, :], over(cols["rsn"][:, 8:16], HD), ALU.mult))
        link(v.tensor_tensor(NXM[:, :, :], NXM[:, :, :], rows(IKG, HD), ALU.mult))
        v.tensor_tensor(KN[:, :, 0:HD], NXM[:, :, :], rows(IKB, HD), ALU.add)
        v.tensor_tensor(KN[:, :, HD:P], NXM[:, :, :], rows(IKB, HD), ALU.add).then_inc(s["v_kn"], 1)
        link(v.tensor_tensor(CKV[:, :, :], ac, over(cols["rsn"][:, 0:8], P), ALU.mult))
        v.tensor_tensor(CKV[:, :, :], CKV[:, :, :], rows(KVG, P), ALU.mult).then_inc(s["v_ckv"], 1)
        v.tensor_scalar(WI[:, :, :], AC[:, :, P + HD:SMALL], H ** -0.5 * HD ** -0.5, None, ALU.mult)\
         .then_inc(s["v_ac"], 1)
        dve.wait_ge(s["v_ac"], 1)

        for n in range((RT - B0) * H):
            b, h = B0 + n // H, n % H
            keys = (b + 1) * P
            dve.wait_ge(s["a_rl"], n + 1)
            if h:
                dve.wait_ge(s["v_acc"], n)
                ins = v.scalar_tensor_tensor(SC[b - B0][:, :], RL[n % 2][:, 0:keys], WI[:, b, h:h + 1],
                                             SC[b - B0][:, :], ALU.mult, ALU.add)
            else:
                ins = v.tensor_scalar(SC[b - B0][:, :], RL[n % 2][:, 0:keys], WI[:, b, h:h + 1], None, ALU.mult)
            ins.then_inc(s["v_acc"], 1)

        def pick_round(b):
            sc_b = SC[b - B0][:, :]
            v.max(M8[:, :], sc_b)
            dve.drain()
            v.match_replace(sc_b, M8[:, :], sc_b, PICKED)
            dve.drain()

        def picked_mask(b):
            sc_b = SC[b - B0][:, :]
            v.tensor_scalar(sc_b, sc_b, (NONCAUSAL + PICKED) / 2, MASKED, ALU.is_gt, ALU.mult).then_inc(s["v_mask"], 1)

        for b in range(B0, RT - 1):
            dve.wait_ge(s["p_caus"], b - B0 + 1)
            with dve.Fori(0, ROUNDS // UNROLL):
                for _ in range(UNROLL):
                    pick_round(b)
            picked_mask(b)

        def ret_norm(hp):
            o = O[hp % 2][:, :, :]
            o16 = o.rearrange("p r (h e) -> p (r h) e", h=2)
            t16 = PT1[:, :, :].rearrange("p r (h e) -> p (r h) e", h=2)
            y16 = Y[:, :, :].rearrange("p r (h e) -> p (r h) e", h=2)

            def per_head(c):
                return cols[c].unsqueeze(2).to_broadcast([P, 2 * RT, HD])

            def gains(g):
                return g[:, hp * P:(hp + 1) * P].unsqueeze(1).to_broadcast([P, RT, P])

            if hp == 0:
                dve.wait_ge(s["load_retg"], 48)
            dve.wait_ge(s["a_o"], RT * (hp + 1))
            link(v.tensor_reduce(cols["ssn"], o16, AX.X, ALU.add))
            link(v.tensor_scalar(cols["ssn"], cols["ssn"], 1.0 / HD, None, ALU.mult))
            if hp >= 1:
                dve.wait_ge(s["t_yr"], hp)
            link(v.tensor_tensor(y16, o16, per_head("ssn"), ALU.subtract))
            link(v.tensor_tensor(t16, y16, y16, ALU.mult))
            link(v.tensor_reduce(cols["ssn"], t16, AX.X, ALU.add))
            v.tensor_scalar(cols["vn"], cols["ssn"], 1.0 / HD, EPS, ALU.mult, ALU.add).then_inc(s["v_lnv"], 1)
            dve.wait_ge(s["p_lnr"], hp + 1)
            link(v.tensor_tensor(y16, y16, per_head("rsn"), ALU.mult))
            link(v.tensor_tensor(Y[:, :, :], Y[:, :, :], gains(RG), ALU.mult))
            link(v.tensor_tensor(Y[:, :, :], Y[:, :, :], gains(RB), ALU.add))
            dve.wait_ge(s["a_silu"], hp + 1)
            v.tensor_tensor(Y[:, :, :], Y[:, :, :], SGR[:, :, :], ALU.mult).then_inc(s["v_y"], 1)

        for hp in range(NP):
            ret_norm(hp)

        def mask_logits(t):
            b, h = divmod(t, H)
            keys = (b + 1) * P
            if h == 0:
                if b == 0:
                    dve.wait_ge(s["p_tri"], 1)
                elif b >= B0:
                    dve.wait_ge(s["v_mask"], b - B0 + 1)
            mask = SC[b - B0][:, :] if b >= B0 else TRI[:, 2 * P - keys:2 * P]
            dve.wait_ge(s["t_lg"], t + 1)
            if t >= 2:
                dve.wait_ge(s["t_tp"], tp_at[("tr", t - 2)] + 1)
            v.tensor_tensor_reduce(LM[t % 2][:, 0:keys], pair(t % 2, keys), mask, -1.0, 3.0e38, ALU.add, ALU.min,
                                   cols["nmax"][:, t % 4:t % 4 + 1]).then_inc(s["v_lm"], 1)

        def read_head_values(g):
            b, half = divmod(g, 2)
            c = (b % 2) * H + 4 * half
            dve.wait_ge(s["a_ex"], 4 * (g + 1))
            link(v.reciprocal(cols["rsum"][:, c:c + 4], cols["sum"][:, c:c + 4]))
            dve.wait_ge(s["t_ms"], ms_at[("y", g)] + 1)
            if half == 0 and b >= 1:
                dve.wait_ge(s["t_ms"], ms_at[("yt", b - 1)] + 1)
            v.tensor_tensor(YD[:, half * 256:(half + 1) * 256].rearrange("p (h e) -> p h e", h=4),
                            bank(7, 256).rearrange("p (h e) -> p h e", h=4),
                            cols["rsum"][:, c:c + 4].unsqueeze(2).to_broadcast([P, 4, HD]), ALU.mult)\
             .then_inc(s["v_ms"], 1)

        def variance(dst, src, b, n, after, sig):
            dve.wait_ge(s[after], b + 1)
            v.tensor_scalar(cols[dst][:, b:b + 1], cols[src][:, b:b + 1], 1.0 / n, EPS, ALU.mult, ALU.add)\
             .then_inc(s[sig], 1)

        def add_mix(b):
            if b == 0:
                dve.wait_ge(s["load_gain"], 32)
            dve.wait_ge(s["p_mr"], b + 1)
            link(v.scalar_tensor_tensor(MXS[:, :], MXS[:, :], cols["rsm"][:, b:b + 1], GPO[:, :], ALU.mult, ALU.mult))
            dve.wait_ge(load_xr[b % 2], 16 * (b // 2 + 1))
            v.tensor_tensor(XR[b % 2][:, :], XR[b % 2][:, :], MXS[:, :], ALU.add).then_inc(s["v_x1"], 1)

        def ffn_norm(b):
            dve.wait_ge(s["p_fr"], b + 1)
            if b >= 1:
                dve.wait_ge(s["t_tp"], tp_at[("ft", b - 1)] + 1)
            v.scalar_tensor_tensor(FN[:, :], XR[b % 2][:, :], cols["rsf"][:, b:b + 1], GPF[:, :], ALU.mult, ALU.mult)\
             .then_inc(s["v_fn"], 1)

        dve.wait_ge(s["p_caus"], RT - B0)
        for t in range(STEPS + TAIL):
            if t < STEPS:
                mask_logits(t)
            if at_half(t, 3) is not None:
                read_head_values(at_half(t, 3))
            if at_block(t, 6) is not None:
                variance("vm", "ssm", at_block(t, 6), D, "a_mss", "v_mv")
            if at_block(t, 7) is not None:
                add_mix(at_block(t, 7))
            if at_block(t, 8) is not None:
                variance("vf", "ssf", at_block(t, 8), D, "a_fss", "v_fv")
            if at_block(t, 9) is not None:
                ffn_norm(at_block(t, 9))
            if H <= t < H + ROUNDS:
                pick_round(RT - 1)
                if t == H + ROUNDS - 1:
                    picked_mask(RT - 1)

        for k in range(KT):
            dve.wait_ge(s["a_fth"], k + 1)
            v.tensor_tensor(FTL[:, k, :], FTR[:, k, :], FTH[:, k, :].bitcast(F32), ALU.subtract)\
             .then_inc(s["v_ftl"], 1)
            if k == 0:
                dve.wait_ge(s["a_gh"], 1)
                v.tensor_tensor(WL[0][:, :, :, :], WR[0][:, :, :, :], WH[0][:, :, :, :].bitcast(F32), ALU.subtract)\
                 .then_inc(s["v_gl"], 1)

        def gate_lo(slot, f):
            dve.wait_ge(s["a_gh"], f + 1)
            v.tensor_tensor(WL[slot][:, :, :, :], WR[slot][:, :, :, :], WH[slot][:, :, :, :].bitcast(F32),
                            ALU.subtract).then_inc(s["v_gl"], 1)

        def hidden(slot, f, half):
            dve.wait_ge(s["a_sg"], f * 2 + (half + 1))
            v.tensor_tensor(HT[:, bass.ds(f, 1), half * 512:(half + 1) * 512], SG[half][:, :].unsqueeze(1),
                            bank(4 * slot + 2 * half + 1).unsqueeze(1), ALU.mult).then_inc(s["v_ht"], 1)

        gate_lo(1, 1)
        for half in range(2):
            hidden(0, 0, half)
        with dve.Fori(1, FT // 2) as i:
            gate_lo(0, i * 2)
            for half in range(2):
                hidden(1, i * 2 - 1, half)
            gate_lo(1, i * 2 + 1)
            for half in range(2):
                hidden(0, i * 2, half)
        for half in range(2):
            hidden(1, FT - 1, half)

        def down_lo(slot, n, f):
            dve.wait_ge(s["a_dwh"], n + 1)
            v.tensor_tensor(DL[slot][:, :], DR[slot][:, :], DH[slot][:, :].bitcast(F32), ALU.subtract)\
             .then_inc(s["v_dwl"], 1)
            dve.wait_ge(s["a_dhh"], n + 1)
            v.tensor_tensor(HTL[slot][:, :].unsqueeze(1), HT[:, bass.ds(f, 1), :],
                            HTH[slot][:, :].bitcast(F32).unsqueeze(1), ALU.subtract).then_inc(s["v_dhl"], 1)

        dve.wait_ge(s["v_ht"], 2 * FT)
        with dve.Fori(0, FT // 2) as i:
            for t in range(2):
                down_lo(t, i * 2 + t, i * 2 + t)
        for t in range(2):
            down_lo(t, FT + t, t)
        for r in range(1, RT, 2):
            dve.wait_ge(s["t_acc"], r + 1)
            v.tensor_copy(FO0[:, r, :], bank(r)).then_inc(s["v_fo"], 1)
        with dve.Fori(1, FT // 2) as i:
            for t in range(2):
                down_lo(t, i * 2 + (FT + t), i * 2 + t)
        for r in range(1, RT, 2):
            dve.wait_ge(s["t_acc"], RT + r + 1)
            v.tensor_copy(FO1[:, r, :], bank(r)).then_inc(s["v_fo"], 1)

        def ple_lo(n):
            dve.wait_ge(s["a_wgh"], n + 1)
            k, dh = divmod(n if n < 4 else n - 4, 2)
            hi, lo = (WUH, WUL) if n < 4 else (WGH, WGL)
            ds = slice(dh * 512, (dh + 1) * 512)
            v.tensor_tensor(lo[:, k, ds], WGR[n % 3][:, :], hi[:, k, ds].bitcast(F32), ALU.subtract)\
             .then_inc(s["v_wgl"], 1)

        def out_variance(r):
            dve.wait_ge(s["a_css"], 2 * r + 2)
            link(v.tensor_tensor(SMF[:, 2 * r:2 * r + 1], SMF[:, 2 * r:2 * r + 1], SMF[:, 2 * r + 1:2 * r + 2], ALU.add))
            v.tensor_scalar(SMF[:, 16 + r:17 + r], SMF[:, 2 * r:2 * r + 1], 1.0 / D, EPS, ALU.mult, ALU.add)\
             .then_inc(s["v_wv"], 1)

        def make_x2(r):
            dve.wait_ge(s["p_wr"], r + 1)
            dve.wait_ge(load_x2[r % 3], 16 * (r // 3 + 1))
            if r == 0:
                dve.wait_ge(s["load_gain2"], 32)
            for dh, fo in enumerate((FO0, FO1)):
                ds = slice(dh * 512, (dh + 1) * 512)
                ins = v.scalar_tensor_tensor(fo[:, r, :], fo[:, r, :], SMF[:, 24 + r:25 + r], GPF2[:, ds],
                                             ALU.mult, ALU.mult)
                link(ins)
                ins = v.tensor_tensor(X2[r % 3][:, ds], X2[r % 3][:, ds], fo[:, r, :], ALU.add)
            ins.then_inc(s["v_x2"], 1)

        def x2_lo(r):
            dve.wait_ge(s["a_x2h"], r + 1)
            v.tensor_tensor(X2L[r % 2][:, :, :], pair(r % 2).rearrange("p (k c) -> p k c", k=KT),
                            X2H[r % 2][:, :, :].bitcast(F32), ALU.subtract).then_inc(s["v_x2l"], 1)

        out_variance(0)
        for n in range(4):
            ple_lo(n)
        for k in range(2):
            dve.wait_ge(s["a_pth"], k + 1)
            v.tensor_tensor(PTL[:, k, :], pair(k), PTH[:, k, :].bitcast(F32), ALU.subtract).then_inc(s["v_ptl"], 1)
        make_x2(0)
        for n in range(4, 20):
            ple_lo(n)
            if n == 8:
                x2_lo(0)
            if n in (5, 11, 17):
                out_variance((n + 1) // 6)
        make_x2(1)
        for r in range(RT):
            if r + 1 < RT:
                x2_lo(r + 1)
            if r + 4 < RT and r >= 0:
                pass
            dve.wait_ge(s["a_sig"], r + 1)
            dve.wait_ge(s["t_em"], r + 1)
            if r >= 2:
                dve.wait_ge(st_out[r % 2], 16 * (r // 2))
            v.tensor_tensor(UU[r % 2][:, :], pair(3), SGG[:, :], ALU.mult).then_inc(s["v_u"], 1)
            if r + 2 < RT:
                make_x2(r + 2)
            dve.wait_ge(s["a_uss"], r + 1)
            v.tensor_scalar(SMF[:, 40 + r:41 + r], SMF[:, 32 + r:33 + r], 1.0 / D, EPS, ALU.mult, ALU.add)\
             .then_inc(s["v_uv"], 1)
            if r + 4 < RT:
                out_variance(r + 4)
            dve.wait_ge(s["p_ur"], r + 1)
            link(v.scalar_tensor_tensor(UU[r % 2][:, :], UU[r % 2][:, :], SMF[:, 48 + r:49 + r], GPL[:, :],
                                        ALU.mult, ALU.mult))
            v.tensor_tensor(UU[r % 2][:, :], UU[r % 2][:, :], X2[r % 3][:, :], ALU.add).then_inc(s["v_out"], 1)

    @block.gpsimd
    def _(pool):
        g_ = nc.gpsimd
        made = [0]

        def link(ins):
            made[0] += 1
            ins.then_inc(s["p_link"], 1)
            pool.wait_ge(s["p_link"], made[0])

        def rsqrt(dst, src):
            n = src.shape[1]
            return g_.tensor_tensor(dst, src, cols["half"][:, 0:n], ALU.pow)

        def w_lo(n):
            c, k = divmod(n, KT)
            w = width(c)
            pool.wait_ge(s["a_whi"], n + 1)
            g_.tensor_tensor(WBL[c % 2][:, k, 0:w], RAW[n % 4][:, 0:w], WBH[c % 2][:, k, 0:w].bitcast(F32),
                             ALU.subtract).then_inc(s["p_wlo"], 1)

        link(g_.memset(cols["half"], -0.5))
        for r in range(RT + 2):
            if r < RT:
                pool.wait_ge(s["v_var"], r + 1)
                rsqrt(cols["rs0"][:, r:r + 1], cols["v0"][:, r:r + 1]).then_inc(s["p_rs"], 1)
            if r >= 2:
                w_lo(r - 2)
        link(g_.memset(TRI[:, :], 0.0))
        g_.affine_select(out=TRI[:, P:2 * P], in_=TRI[:, P:2 * P], compare_op=ALU.is_ge, fill=MASKED, base=0,
                         pattern=[[-1, P]], channel_multiplier=1).then_inc(s["p_tri"], 1)
        for n in range(KT, 3 * KT):
            w_lo(n)
        pool.wait_ge(s["v_nrm"], 1)
        rsqrt(cols["rsn"], cols["vn"]).then_inc(s["p_nrs"], 1)

        for b in range(B0, RT):
            pool.wait_ge(s["v_acc"], H * (b - B0 + 1))
            diag = SC[b - B0][:, b * P:(b + 1) * P]
            g_.affine_select(out=diag, in_=diag, compare_op=ALU.is_ge, fill=NONCAUSAL, base=0,
                             pattern=[[-1, P]], channel_multiplier=1).then_inc(s["p_caus"], 1)

        def rotate(n):
            r = n % RT
            st = STG[n % 2]
            pool.wait_ge(s["a_ev"], 2 * KT + n + 1)
            if n == 0:
                pool.wait_ge(s["a_trig"], 2)
                pool.wait_ge(s["v_nsin"], 1)
            else:
                pool.wait_ge(s["p_rot"], n)
            x8 = st[:, 0:256].rearrange("p (g c) -> p g c", c=32)
            x4 = st[:, 0:256].rearrange("p (g a c) -> p g a c", a=2, c=32)
            t4 = RT2[:, :].rearrange("p (g a c) -> p g a c", a=2, c=32)
            cos8 = COS[:, r, :].unsqueeze(1).to_broadcast([P, 8, 32])
            sin4, nsin4 = (a[:, r, :].unsqueeze(1).to_broadcast([P, 4, 32]) for a in (SIN, NSIN))
            g_.tensor_tensor(RT1[:, :].rearrange("p (g c) -> p g c", c=32), x8, cos8, ALU.mult)
            g_.tensor_tensor(t4[:, :, 0, :], x4[:, :, 1, :], nsin4, ALU.mult)
            link(g_.tensor_tensor(t4[:, :, 1, :], x4[:, :, 0, :], sin4, ALU.mult))
            g_.tensor_tensor(st[:, 0:256], RT1[:, :], RT2[:, :], ALU.add).then_inc(s["p_rot"], 1)

        for g in range(2 * KT, LAST):
            if g + KT < LAST:
                w_lo(g + KT)
            if g < 6 * KT:
                rotate(g - 2 * KT)

        def next_state(n):
            hp, r = divmod(n, RT)
            pool.wait_ge(s["a_rb"], n + 1)
            if r == 0 and hp >= 2:
                pool.wait_ge(s["t_ro"], RT * (hp - 1))
            kv, rs = QKT[hp % 2][:, r, 2 * P:3 * P], RST[hp % 2]
            link(g_.tensor_tensor(rs[:, r + 1, :], rs[:, r, :], kv, ALU.add))
            ins = g_.tensor_tensor(rs[:, r + 1, :], rs[:, r + 1, :], CD[:, hp, :], ALU.mult)
            ins.then_inc(s["p_rst"], 1)
            pool.wait_ge(s["p_rst"], hp * (RT - 1) + r + 1)

        def causal_scores(n):
            pool.wait_ge(s["a_st"], n + 1)
            st = ST[n % 2][:, :].rearrange("p (h i) -> p h i", h=2)
            g_.affine_select(out=st, in_=st, compare_op=ALU.is_ge, fill=0.0, base=0,
                             pattern=[[0, 2], [1, P]], channel_multiplier=-1).then_inc(s["p_st"], 1)

        pool.wait_ge(s["t_unit"], LAST)
        for i in range(2):
            g_.memset(RST[i][:, :, :], 0.0).then_inc(s["p_zero"], 1)
        pool.wait_ge(s["p_zero"], 2)
        pool.wait_ge(s["load_retg"], 48)
        for r in range(RT - 1):
            next_state(r)
        for hp in range(NP):
            for r in range(RT):
                if r < RT - 1 and hp + 1 < NP:
                    next_state((hp + 1) * RT + r)
                causal_scores(hp * RT + r)
            if hp >= 1:
                pool.wait_ge(s["v_lnv"], hp)
                rsqrt(cols["rsn"], cols["vn"]).then_inc(s["p_lnr"], 1)
        pool.wait_ge(s["v_lnv"], NP)
        rsqrt(cols["rsn"], cols["vn"]).then_inc(s["p_lnr"], 1)

        for b in range(RT):
            pool.wait_ge(s["v_mv"], b + 1)
            rsqrt(cols["rsm"][:, b:b + 1], cols["vm"][:, b:b + 1]).then_inc(s["p_mr"], 1)
            pool.wait_ge(s["v_fv"], b + 1)
            rsqrt(cols["rsf"][:, b:b + 1], cols["vf"][:, b:b + 1]).then_inc(s["p_fr"], 1)

        def out_rsqrt(r):
            pool.wait_ge(s["v_wv"], r + 1)
            rsqrt(SMF[:, 24 + r:25 + r], SMF[:, 16 + r:17 + r]).then_inc(s["p_wr"], 1)

        for r in range(4):
            out_rsqrt(r)
        for r in range(RT):
            pool.wait_ge(s["v_uv"], r + 1)
            rsqrt(SMF[:, 48 + r:49 + r], SMF[:, 40 + r:41 + r]).then_inc(s["p_ur"], 1)
            if r + 4 < RT:
                out_rsqrt(r + 4)

    ctx.close()


_INS = ["x", "p", "positions", "pre_mix_g", "w_in", "ret_norm_g", "ret_norm_b", "kv_norm_g", "idx_k_norm_g",
        "idx_k_norm_b", "w_uk", "w_uv", "w_out", "post_mix_g", "pre_ffn_g", "w_ffn_gate", "w_ffn_up",
        "w_ffn_down", "post_ffn_g", "w_ple_up", "w_ple_gate", "ple_norm_g"]


def kernel(**inputs):
    import concourse.bacc as bacc
    from concourse.bass_utils import run_bass_kernel_spmd

    nc = bacc.Bacc("TRN2", target_bir_lowering=False, num_devices=1)
    arrays, args = {}, []
    inv_freq, small, decay = shape_tables()
    for name, a in [(n, inputs[n]) for n in _INS] + [("inv_freq", inv_freq), ("small_tab", small), ("decay_tab", decay)]:
        a = np.ascontiguousarray(a)
        arrays[f"in_{name}"] = a
        args.append(nc.dram_tensor(f"in_{name}", a.shape, mybir.dt.from_np(a.dtype), kind="ExternalInput").ap())
    args.append(nc.dram_tensor("out_0", (1, S, D), F32, kind="ExternalOutput").ap())
    args.append(nc.dram_tensor("x1_rows", (S, D), F32, kind="Internal").ap())
    args.append(nc.dram_tensor("ret_rows", (NP, S, 512), F32, kind="Internal").ap())
    build(nc, *args)
    r = run_bass_kernel_spmd(nc, [arrays], core_ids=[0])
    return r.results[0]["out_0"]
```

```python
from contextlib import ExitStack

import numpy as np

import concourse.bass as bass
from concourse import mybir

F32 = mybir.dt.float32
F32R = mybir.dt.float32r
I32 = mybir.dt.int32
ALU = mybir.AluOpType
ACT = mybir.ActivationFunctionType
AX = mybir.AxisListType

P = 128
S = 1024
D = 1024
RT = S // P
KT = D // P
H = 8
HD = 64
NP = H // 2
FF = 2816
FT = FF // P
PLE = 256
TOPK = 256
B0 = TOPK // P
C_RET, C_AQ, C_AC, C_IQ, C_IK, C_IW = 0, 2048, 2560, 2688, 3200, 3264
SMALL = P + HD + H
RW = 640
RV, RG_ = 2 * P, 4 * P
EPS = 1e-6
NONCAUSAL = -3.0e38
PICKED = -3.4e38
MASKED = -1.0e30
ROUNDS = TOPK // 8
UNROLL = 8
TWO_PI = 2.0 * np.pi
MAGIC = 12582912.0
PI_CAP = 3.1415925


def shape_tables():
    inv_freq = (1.0 / (10000.0 ** (np.arange(0, HD, 2, dtype=np.float64) / HD))).astype(np.float32)
    g = 1.0 - 2.0 ** (-5.0 - np.arange(H, dtype=np.float64))
    i = np.arange(P, dtype=np.float64)[:, None]
    q_scale = g[None, :] ** (i + 1.0)
    k_scale = g[None, :] ** (-(i + 1.0)) * HD ** -0.5
    small = np.concatenate([q_scale, k_scale, np.eye(P)], axis=1).astype(np.float32)
    same_head = np.kron(np.eye(2), np.ones((HD, HD)))
    chunk_decay = same_head[:, None, :] * np.repeat((g ** P).reshape(NP, 2), HD, axis=1)[None]
    return np.tile(inv_freq, (P, 1)), small, chunk_decay.astype(np.float32)


def cody_waite():
    c1 = 6.28125
    c2 = float(np.float32(TWO_PI - c1))
    c2 = float(np.float32(np.round(c2 * 2.0 ** 20) / 2.0 ** 20))
    return c1, c2, float(np.float32(TWO_PI - c1 - c2))


def build(nc, x, p, positions, pre_mix_g, w_in, ret_norm_g, ret_norm_b, kv_norm_g, idx_k_norm_g,
          idx_k_norm_b, w_uk, w_uv, w_out, post_mix_g, pre_ffn_g, w_ffn_gate, w_ffn_up, w_ffn_down,
          post_ffn_g, w_ple_up, w_ple_gate, ple_norm_g, inv_freq, small_tab, decay_tab, out, x1_dram, ret_dram):
    ctx = ExitStack()
    base = 16512
    kb = 1024

    def sb(name, shape, at, dt=F32):
        return nc.alloc_sbuf_tensor_at(name, shape, dt, offset=base + int(at * kb))

    def sem(name):
        return nc.alloc_semaphore(name)

    TAB = sb("tab", [P, 2 * H + P], 0)
    QSC, KSC, ID = TAB[:, 0:H], TAB[:, H:2 * H], TAB[:, 2 * H:]
    SML = sb("sml", [P, 256], 0.75)
    KVG = sb("kvg", [P, P], 1.75)
    IKG = sb("ikg", [P, HD], 2.25)
    IKB = sb("ikb", [P, HD], 2.5)
    INV = sb("inv", [P, 32], 2.75)
    COS = sb("cos", [P, RT, 32], 3)
    SIN = sb("sin", [P, RT, 32], 4)
    RT2 = sb("rt2", [P, 256], 5)
    TRI = sb("tri", [P, 2 * P], 6)
    WI = sb("wi", [P, RT, H], 7)
    M8 = sb("m8", [P, 8], 7.25)
    POSI = sb("posi", [P, RT], 7.3125, I32)

    cols = {}
    at = 0
    for name, n in (("ss0", 8), ("v0", 8), ("rs0", 8), ("half", 16), ("ssn", 16), ("vn", 16), ("rsn", 16),
                    ("mu", 8), ("pos", 8), ("sum", 16), ("rsum", 16), ("nmax", 4), ("ssm", 8), ("vm", 8),
                    ("rsm", 8), ("ssf", 8), ("vf", 8), ("rsf", 8), ("cap", 1)):
        cols[name] = SML[:, at:at + n]
        at += n
    assert at <= 256

    XTH = sb("xth", [P, KT, S], 12, F32R)
    XTL = sb("xtl", [P, KT, S], 44, F32R)
    WBH = [sb(f"wbh{i}", [P, KT, 512], 76 + 32 * i, F32R) for i in range(2)]
    WBL = [sb(f"wbl{i}", [P, KT, 512], 92 + 32 * i, F32R) for i in range(2)]
    XN = sb("xn", [P, RT, D], 108)
    RAW = [sb(f"raw{i}", [P, 512], 140 + 2 * i) for i in range(4)]
    QW = S - B0 * P
    QS = sb("qs", [P, H, QW], 148, F32R)
    AQ = sb("aq", [P, NP, S], 148)
    CKVT = sb("ckvt", [P, S], 164)
    CKV = sb("ckv", [P, RT, P], 172)
    sc_off = [sum(range(B0 + 1, b + 1)) * P for b in range(B0, RT)]
    SC = [sb(f"sc{b}", [P, (b + 1) * P], 176 + sc_off[b - B0] * 4 / kb) for b in range(B0, RT)]
    GIN = sb("gin", [P, D], 176)
    ANG = sb("ang", [P, RT, 32], 180)
    ANK = sb("ank", [P, RT, 32], 181)
    ANR = sb("anr", [P, RT, 32], 182)
    NTMP = sb("ntmp", [P, RT, P], 176)
    NXM = sb("nxm", [P, RT, HD], 184)
    KN = sb("kn", [P, RT, P], 186)
    KH = sb("kh", [P, S], 192.5, F32R)
    KL = sb("kl", [P, S], 196.5, F32R)
    AC = sb("ac", [P, RT, SMALL], 200.5)
    STG = [sb(f"stg{i}", [P, RW], 200.5 + 2.5 * i) for i in range(2)]
    RT1 = sb("rt1", [P, 256], 205.5)

    RP = [sb(f"rp{i}", [P, RT, RW], 108 + 20 * i) for i in range(2)]
    QKT = [sb("qkt0", [P, RT, 384], 60), sb("qkt1", [P, RT, 384], 24)]
    ST = [sb(f"st{i}", [P, 256], 36 + i) for i in range(2)]
    RST = [sb("rst0", [P, RT, P], 72), sb("rst1", [P, RT, P], 54)]
    CD = sb("cd", [P, NP, P], 38)
    O = [sb(f"o{i}", [P, RT, P], 42 + 4 * i) for i in range(2)]
    SGR = sb("sgr", [P, RT, P], 50)
    PT1 = sb("pt1", [P, RT, P], 20)
    Y = sb("y", [P, RT, P], 12)
    RG = sb("rg", [P, 512], 16)
    RB = sb("rb", [P, 512], 18)
    YRT = [sb(f"yrt{i}", [P, S], a) for i, a in enumerate((168, 192.5, 196.5, 200.5))]

    WO = sb("wo", [P, KT, D], 76)
    WUK = sb("wuk", [P, H, P], 64)
    WUV = sb("wuv", [P, H, P], 68)
    FTR = sb("ftr", [P, KT, S], 12)
    XR = [sb(f"xr{i}", [P, D], 44 + 4 * i) for i in range(2)]
    GPO = sb("gpo", [P, D], 52)
    GPF = sb("gpf", [P, D], 56)
    QL = [sb("ql0", [P, H, P], 108), sb("ql1", [P, H, P], 60)]
    LM = [sb(f"lm{i}", [P, S], 112 + 4 * i) for i in range(2)]
    PT = [sb(f"pt{i}", [P, S], 120 + 4 * i) for i in range(2)]
    OTS = [sb(f"ots{i}", [P, 512], 128 + 2 * i) for i in range(2)]
    YD = sb("yd", [P, 512], 132)
    YDT = sb("ydt", [P, NP, P], 134)
    MXS = sb("mxs", [P, D], 136)
    FN = sb("fn", [P, D], 140)
    JK = sb("jk", [P, D], 144)

    FTH = sb("fth", [P, KT, S], 44, F32R)
    FTL = sb("ftl", [P, KT, S], 12, F32R)
    HT = sb("ht", [P, FT, S], 76)
    WR = [sb("wr0", [P, 2, KT, P], 2), sb("wr1", [P, 2, KT, P], 164)]
    WH = [sb(f"wh{i}", [P, 2, KT, P], 172 + 16 * i, F32R) for i in range(2)]
    WL = [sb(f"wl{i}", [P, 2, KT, P], 180 + 16 * i, F32R) for i in range(2)]
    SG = [sb("sg0", [P, 512], 204), sb("sg1", [P, 512], 10)]
    HTH = [sb(f"hth{i}", [P, S], 164 + 8 * i, F32R) for i in range(2)]
    HTL = [sb(f"htl{i}", [P, S], 168 + 8 * i, F32R) for i in range(2)]
    DR = [sb(f"dr{i}", [P, 512], 180 + 2 * i) for i in range(2)]
    DH = [sb(f"dh{i}", [P, 512], 188 + 4 * i, F32R) for i in range(2)]
    DL = [sb(f"dl{i}", [P, 512], 190 + 4 * i, F32R) for i in range(2)]
    FO0 = sb("fo0", [P, RT, 512], 28)
    FO1 = sb("fo1", [P, RT, 512], 12)

    WGH = sb("wgh", [P, KT, D], 76, F32R)
    WGL = sb("wgl", [P, KT, D], 108, F32R)
    WUH = sb("wuh", [P, 2, D], 140, F32R)
    WUL = sb("wul", [P, 2, D], 148, F32R)
    PTH = sb("pth", [P, 2, S], 156, F32R)
    PTL = sb("ptl", [P, 2, S], 164, F32R)
    X2 = [sb(f"x2{i}", [P, D], 172 + 4 * i) for i in range(3)]
    X2H = [sb(f"x2h{i}", [P, KT, P], 44 + 8 * i, F32R) for i in range(2)]
    X2L = [sb(f"x2l{i}", [P, KT, P], 48 + 8 * i, F32R) for i in range(2)]
    GPF2 = sb("gpf2", [P, D], 60)
    GPL = sb("gpl", [P, D], 64)
    SGG = sb("sgg", [P, D], 68)
    UU = [sb("uu0", [P, D], 72), sb("uu1", [P, D], 184)]
    JF = sb("jf", [P, D], 188)
    PN = sb("pn", [P, RT, PLE], 192)
    WGR = [sb(f"wgr{i}", [P, 512], 200 + 2 * i) for i in range(3)]
    SMF = sb("smf", [P, 64], 206.25)

    PS = ctx.enter_context(nc.psum_tensor("ps", [P, 8 * 512], F32))

    def bank(i, n=512):
        return PS[:, 512 * i:512 * i + n]

    names = """a_sq v_var p_rs v_xn t_xt a_xh v_xl p_half v_ang a_trig a_whi v_qlo a_kh v_kl p_pad p_wz p_wlo t_unit a_ev
        v_link p_link v_nrm p_nrs v_kn v_ckv v_wi v_ac t_nt a_nt t_ix a_rl v_acc p_caus v_mask p_tri p_rot
        t_rb a_rb p_rst t_sc a_st p_st t_ro a_o a_silu p_zero v_lnv p_lnr v_y t_yr a_yrt
        t_lg v_lm a_ex t_tp a_tp t_pv a_ots t_ms a_ms v_ms a_mss v_mv p_mr v_x1 a_fss v_fv p_fr v_fn
        a_fth v_ftl a_gh v_gl t_gu a_sg v_ht a_dwh v_dwl a_dhh v_dhl t_dn t_acc a_fo v_fo
        a_wgh v_wgl t_pt a_pth v_ptl a_css v_wv p_wr v_x2 t_x2 a_x2h v_x2l t_gt t_em a_sig v_u a_uss v_uv p_ur
        v_out load_cd load_tab load_pos load_const load_gin load_gain load_wuk load_wo load_retg load_pn load_gain2 st_x1""".split()
    s = {n: sem(n) for n in names}
    load_x = [sem(f"load_x{i}") for i in range(RT)]
    load_raw = [sem(f"load_raw{i}") for i in range(4)]
    st_ret = [sem(f"st_ret{i}") for i in range(2)]
    st_out = [sem(f"st_out{i}") for i in range(2)]
    load_rp = [sem(f"load_rp{i}") for i in range(2)]
    load_xr = [sem(f"load_xr{i}") for i in range(2)]
    load_wr = [sem(f"load_wr{i}") for i in range(2)]
    load_dr = [sem(f"load_dr{i}") for i in range(2)]
    load_wg = [sem(f"load_wg{i}") for i in range(3)]
    load_x2 = [sem(f"load_x2{i}") for i in range(3)]

    NCH = 7
    block = ctx.enter_context(nc.Block())


    def pair(j, n=1024):
        return PS[:, 1024 * j:1024 * j + n]

    def raw_count(n):
        return 16 * sum(2 if m // KT == 1 else 1 for m in range(n % 4, n + 1, 4))

    def width(c):
        return SMALL if c == 1 else 512

    def unit_width(g):
        return 512 - B0 * P if g < 4 else width(g // KT)

    IX0, ITEMS, PER = 2 * KT + 2, (RT - B0) * H, 3

    def items(g):
        return range(max(0, (g - IX0) * PER), min(ITEMS, (g - IX0 + 1) * PER)) if g >= IX0 else range(0)

    EARLY = 24
    BESIDE = {0: 4, 1: 6, 2: 8, 3: 12, 4: 10, 5: 16, 6: 16}
    MIX_ROUNDS = 4
    beside = [(RT - 3, n) for n in range(EARLY, ROUNDS)] + [(b, n) for b in (RT - 2, RT - 1) for n in range(ROUNDS)]
    assert sum(BESIDE.values()) == len(beside)
    assert all(sum(BESIDE[i] for i in range(b)) >= sum(c[0] <= b for c in beside) for b in range(RT - 3, RT))

    def rounds_beside(t):
        b, h = divmod(t, H)
        n = BESIDE.get(b, 0)
        m = min(n // 2, MIX_ROUNDS)
        return (n - m) * (h + 1) // H - (n - m) * h // H + (m if h == 4 else 0)

    HALF = (slice(0, HD), slice(HD, P))

    def query_cols(g):
        return slice(0, 512 - B0 * P) if g < 4 else slice(512 - B0 * P, S - B0 * P)

    LAST = NCH * KT
    SAHEAD = 2
    RAHEAD = 3
    STEPS = RT * H
    ADD_LAG, SQ_LAG, FV_LAG, FN_LAG, FT_LAG = 8, 8, 9, 10, 11
    TAIL = FT_LAG + 1
    YR_STEP = 8

    def at_block(t, lag):
        b, h = divmod(t - lag, H)
        return b if h == H - 1 and 0 <= b < RT else None

    def at_half(t, lag):
        g, h = divmod(t - lag, 4)
        return g if h == 3 and 0 <= g < 2 * RT else None

    def ql_due(t):
        b, h = divmod(t + 4, H)
        return (b, h) if h < 2 and 1 <= b < RT else None

    tp_use, ms_use = [], [("ql", 0, 0), ("ql", 0, 1)]
    for t in range(STEPS + TAIL):
        if at_block(t, 5) is not None:
            tp_use.append(("mx", at_block(t, 5)))
        if 1 <= t <= STEPS:
            tp_use.append(("tr", t - 1))
        if t == YR_STEP:
            tp_use.append(("yr",))
        if at_block(t, FT_LAG) is not None:
            tp_use.append(("ft", at_block(t, FT_LAG)))
        if ql_due(t) is not None:
            ms_use.append(("ql", *ql_due(t)))
        if at_half(t, 3) is not None:
            ms_use.append(("y", at_half(t, 3)))
        if at_block(t, 4) is not None:
            ms_use.append(("yt", at_block(t, 4)))
    tp_at = {u: n for n, u in enumerate(tp_use)}
    ms_at = {u: n for n, u in enumerate(ms_use)}

    def ms_read(n):
        v = sum(u[0] == "y" for u in ms_use[:n])
        return n - v, v

    @block.sync
    def _(sp):
        x_t = x.rearrange("b (r p) d -> p (b r) d", p=P)

        def row_gain(dst, g, sm):
            sp.dma_start(dst[:, :], g[0:1, :].to_broadcast([P, g.shape[1]])).then_inc(s[sm], 16)

        def proj_weights(n):
            c, k = divmod(n, KT)
            if n >= 4:
                sp.wait_ge(s["a_whi"], n - 3)
                sp.wait_ge(s["p_wlo"], n - 3)
            dst, sm = RAW[n % 4], load_raw[n % 4]
            w = w_in[0, k * P:(k + 1) * P, :]
            if c == 0:
                sp.dma_start(dst[:, :], w[:, C_IQ:C_IQ + 512]).then_inc(sm, 16)
            elif c == 1:
                sp.dma_start(dst[:, 0:P], w[:, C_AC:C_AC + P]).then_inc(sm, 16)
                sp.dma_start(dst[:, P:SMALL], w[:, C_IK:C_IK + HD + H]).then_inc(sm, 16)
            elif c == 6:
                sp.dma_start(dst[:, :], w[:, C_AQ:C_AQ + 512]).then_inc(sm, 16)
            else:
                src = w[:, 0:4 * 512].rearrange("p (g c) -> p g c", g=4)[:, :, (c - 2) * P:(c - 1) * P]
                sp.dma_start(dst[:, :].rearrange("p (g c) -> p g c", g=4), src).then_inc(sm, 16)

        def store_retention(n):
            hp, r = divmod(n, RT)
            sp.wait_ge(s["p_rot"], n + 1)
            sp.dma_start(ret_dram[hp, r * P:(r + 1) * P, :], STG[n % 2][:, :]).then_inc(st_ret[n % 2], 16)

        sp.dma_start(XN[:, 0, :], x_t[:, 0, :]).then_inc(load_x[0], 16)
        row_gain(GIN, pre_mix_g, "load_gin")
        sp.dma_start(TAB[:, :], small_tab).then_inc(s["load_tab"], 16)
        for r in range(1, 4):
            sp.dma_start(XN[:, r, :], x_t[:, r, :]).then_inc(load_x[r], 16)
        for n in range(4):
            proj_weights(n)
        with nc.allow_non_contiguous_dma(reason="1024 positions, once"):
            sp.dma_start(POSI[:, :], positions[0].rearrange("(r p) -> p r", p=P)).then_inc(s["load_pos"], 16)
        sp.dma_start(INV[:, :], inv_freq).then_inc(s["load_pos"], 16)
        for r in range(4, RT):
            sp.dma_start(XN[:, r, :], x_t[:, r, :]).then_inc(load_x[r], 16)
        row_gain(KVG, kv_norm_g, "load_const")
        row_gain(IKG, idx_k_norm_g, "load_const")
        row_gain(IKB, idx_k_norm_b, "load_const")
        for g in range(-8, LAST):
            if 4 <= g + 12 < LAST:
                proj_weights(g + 12)
            if 0 <= g - 17 < NP * RT:
                store_retention(g - 17)
        sp.wait_ge(s["t_unit"], 6 * RT)
        for hp in range(NP):
            for i in range(2):
                sp.wait_ge(st_ret[i], 16 * 4 * (hp + 1))
            if hp == 1:
                sp.wait_ge(s["t_unit"], LAST)
                sp.dma_start(CD[:, :, :], decay_tab).then_inc(s["load_cd"], 16)
            if hp >= 2:
                sp.wait_ge(s["t_ro"], RT * (hp - 1))
                sp.wait_ge(s["a_silu"], hp - 1)
            sp.dma_start(RP[hp % 2][:, :, :], ret_dram[hp].rearrange("(r p) c -> p r c", p=P))\
              .then_inc(load_rp[hp % 2], 16)
            if hp == 1:
                for dst, g in ((RG, ret_norm_g), (RB, ret_norm_b)):
                    sp.dma_start(dst[:, :], g[0:1].rearrange("a h d -> a (h d)").to_broadcast([P, 512]))\
                      .then_inc(s["load_retg"], 16)
                sp.dma_start(WO[:, :, :], w_out[0].rearrange("(k p) d -> p k d", p=P)).then_inc(s["load_wo"], 16)
        sp.wait_ge(s["p_wz"], 2)
        for h in range(H):
            j = HD * (h % 2)
            sp.dma_start(WUK[j:j + HD, h, :], w_uk[0, h]).then_inc(s["load_wuk"], 16)
            sp.dma_start(WUV[:, h, j:j + HD], w_uv[0, h]).then_inc(s["load_wuk"], 16)
        sp.wait_ge(s["v_y"], NP)
        row_gain(GPO, post_mix_g, "load_gain")
        row_gain(GPF, pre_ffn_g, "load_gain")
        for b in range(2):
            sp.dma_start(XR[b][:, :], x_t[:, b, :]).then_inc(load_xr[b], 16)
        for b in range(RT):
            sp.wait_ge(s["v_x1"], b + 1)
            sp.dma_start(x1_dram[b * P:(b + 1) * P, :], XR[b % 2][:, :]).then_inc(s["st_x1"], 16)
            if b + 2 < RT:
                sp.wait_ge(s["st_x1"], 16 * (b + 1))
                sp.wait_ge(s["a_fss"], b + 1)
                sp.wait_ge(s["v_fn"], b + 1)
                sp.dma_start(XR[b % 2][:, :], x_t[:, b + 2, :]).then_inc(load_xr[b % 2], 16)

        def gate_up(slot, f):
            for j, w in enumerate((w_ffn_gate, w_ffn_up)):
                src = w[0].rearrange("(k p) f -> p k f", p=P)[:, :, bass.ds(f * P, P)]
                sp.dma_start(WR[slot][:, j, :, :], src).then_inc(load_wr[slot], 16)

        sp.wait_ge(s["t_ms"], len(ms_use))
        sp.wait_ge(s["v_lm"], STEPS)
        sp.wait_ge(s["t_pv"], STEPS)
        gate_up(0, 0)
        gate_up(1, 1)
        with sp.Fori(1, FT // 2) as i:
            for t in range(2):
                sp.wait_ge(s["v_gl"], i * 2 + (t - 1))
                gate_up(t, i * 2 + t)

        def down(slot, f, dh):
            src = w_ffn_down[0, bass.ds(f * P, P), dh * 512:(dh + 1) * 512]
            sp.dma_start(DR[slot][:, :], src).then_inc(load_dr[slot], 16)

        sp.wait_ge(s["t_gu"], 2 * FT)
        for t in range(2):
            down(t, t, 0)
        with sp.Fori(1, FT // 2) as i:
            for t in range(2):
                sp.wait_ge(s["v_dwl"], i * 2 + (t - 1))
                down(t, i * 2 + t, 0)
        with sp.Fori(0, FT // 2) as i:
            for t in range(2):
                sp.wait_ge(s["v_dwl"], i * 2 + (FT + t - 1))
                down(t, i * 2 + t, 1)
        sp.wait_ge(s["t_dn"], 2 * FT)
        sp.dma_start(PN[:, :, :], p[0, 0].rearrange("(r q) c -> q r c", q=P)).then_inc(s["load_pn"], 16)
        row_gain(GPF2, post_ffn_g, "load_gain2")
        sp.wait_ge(s["st_x1"], 16 * RT)
        for r in range(3):
            sp.dma_start(X2[r][:, :], x1_dram[r * P:(r + 1) * P, :]).then_inc(load_x2[r], 16)
        row_gain(GPL, ple_norm_g, "load_gain2")
        for n in range(2 * (2 + KT)):
            k, dh = divmod(n if n < 4 else n - 4, 2)
            src = w_ple_up[0] if n < 4 else w_ple_gate[0]
            if n >= 3:
                sp.wait_ge(s["v_wgl"], n - 2)
            sp.dma_start(WGR[n % 3][:, :], src[k * P:(k + 1) * P, dh * 512:(dh + 1) * 512])\
              .then_inc(load_wg[n % 3], 16)
        for r in range(RT):
            sp.wait_ge(s["v_out"], r + 1)
            sp.dma_start(out[0, r * P:(r + 1) * P, :], UU[r % 2][:, :]).then_inc(st_out[r % 2], 16)
            if r + 3 < RT:
                sp.dma_start(X2[r % 3][:, :], x1_dram[(r + 3) * P:(r + 4) * P, :]).then_inc(load_x2[r % 3], 16)
        for i in range(2):
            sp.wait_ge(st_out[i], 16 * RT // 2)

    @block.tensor
    def _(pe):
        def mm3(o, ah, al, wh, wl, start, stop):
            pe.matmul(o, ah, wh, start=start, stop=False)
            pe.matmul(o, ah, wl, start=False, stop=False)
            return pe.matmul(o, al, wh, start=False, stop=stop)

        pe.wait_ge(s["load_tab"], 16)
        for r in range(RT):
            pe.wait_ge(s["v_xn"], r + 1)
            if r >= 2:
                pe.wait_ge(s["v_xl"], r - 1)
            for k in range(KT):
                m = pe.transpose(pair(1 + r % 2)[:, k * P:(k + 1) * P], XN[:, r, k * P:(k + 1) * P], ID)
            m.then_inc(s["t_xt"], 1)

        def key_transposes():
            pe.wait_ge(s["v_kn"], 1)
            for r in range(RT):
                m = pe.transpose(pair(1)[:, r * P:(r + 1) * P], KN[:, r, :], ID)
            m.then_inc(s["t_nt"], 1)

        def indexer_scores(n):
            b, h = B0 + n // H, n % H
            if n == 0:
                pe.wait_ge(s["v_kl"], 1)
            if n >= 2:
                pe.wait_ge(s["v_acc"], n - 1)
            keys = (b + 1) * P
            for k0 in range(0, keys, 512):
                k1 = min(k0 + 512, keys)
                for key in (KH, KL):
                    m = pe.matmul(pair(1 + n % 2)[:, k0:k1], QS[:, h, (b - B0) * P:(b - B0 + 1) * P], key[:, k0:k1],
                                  start=(key is KH), stop=(key is KL))
            m.then_inc(s["t_ix"], 1)

        def unit(g):
            c, u = divmod(g, KT)
            if g >= 2:
                pe.wait_ge(s["a_ev"], g - 1)
                pe.wait_ge(s["v_qlo"], min(g - 1, KT))
            if c == 0 and u % 4 == 0:
                pe.wait_ge(s["v_xl"], u + 4)
            if c == 1 and u == 0:
                pe.wait_ge(s["v_xl"], RT)
            o = bank(g % 2, unit_width(g))
            hi, lo = WBH[c % 2], WBL[c % 2]
            todo = list(items(g))
            for k in range(KT):
                if todo and k in (1, 4, 7):
                    indexer_scores(todo.pop(0))
                if u == 0:
                    pe.wait_ge(s["p_wlo"], c * KT + k + 1)
                if c in (0, 6):
                    m, half = u % 4, u // 4
                    cs, rs = slice(m * P, (m + 1) * P), slice(half * 512 + 512 - unit_width(g), (half + 1) * 512)
                    last = mm3(o, hi[:, k, cs], lo[:, k, cs], XTH[:, k, rs], XTL[:, k, rs], k == 0, k == KT - 1)
                else:
                    rs = slice(u * P, (u + 1) * P)
                    last = mm3(o, XTH[:, k, rs], XTL[:, k, rs], hi[:, k, 0:width(c)], lo[:, k, 0:width(c)],
                               k == 0, k == KT - 1)
            last.then_inc(s["t_unit"], 1)

        for g in range(2 * KT):
            unit(g)
        for g in range(2 * KT, LAST):
            unit(g)
            if g == 2 * KT + 1:
                key_transposes()

        def pair_bank(n):
            hp, r = divmod(n, RT)
            if r == 0:
                pe.wait_ge(load_rp[hp % 2], 16 * (hp // 2 + 1))
            if n == 0:
                pe.wait_ge(s["a_ev"], LAST)
            if n >= 2:
                pe.wait_ge(s["a_rb"], n - 1)
            if n >= RAHEAD + 2 * RT and (n - RAHEAD) % RT == 0:
                pe.wait_ge(s["a_yrt"], (n - RAHEAD) // RT - 1)
            rp, o = RP[hp % 2], bank(n % 2)
            pe.transpose(o[:, 0:P], rp[:, r, 0:P], ID)
            m = pe.transpose(o[:, P:2 * P], rp[:, r, P:2 * P], ID)
            if r < RT - 1:
                v01 = rp[:, r, RV:RV + 384].rearrange("p (h c) -> p h c", h=2)[:, :, 0:HD]
                m = pe.matmul(o[:, 2 * P:3 * P], rp[:, r, P:2 * P], v01, start=True, stop=True)
            m.then_inc(s["t_rb"], 1)

        def scores(n):
            hp, r = divmod(n, RT)
            pe.wait_ge(s["a_rb"], n + 1)
            if n >= 2:
                pe.wait_ge(s["a_st"], n - 1)
            for h in range(2):
                j = slice(HD * h, HD * h + HD)
                qk = QKT[hp % 2]
                m = pe.matmul(bank(2 + 2 * (n % 2) + h, P), qk[j, r, P:2 * P], qk[j, r, 0:P],
                              start=True, stop=True)
            m.then_inc(s["t_sc"], 1)

        def ret_out(n):
            hp, r = divmod(n, RT)
            pe.wait_ge(s["p_st"], n + 1)
            if r > 0:
                pe.wait_ge(s["p_rst"], hp * (RT - 1) + r)
            else:
                pe.wait_ge(s["p_zero"], 2)
            if n >= 2:
                pe.wait_ge(s["a_o"], n - 1)
            o = bank(6 + n % 2, P)
            pe.matmul(o, QKT[hp % 2][:, r, 0:P], RST[hp % 2][:, r, :], start=True, stop=False)
            for h in range(2):
                m = pe.matmul(o, ST[n % 2][:, h * P:(h + 1) * P], RP[hp % 2][:, r, RV + h * P:RV + (h + 1) * P],
                              start=False, stop=(h == 1))
            m.then_inc(s["t_ro"], 1)

        def ret_transpose(hp):
            pe.wait_ge(s["v_y"], hp + 1)
            pe.wait_ge(s["a_rb"], min((hp + 2) * RT + RAHEAD, NP * RT))
            for r in range(RT):
                m = pe.transpose(pair(0)[:, r * P:(r + 1) * P], Y[:, r, :], ID)
            m.then_inc(s["t_yr"], 1)

        for n in range(RAHEAD):
            pair_bank(n)
        for n in range(NP * RT + 1):
            if n + RAHEAD < NP * RT:
                pair_bank(n + RAHEAD)
            if n < NP * RT:
                scores(n)
            if n >= 1:
                ret_out(n - 1)
            if n % RT == RT - 1 and n > RT:
                ret_transpose(n // RT - 1)

        def tp_free(use):
            if tp_at[use] >= 1:
                pe.wait_ge(s["a_tp"], tp_at[use])

        def ms_free(use):
            a, v = ms_read(ms_at[use])
            if a:
                pe.wait_ge(s["a_ms"], a)
            if v:
                pe.wait_ge(s["v_ms"], v)

        def latent_queries(b, half):
            ms_free(("ql", b, half))
            for hh in range(4):
                h = 4 * half + hh
                m = pe.matmul(bank(7)[:, hh * P:(hh + 1) * P], WUK[:, h, :], AQ[:, h // 2, b * P:(b + 1) * P],
                              start=True, stop=True)
            m.then_inc(s["t_ms"], 1)

        def logits(t):
            b, h = divmod(t, H)
            if h == 0:
                pe.wait_ge(s["a_ms"], ms_read(ms_at[("ql", b, 1)])[0] + 1)
            if t == 0:
                pe.wait_ge(s["a_nt"], 1)
            if t >= 2:
                pe.wait_ge(s["v_lm"], t - 1)
            keys = (b + 1) * P
            for k0 in range(0, keys, 512):
                k1 = min(k0 + 512, keys)
                m = pe.matmul(pair(t % 2)[:, k0:k1], QL[b % 2][:, h, :], CKVT[:, k0:k1], start=True, stop=True)
            m.then_inc(s["t_lg"], 1)

        def prob_transposes(t):
            b = t // H
            tp_free(("tr", t))
            pe.wait_ge(s["a_ex"], t + 1)
            for j in range(b + 1):
                m = pe.transpose(pair(2)[:, j * P:(j + 1) * P], LM[t % 2][:, j * P:(j + 1) * P], ID)
            m.then_inc(s["t_tp"], 1)

        def prob_values(t):
            b, h = divmod(t, H)
            pe.wait_ge(s["a_tp"], tp_at[("tr", t)] + 1)
            if t % 4 == 0 and t >= 4:
                pe.wait_ge(s["a_ots"], t // 4)
            for j in range(b + 1):
                m = pe.matmul(bank(6)[:, (h % 4) * P:(h % 4 + 1) * P], CKV[:, j, :], PT[t % 2][:, j * P:(j + 1) * P],
                              start=(j == 0), stop=(j == b))
            m.then_inc(s["t_pv"], 1)

        def head_values(g):
            pe.wait_ge(s["a_ots"], g + 1)
            ms_free(("y", g))
            for hh in range(4):
                m = pe.matmul(bank(7)[:, hh // 2 * P:(hh // 2 + 1) * P], OTS[g % 2][:, hh * P:(hh + 1) * P],
                              WUV[:, 4 * (g % 2) + hh, :], start=(hh % 2 == 0), stop=(hh % 2 == 1))
            m.then_inc(s["t_ms"], 1)

        def y_transposes(b):
            ms_free(("yt", b))
            for k in range(NP):
                m = pe.transpose(bank(7)[:, k * P:(k + 1) * P], YD[:, k * P:(k + 1) * P], ID)
            m.then_inc(s["t_ms"], 1)

        def pair_outputs_transposes():
            pe.wait_ge(s["v_y"], NP)
            tp_free(("yr",))
            for r in range(RT):
                m = pe.transpose(pair(2)[:, r * P:(r + 1) * P], Y[:, r, :], ID)
            m.then_inc(s["t_tp"], 1)

        def out_projection(b, part):
            if part == 0:
                tp_free(("mx", b))
            else:
                pe.wait_ge(s["a_ms"], ms_read(ms_at[("yt", b)])[0] + 1)
            for k in range(part * NP, (part + 1) * NP):
                src = YRT[k][:, b * P:(b + 1) * P] if k < NP else YDT[:, k - NP, :]
                for dh in range(2):
                    m = pe.matmul(pair(2)[:, dh * 512:(dh + 1) * 512], src, WO[:, k, dh * 512:(dh + 1) * 512],
                                  start=(k == 0), stop=(k == KT - 1))
            if part == 1:
                m.then_inc(s["t_tp"], 1)

        def ffn_transposes(b):
            pe.wait_ge(s["v_fn"], b + 1)
            tp_free(("ft", b))
            for k in range(KT):
                m = pe.transpose(pair(2)[:, k * P:(k + 1) * P], FN[:, k * P:(k + 1) * P], ID)
            m.then_inc(s["t_tp"], 1)

        pe.wait_ge(s["a_yrt"], NP - 1)
        pe.wait_ge(s["a_rb"], NP * RT)
        for r in range(RT):
            m = pe.transpose(pair(0)[:, r * P:(r + 1) * P], CKV[:, r, :], ID)
        m.then_inc(s["t_nt"], 1)
        pe.wait_ge(s["load_wuk"], 16 * 2 * H)
        pe.wait_ge(s["load_wo"], 16)
        pe.wait_ge(s["a_o"], NP * RT)
        latent_queries(0, 0)
        latent_queries(0, 1)
        for t in range(STEPS + TAIL):
            if t < STEPS:
                logits(t)
            if at_block(t, 5) is not None:
                out_projection(at_block(t, 5), 1)
            if 1 <= t <= STEPS:
                prob_transposes(t - 1)
            if 2 <= t <= STEPS + 1:
                prob_values(t - 2)
            if ql_due(t) is not None:
                latent_queries(*ql_due(t))
            if at_half(t, 3) is not None:
                head_values(at_half(t, 3))
            if t == YR_STEP:
                pair_outputs_transposes()
            if at_block(t, FT_LAG) is not None:
                ffn_transposes(at_block(t, FT_LAG))
            if at_block(t, 4) is not None:
                out_projection(at_block(t, 4), 0)
                y_transposes(at_block(t, 4))

        def gate_up(slot, f, first):
            pe.wait_ge(s["v_gl"], f + 1)
            for half in range(2):
                if not first:
                    pe.wait_ge(s["v_ht"], f * 2 + (half - 3))
                rs = slice(half * 512, (half + 1) * 512)
                for j in range(2):
                    o = bank(4 * slot + 2 * half + j)
                    for k in range(KT):
                        if first and slot == 0 and half == 0 and j == 0:
                            pe.wait_ge(s["v_ftl"], k + 1)
                        m = mm3(o, WH[slot][:, j, k, :], WL[slot][:, j, k, :], FTH[:, k, rs], FTL[:, k, rs],
                                k == 0, k == KT - 1)
                m.then_inc(s["t_gu"], 1)

        pe.wait_ge(s["a_tp"], len(tp_use))
        for t in range(2):
            gate_up(t, t, True)
        with pe.Fori(1, FT // 2) as i:
            for t in range(2):
                gate_up(t, i * 2 + t, False)

        def down(slot, n, start, stop, fresh=None):
            pe.wait_ge(s["v_dwl"], n + 1)
            pe.wait_ge(s["v_dhl"], n + 1)
            for r in range(RT):
                rs = slice(r * P, (r + 1) * P)
                if fresh is not None:
                    fresh(r)
                m = mm3(bank(r), HTH[slot][:, rs], HTL[slot][:, rs], DH[slot][:, :], DL[slot][:, :], start, stop)
                if stop:
                    m.then_inc(s["t_acc"], 1)
            if stop:
                pe.wait_ge(s["t_acc"], (n + 1) // FT * RT)
                pe.sem_inc(s["t_dn"], 1)
            else:
                m.then_inc(s["t_dn"], 1)

        def after_gate_up(r):
            if r == 0:
                pe.wait_ge(s["v_ht"], 2 * FT)

        def after_first_half(r):
            pe.wait_ge(s["a_fo" if r % 2 == 0 else "v_fo"], r // 2 + 1)

        for dh, fresh in enumerate((after_gate_up, after_first_half)):
            n0 = dh * FT
            down(0, n0, True, False, fresh)
            down(1, n0 + 1, False, False)
            with pe.Fori(1, FT // 2 - 1) as i:
                for t in range(2):
                    down(t, i * 2 + (n0 + t), False, False)
            down(0, n0 + FT - 2, False, False)
            down(1, n0 + FT - 1, False, True)

        pe.wait_ge(s["load_pn"], 16)
        for k in range(2):
            pe.wait_ge(s["a_fo"], 2 * RT // 2)
            pe.wait_ge(s["v_fo"], 2 * RT // 2)
            for r in range(RT):
                m = pe.transpose(pair(k)[:, r * P:(r + 1) * P], PN[:, r, k * P:(k + 1) * P], ID)
            m.then_inc(s["t_pt"], 1)

        def x2_transposes(r):
            pe.wait_ge(s["v_x2"], r + 1)
            if r < 2:
                pe.wait_ge(s["v_ptl"], r + 1)
            else:
                pe.wait_ge(s["v_x2l"], r - 1)
            for k in range(KT):
                m = pe.transpose(pair(r % 2)[:, k * P:(k + 1) * P], X2[r % 3][:, k * P:(k + 1) * P], ID)
            m.then_inc(s["t_x2"], 1)

        def gate(r):
            pe.wait_ge(s["v_x2l"], r + 1)
            if r >= 1:
                pe.wait_ge(s["a_sig"], r)
            for dh in range(2):
                ds = slice(dh * 512, (dh + 1) * 512)
                for k in range(KT):
                    if r == 0 and dh == 0:
                        pe.wait_ge(s["v_wgl"], 4 + 2 * (k + 1))
                    m = mm3(pair(2)[:, ds], X2H[r % 2][:, k, :], X2L[r % 2][:, k, :], WGH[:, k, ds], WGL[:, k, ds],
                            k == 0, k == KT - 1)
            m.then_inc(s["t_gt"], 1)

        def embed(r):
            if r == 0:
                pe.wait_ge(s["v_ptl"], 2)
                pe.wait_ge(s["v_wgl"], 4)
            if r >= 1:
                pe.wait_ge(s["v_u"], r)
            rs = slice(r * P, (r + 1) * P)
            for dh in range(2):
                ds = slice(dh * 512, (dh + 1) * 512)
                for k in range(2):
                    m = mm3(pair(3)[:, ds], PTH[:, k, rs], PTL[:, k, rs], WUH[:, k, ds], WUL[:, k, ds], k == 0, k == 1)
            m.then_inc(s["t_em"], 1)

        x2_transposes(0)
        for r in range(RT):
            embed(r)
            gate(r)
            if r + 1 < RT:
                x2_transposes(r + 1)

    @block.scalar
    def _(act):
        sc = nc.scalar

        def square(r):
            act.wait_ge(load_x[r], 16)
            if r:
                act.wait_ge(s["a_sq"], r)
            sc.activation(pair(3), XN[:, r, :], ACT.Square, accum_out=cols["ss0"][:, r:r + 1]).then_inc(s["a_sq"], 1)

        def x_hi(r):
            act.wait_ge(s["t_xt"], r + 1)
            sc.copy(XTH[:, :, r * P:(r + 1) * P], pair(1 + r % 2).rearrange("p (k c) -> p k c", k=KT))\
              .then_inc(s["a_xh"], 1)

        def w_hi(n):
            c, k = divmod(n, KT)
            act.wait_ge(load_raw[n % 4], raw_count(n))
            if k == 0 and c == 1:
                act.wait_ge(s["t_xt"], RT)
            if k == 0 and c >= 2:
                act.wait_ge(s["t_unit"], KT * (c - 1))
            w = width(c)
            sc.copy(WBH[c % 2][:, k, 0:w], RAW[n % 4][:, 0:w]).then_inc(s["a_whi"], 1)

        def evacuate(g):
            c, u = divmod(g, KT)
            act.wait_ge(s["t_unit"], g + 1)
            o = bank(g % 2)
            m, half = u % 4, u // 4
            if c == 0:
                for h, j in enumerate(HALF):
                    ins = sc.copy(QS[j, 2 * m + h, query_cols(g)], bank(g % 2, unit_width(g))[j, :])
            elif c == 6:
                ins = sc.copy(AQ[:, m, half * 512:(half + 1) * 512], o)
            elif c == 1:
                ins = sc.copy(AC[:, u, :], o[:, 0:SMALL])
            else:
                n, hp = g - 2 * KT, c - 2
                if n == 0:
                    act.wait_ge(s["p_pad"], 2)
                if n >= 2:
                    act.wait_ge(st_ret[n % 2], 16 * (n // 2))
                for j in range(4):
                    col = (QSC if j < 2 else KSC)[:, 2 * hp + j % 2:2 * hp + j % 2 + 1]
                    sc.activation(STG[n % 2][:, j * HD:(j + 1) * HD], o[:, j * HD:(j + 1) * HD], ACT.Copy, scale=col)
                v01 = STG[n % 2][:, RV:RV + 384].rearrange("p (h c) -> p h c", h=2)[:, :, 0:HD]
                sc.copy(v01, o[:, 2 * P:3 * P].rearrange("p (h c) -> p h c", h=2))
                ins = sc.copy(STG[n % 2][:, RG_:RG_ + P], o[:, 3 * P:4 * P])
            ins.then_inc(s["a_ev"], 1)

        for r in range(RT + 2):
            if r < RT:
                square(r)
            if r >= 2:
                x_hi(r - 2)
                w_hi(r - 2)
        act.wait_ge(s["v_ang"], 1)
        sc.activation(SIN[:, :, :], ANR[:, :, :], ACT.Sin).then_inc(s["a_trig"], 1)
        sc.activation(COS[:, :, :], ANK[:, :, :], ACT.Sin).then_inc(s["a_trig"], 1)
        for g in range(2 * KT):
            w_hi(g + KT)
            evacuate(g)

        def relu_scores(n):
            o = pair(1 + n % 2, (B0 + n // H + 1) * P)
            act.wait_ge(s["t_ix"], n + 1)
            sc.activation(o, o, ACT.Relu).then_inc(s["a_rl"], 1)

        for g in range(2 * KT, LAST):
            for n in items(g):
                relu_scores(n)
            if g + KT < LAST:
                w_hi(g + KT)
            evacuate(g)
            if g == 2 * KT + 1:
                act.wait_ge(s["t_nt"], 1)
                sc.copy(KH[:, :], pair(1)).then_inc(s["a_kh"], 1)

        def read_pair_bank(n):
            hp, r = divmod(n, RT)
            act.wait_ge(s["t_rb"], n + 1)
            w = 3 * P if r < RT - 1 else 2 * P
            sc.copy(QKT[hp % 2][:, r, 0:w], bank(n % 2, w)).then_inc(s["a_rb"], 1)

        def read_scores(n):
            act.wait_ge(s["t_sc"], n + 1)
            if n >= 2:
                act.wait_ge(s["t_ro"], n - 1)
            b0 = 1024 * (1 + n % 2)
            src = PS[:, b0:b0 + 1024].rearrange("p (h i) -> p h i", h=2)[:, :, 0:P]
            sc.copy(ST[n % 2][:, :].rearrange("p (h i) -> p h i", h=2), src).then_inc(s["a_st"], 1)

        def read_out(n):
            hp, r = divmod(n, RT)
            if r == 0 and hp >= 2:
                act.wait_ge(s["v_y"], hp - 1)
            act.wait_ge(s["t_ro"], n + 1)
            sc.copy(O[hp % 2][:, r, :], bank(6 + n % 2, P)).then_inc(s["a_o"], 1)

        def ret_gate(hp):
            act.wait_ge(load_rp[hp % 2], 16 * (hp // 2 + 1))
            if hp >= 1:
                act.wait_ge(s["v_y"], hp)
            sc.activation(SGR[:, :, :], RP[hp % 2][:, :, RG_:RG_ + P], ACT.Silu).then_inc(s["a_silu"], 1)

        def read_ret(hp):
            if hp == 0:
                for i in range(2):
                    act.wait_ge(st_ret[i], 16 * 4 * NP)
            act.wait_ge(s["t_yr"], hp + 1)
            sc.copy(YRT[hp][:, :], pair(0)).then_inc(s["a_yrt"], 1)

        for n in range(RAHEAD):
            read_pair_bank(n)
        for n in range(NP * RT + 1):
            if n + RAHEAD < NP * RT:
                read_pair_bank(n + RAHEAD)
            if n < NP * RT:
                read_scores(n)
            if n >= 1:
                read_out(n - 1)
            if n % RT == RT - 1:
                ret_gate(n // RT)
                if n > RT:
                    read_ret(n // RT - 1)

        def read_queries(b, half):
            n = ms_at[("ql", b, half)]
            act.wait_ge(s["t_ms"], n + 1)
            if b >= 2:
                act.wait_ge(s["t_lg"], H * (b - 1))
            sc.mul(QL[b % 2][:, 4 * half:4 * half + 4, :], bank(7).rearrange("p (h c) -> p h c", h=4), HD ** -0.5)\
              .then_inc(s["a_ms"], 1)

        def exponent(t):
            b, h = divmod(t, H)
            keys = (b + 1) * P
            act.wait_ge(s["v_lm"], t + 1)
            if h == 0 and b >= 2:
                act.wait_ge(s["v_ms"], 2 * (b - 1))
            c = (b % 2) * H + h
            sc.activation(LM[t % 2][:, 0:keys], LM[t % 2][:, 0:keys], ACT.Exp, scale=-1.0,
                          bias=cols["nmax"][:, t % 4:t % 4 + 1], accum_out=cols["sum"][:, c:c + 1])\
              .then_inc(s["a_ex"], 1)

        def read_probs(t):
            keys = (t // H + 1) * P
            act.wait_ge(s["t_tp"], tp_at[("tr", t)] + 1)
            if t >= 2:
                act.wait_ge(s["t_pv"], t - 1)
            sc.copy(PT[t % 2][:, 0:keys], pair(2, keys)).then_inc(s["a_tp"], 1)

        def read_latent(g):
            act.wait_ge(s["t_pv"], 4 * (g + 1))
            if g >= 2:
                act.wait_ge(s["t_ms"], ms_at[("y", g - 2)] + 1)
            sc.copy(OTS[g % 2][:, :], bank(6)).then_inc(s["a_ots"], 1)

        def read_y(b):
            act.wait_ge(s["t_ms"], ms_at[("yt", b)] + 1)
            if b >= 1:
                act.wait_ge(s["t_tp"], tp_at[("mx", b - 1)] + 1)
            sc.copy(YDT[:, :, :], bank(7).rearrange("p (k c) -> p k c", k=NP)).then_inc(s["a_ms"], 1)

        def read_mix(b):
            act.wait_ge(s["t_tp"], tp_at[("mx", b)] + 1)
            if b >= 1:
                act.wait_ge(s["v_x1"], b)
            sc.copy(MXS[:, :], pair(2)).then_inc(s["a_tp"], 1)

        def mix_square(b):
            act.wait_ge(s["a_tp"], tp_at[("mx", b)] + 1)
            if b >= 1:
                act.wait_ge(s["a_fss"], b)
            sc.activation(JK[:, :], MXS[:, :], ACT.Square, accum_out=cols["ssm"][:, b:b + 1]).then_inc(s["a_mss"], 1)

        def ffn_square(b):
            act.wait_ge(s["v_x1"], b + 1)
            act.wait_ge(s["a_mss"], b + 1)
            sc.activation(JK[:, :], XR[b % 2][:, :], ACT.Square, accum_out=cols["ssf"][:, b:b + 1])\
              .then_inc(s["a_fss"], 1)

        def read_ffn_rows(b):
            act.wait_ge(s["t_tp"], tp_at[("ft", b)] + 1)
            sc.copy(FTR[:, :, b * P:(b + 1) * P], pair(2).rearrange("p (k c) -> p k c", k=KT)).then_inc(s["a_tp"], 1)

        act.wait_ge(s["t_nt"], 2)
        sc.copy(CKVT[:, :], pair(0)).then_inc(s["a_nt"], 1)
        read_queries(0, 0)
        read_queries(0, 1)
        for t in range(STEPS + TAIL):
            if t < STEPS:
                exponent(t)
            if at_block(t, 5) is not None:
                read_mix(at_block(t, 5))
            if 1 <= t <= STEPS:
                read_probs(t - 1)
            if at_block(t, 5) is not None:
                mix_square(at_block(t, 5))
            if at_half(t, 2) is not None:
                read_latent(at_half(t, 2))
            if ql_due(t) is not None:
                read_queries(*ql_due(t))
            if t == YR_STEP:
                act.wait_ge(s["t_tp"], tp_at[("yr",)] + 1)
                sc.copy(YRT[NP - 1][:, :], pair(2)).then_inc(s["a_tp"], 1)
            if at_block(t, FT_LAG) is not None:
                read_ffn_rows(at_block(t, FT_LAG))
            if at_block(t, 4) is not None:
                read_y(at_block(t, 4))
            if at_block(t, SQ_LAG) is not None:
                ffn_square(at_block(t, SQ_LAG))

        for k in range(KT):
            if k == 0:
                act.wait_ge(s["a_tp"], len(tp_use))
                act.wait_ge(s["st_x1"], 16 * RT)
            sc.copy(FTH[:, k, :], FTR[:, k, :]).then_inc(s["a_fth"], 1)
            if k == 0:
                act.wait_ge(load_wr[0], 32)
                sc.copy(WH[0][:, :, :, :], WR[0][:, :, :, :]).then_inc(s["a_gh"], 1)

        def gate_hi(slot, f, first=False):
            act.wait_ge(load_wr[slot], (f - slot) * 16 + 32)
            if not first:
                act.wait_ge(s["t_gu"], f * 2 - 2)
            sc.copy(WH[slot][:, :, :, :], WR[slot][:, :, :, :]).then_inc(s["a_gh"], 1)

        def silu_gate(slot, f, half, first=False):
            act.wait_ge(s["t_gu"], f * 2 + (half + 1))
            if not first:
                act.wait_ge(s["v_ht"], f * 2 + (half - 1))
            sc.activation(SG[half][:, :], bank(4 * slot + 2 * half), ACT.Silu).then_inc(s["a_sg"], 1)

        gate_hi(1, 1, True)
        silu_gate(0, 0, 0, True)
        silu_gate(0, 0, 1, True)
        with act.Fori(1, FT // 2) as i:
            gate_hi(0, i * 2)
            for half in range(2):
                silu_gate(1, i * 2 - 1, half)
            gate_hi(1, i * 2 + 1)
            for half in range(2):
                silu_gate(0, i * 2, half)
        for half in range(2):
            silu_gate(1, FT - 1, half)

        def down_hi(slot, n, f, first=False):
            act.wait_ge(load_dr[slot], (n - slot) * 8 + 16)
            if not first:
                act.wait_ge(s["t_dn"], n - 1)
            sc.copy(DH[slot][:, :], DR[slot][:, :]).then_inc(s["a_dwh"], 1)
            sc.copy(HTH[slot][:, :], HT[:, bass.ds(f, 1), :]).then_inc(s["a_dhh"], 1)

        act.wait_ge(s["t_gu"], 2 * FT)
        act.wait_ge(s["v_ht"], 2 * FT)
        for t in range(2):
            down_hi(t, t, t, True)
        with act.Fori(1, FT // 2) as i:
            for t in range(2):
                down_hi(t, i * 2 + t, i * 2 + t)
        for t in range(2):
            down_hi(t, FT + t, t)
        for r in range(0, RT, 2):
            act.wait_ge(s["t_acc"], r + 1)
            sc.copy(FO0[:, r, :], bank(r)).then_inc(s["a_fo"], 1)
        with act.Fori(1, FT // 2) as i:
            for t in range(2):
                down_hi(t, i * 2 + (FT + t), i * 2 + t)
        for r in range(0, RT, 2):
            act.wait_ge(s["t_acc"], RT + r + 1)
            sc.copy(FO1[:, r, :], bank(r)).then_inc(s["a_fo"], 1)

        def ffn_out_square(r):
            if r == 0:
                act.wait_ge(s["a_fo"], RT)
                act.wait_ge(s["v_fo"], RT)
            else:
                act.wait_ge(s["a_css"], 2 * r)
            if r >= 4:
                act.wait_ge(s["a_uss"], r - 3)
            for dh, fo in enumerate((FO0, FO1)):
                sc.activation(JF[:, 512 * dh:512 * (dh + 1)], fo[:, r, :], ACT.Square,
                              accum_out=SMF[:, 2 * r + dh:2 * r + dh + 1]).then_inc(s["a_css"], 1)

        def ple_hi(n):
            act.wait_ge(load_wg[n % 3], 16 * (n // 3 + 1))
            k, dh = divmod(n if n < 4 else n - 4, 2)
            dst = WUH if n < 4 else WGH
            sc.copy(dst[:, k, dh * 512:(dh + 1) * 512], WGR[n % 3][:, :]).then_inc(s["a_wgh"], 1)

        def x2_hi(r):
            act.wait_ge(s["t_x2"], r + 1)
            if r >= 2:
                act.wait_ge(s["t_gt"], r - 1)
            sc.copy(X2H[r % 2][:, :, :], pair(r % 2).rearrange("p (k c) -> p k c", k=KT)).then_inc(s["a_x2h"], 1)

        ffn_out_square(0)
        for n in range(4):
            ple_hi(n)
        for k in range(2):
            act.wait_ge(s["t_pt"], k + 1)
            sc.copy(PTH[:, k, :], pair(k)).then_inc(s["a_pth"], 1)
        for n in range(4, 20):
            ple_hi(n)
            if n == 8:
                x2_hi(0)
            if n in (5, 11, 17):
                ffn_out_square((n + 1) // 6)
        for r in range(RT):
            if r + 1 < RT:
                x2_hi(r + 1)
            act.wait_ge(s["t_gt"], r + 1)
            if r >= 1:
                act.wait_ge(s["v_u"], r)
            sc.activation(SGG[:, :], pair(2), ACT.Sigmoid).then_inc(s["a_sig"], 1)
            act.wait_ge(s["v_u"], r + 1)
            act.wait_ge(s["a_css"], 2 * min(r + 4, RT))
            if r:
                act.wait_ge(s["a_uss"], r)
            sc.activation(JF[:, :], UU[r % 2][:, :], ACT.Square, accum_out=SMF[:, 32 + r:33 + r])\
              .then_inc(s["a_uss"], 1)
            if r + 4 < RT:
                ffn_out_square(r + 4)

    @block.vector
    def _(dve):
        v = nc.vector
        made = [0]

        def link(ins):
            made[0] += 1
            ins.then_inc(s["v_link"], 1)
            dve.wait_ge(s["v_link"], made[0])

        def norm_x(r):
            if r == 0:
                dve.wait_ge(s["load_gin"], 16)
            dve.wait_ge(s["p_rs"], r + 1)
            v.scalar_tensor_tensor(XN[:, r, :], XN[:, r, :], cols["rs0"][:, r:r + 1], GIN[:, :], ALU.mult, ALU.mult)\
             .then_inc(s["v_xn"], 1)

        def x_lo(r):
            dve.wait_ge(s["a_xh"], r + 1)
            rs = slice(r * P, (r + 1) * P)
            v.tensor_tensor(XTL[:, :, rs], pair(1 + r % 2).rearrange("p (k c) -> p k c", k=KT),
                            XTH[:, :, rs].bitcast(F32), ALU.subtract).then_inc(s["v_xl"], 1)

        def query_lo(g):
            dve.wait_ge(s["a_ev"], g + 1)
            for h, (j, i) in enumerate(zip(HALF, HALF[::-1])):
                q = QS[:, 2 * (g % 4) + h, query_cols(g)]
                ins = v.tensor_tensor(q[i, :], bank(g % 2, unit_width(g))[j, :], q[j, :].bitcast(F32), ALU.subtract)
            ins.then_inc(s["v_qlo"], 1)

        def rotation_angles():
            c1, c2, c3 = cody_waite()
            dve.wait_ge(s["load_pos"], 32)
            link(v.tensor_copy(cols["pos"], POSI[:, :]))
            inv_b = INV[:, :].unsqueeze(1).to_broadcast([P, RT, 32])
            link(v.tensor_tensor(ANG[:, :, :], cols["pos"].unsqueeze(2).to_broadcast([P, RT, 32]), inv_b, ALU.mult))
            link(v.tensor_scalar(ANK[:, :, :], ANG[:, :, :], 1.0 / TWO_PI, MAGIC, ALU.mult, ALU.add))
            link(v.tensor_scalar(ANK[:, :, :], ANK[:, :, :], MAGIC, None, ALU.subtract))
            flat = [a[:, :, :].rearrange("p r c -> p (r c)") for a in (ANG, ANK, ANR)]
            link(v.scalar_tensor_tensor(flat[2], flat[1], -c1, flat[0], ALU.mult, ALU.add))
            link(v.scalar_tensor_tensor(flat[2], flat[1], -c2, flat[2], ALU.mult, ALU.add))
            link(v.scalar_tensor_tensor(flat[2], flat[1], -c3, flat[2], ALU.mult, ALU.add))
            link(v.tensor_scalar(flat[0], flat[2], np.pi / 2, None, ALU.add))
            link(v.tensor_scalar(flat[1], flat[0], np.pi, TWO_PI, ALU.is_gt, ALU.mult))
            link(v.tensor_tensor(flat[1], flat[0], flat[1], ALU.subtract))
            link(v.tensor_scalar(flat[1], flat[1], PI_CAP, -PI_CAP, ALU.min, ALU.max))
            v.tensor_scalar(flat[2], flat[2], PI_CAP, -PI_CAP, ALU.min, ALU.max).then_inc(s["v_ang"], 1)

        for r in range(RT + 2):
            if r < RT:
                dve.wait_ge(s["a_sq"], r + 1)
                v.tensor_scalar(cols["v0"][:, r:r + 1], cols["ss0"][:, r:r + 1], 1.0 / D, EPS, ALU.mult, ALU.add)\
                 .then_inc(s["v_var"], 1)
            if 1 <= r <= RT:
                norm_x(r - 1)
            if r >= 2:
                x_lo(r - 2)
            if r == 5:
                rotation_angles()
        for g in range(KT):
            query_lo(g)

        def over(col, n):
            return col.unsqueeze(2).to_broadcast([P, RT, n])

        def rows(g, n):
            return g[:, :].unsqueeze(1).to_broadcast([P, RT, n])

        dve.wait_ge(s["a_ev"], 2 * KT)
        dve.wait_ge(s["a_trig"], 2)
        dve.wait_ge(s["load_const"], 48)
        ac, ak = AC[:, :, 0:P], AC[:, :, P:P + HD]
        link(v.tensor_tensor(NTMP[:, :, :], ac, ac, ALU.mult))
        link(v.tensor_reduce(cols["ssn"][:, 0:8], NTMP[:, :, :], AX.X, ALU.add))
        link(v.tensor_reduce(cols["mu"], ak, AX.X, ALU.add))
        link(v.tensor_scalar(cols["mu"], cols["mu"], 1.0 / HD, None, ALU.mult))
        link(v.tensor_tensor(NXM[:, :, :], ak, over(cols["mu"], HD), ALU.subtract))
        link(v.tensor_tensor(NTMP[:, :, 0:HD], NXM[:, :, :], NXM[:, :, :], ALU.mult))
        link(v.tensor_reduce(cols["ssn"][:, 8:16], NTMP[:, :, 0:HD], AX.X, ALU.add))
        v.tensor_scalar(cols["vn"][:, 0:8], cols["ssn"][:, 0:8], 1.0 / P, EPS, ALU.mult, ALU.add)
        v.tensor_scalar(cols["vn"][:, 8:16], cols["ssn"][:, 8:16], 1.0 / HD, EPS, ALU.mult, ALU.add)\
         .then_inc(s["v_nrm"], 1)
        dve.wait_ge(s["p_nrs"], 1)
        link(v.tensor_tensor(NXM[:, :, :], NXM[:, :, :], over(cols["rsn"][:, 8:16], HD), ALU.mult))
        link(v.tensor_tensor(NXM[:, :, :], NXM[:, :, :], rows(IKG, HD), ALU.mult))
        v.tensor_tensor(KN[:, :, 0:HD], NXM[:, :, :], rows(IKB, HD), ALU.add)
        v.tensor_tensor(KN[:, :, HD:P], NXM[:, :, :], rows(IKB, HD), ALU.add).then_inc(s["v_kn"], 1)
        link(v.tensor_tensor(CKV[:, :, :], ac, over(cols["rsn"][:, 0:8], P), ALU.mult))
        v.tensor_tensor(CKV[:, :, :], CKV[:, :, :], rows(KVG, P), ALU.mult).then_inc(s["v_ckv"], 1)
        v.tensor_scalar(WI[:, :, :], AC[:, :, P + HD:SMALL], H ** -0.5 * HD ** -0.5, None, ALU.mult)\
         .then_inc(s["v_ac"], 1)
        dve.wait_ge(s["v_ac"], 1)
        dve.wait_ge(s["a_kh"], 1)
        v.tensor_tensor(KL[:, :], pair(1), KH[:, :].bitcast(F32), ALU.subtract).then_inc(s["v_kl"], 1)

        def add_head(n):
            b, h = B0 + n // H, n % H
            o, sc_b = pair(1 + n % 2, (b + 1) * P), SC[b - B0][:, :]
            dve.wait_ge(s["a_rl"], n + 1)
            if h:
                dve.wait_ge(s["v_acc"], n)
                ins = v.scalar_tensor_tensor(sc_b, o, WI[:, b, h:h + 1], sc_b, ALU.mult, ALU.add)
            else:
                ins = v.tensor_scalar(sc_b, o, WI[:, b, h:h + 1], None, ALU.mult)
            ins.then_inc(s["v_acc"], 1)

        def pick_round(b, first=False):
            sc_b = SC[b - B0][:, :]
            if first:
                dve.wait_ge(s["p_caus"], b - B0 + 1)
            v.max(M8[:, :], sc_b)
            dve.drain()
            v.match_replace(sc_b, M8[:, :], sc_b, PICKED)
            dve.drain()

        def picked_mask(b):
            sc_b = SC[b - B0][:, :]
            v.tensor_scalar(sc_b, sc_b, (NONCAUSAL + PICKED) / 2, MASKED, ALU.is_gt, ALU.mult).then_inc(s["v_mask"], 1)

        def pick_rounds(b, rounds):
            assert rounds % UNROLL == 0
            with dve.Fori(0, rounds // UNROLL):
                for _ in range(UNROLL):
                    pick_round(b)

        done = 0
        for g in range(IX0, IX0 + ITEMS // PER):
            for j, n in enumerate(items(g)):
                add_head(n)
                if g > IX0 + (H - 1) // PER and done < ROUNDS + UNROLL:
                    for _ in range((1, 1, 2)[j]):
                        pick_round(B0 + done // ROUNDS, done % ROUNDS == 0)
                        done += 1
                        if done % ROUNDS == 0:
                            picked_mask(B0 + done // ROUNDS - 1)
        b = B0 + done // ROUNDS
        pick_rounds(b, ROUNDS - done % ROUNDS)
        picked_mask(b)
        dve.wait_ge(s["p_caus"], b + 1 - B0 + 1)
        pick_rounds(b + 1, ROUNDS)
        picked_mask(b + 1)

        def ret_norm(hp, part=None):
            o = O[hp % 2][:, :, :]
            o16 = o.rearrange("p r (h e) -> p (r h) e", h=2)
            t16 = PT1[:, :, :].rearrange("p r (h e) -> p (r h) e", h=2)
            y16 = Y[:, :, :].rearrange("p r (h e) -> p (r h) e", h=2)

            def per_head(c):
                return cols[c].unsqueeze(2).to_broadcast([P, 2 * RT, HD])

            def gains(g):
                return g[:, hp * P:(hp + 1) * P].unsqueeze(1).to_broadcast([P, RT, P])

            if part != 1:
                center(hp, o16, y16, t16, per_head)
            if part == 0:
                return
            dve.wait_ge(s["p_lnr"], hp + 1)
            link(v.tensor_tensor(y16, y16, per_head("rsn"), ALU.mult))
            link(v.tensor_tensor(Y[:, :, :], Y[:, :, :], gains(RG), ALU.mult))
            link(v.tensor_tensor(Y[:, :, :], Y[:, :, :], gains(RB), ALU.add))
            dve.wait_ge(s["a_silu"], hp + 1)
            v.tensor_tensor(Y[:, :, :], Y[:, :, :], SGR[:, :, :], ALU.mult).then_inc(s["v_y"], 1)

        def center(hp, o16, y16, t16, per_head):
            if hp == 0:
                dve.wait_ge(s["load_retg"], 32)
            dve.wait_ge(s["a_o"], RT * (hp + 1))
            link(v.tensor_reduce(cols["ssn"], o16, AX.X, ALU.add))
            link(v.tensor_scalar(cols["ssn"], cols["ssn"], 1.0 / HD, None, ALU.mult))
            if hp >= 1:
                dve.wait_ge(s["t_yr"], hp)
            link(v.tensor_tensor(y16, o16, per_head("ssn"), ALU.subtract))
            link(v.tensor_tensor(t16, y16, y16, ALU.mult))
            link(v.tensor_reduce(cols["ssn"], t16, AX.X, ALU.add))
            v.tensor_scalar(cols["vn"], cols["ssn"], 1.0 / HD, EPS, ALU.mult, ALU.add).then_inc(s["v_lnv"], 1)

        dve.wait_ge(s["p_caus"], RT - 3 - B0 + 1)
        pick_rounds(RT - 3, EARLY)
        for hp in range(NP - 1):
            ret_norm(hp)
        ret_norm(NP - 1, 0)

        def mask_logits(t):
            b, h = divmod(t, H)
            keys = (b + 1) * P
            if h == 0:
                if b == 0:
                    dve.wait_ge(s["p_tri"], 1)
                elif b >= B0:
                    dve.wait_ge(s["v_mask"], b - B0 + 1)
            mask = SC[b - B0][:, :] if b >= B0 else TRI[:, 2 * P - keys:2 * P]
            dve.wait_ge(s["t_lg"], t + 1)
            if t >= 2:
                dve.wait_ge(s["t_tp"], tp_at[("tr", t - 2)] + 1)
            v.tensor_tensor_reduce(LM[t % 2][:, 0:keys], pair(t % 2, keys), mask, -1.0, 3.0e38, ALU.add, ALU.min,
                                   cols["nmax"][:, t % 4:t % 4 + 1]).then_inc(s["v_lm"], 1)

        def read_head_values(g):
            b, half = divmod(g, 2)
            c = (b % 2) * H + 4 * half
            dve.wait_ge(s["a_ex"], 4 * (g + 1))
            link(v.reciprocal(cols["rsum"][:, c:c + 4], cols["sum"][:, c:c + 4]))
            dve.wait_ge(s["t_ms"], ms_at[("y", g)] + 1)
            if half == 0 and b >= 1:
                dve.wait_ge(s["t_ms"], ms_at[("yt", b - 1)] + 1)
            v.tensor_tensor(YD[:, half * 256:(half + 1) * 256].rearrange("p (h e) -> p h e", h=4),
                            bank(7, 256).rearrange("p (h e) -> p h e", h=4),
                            cols["rsum"][:, c:c + 4].unsqueeze(2).to_broadcast([P, 4, HD]), ALU.mult)\
             .then_inc(s["v_ms"], 1)

        def variance(dst, src, b, n, after, sig):
            dve.wait_ge(s[after], b + 1)
            v.tensor_scalar(cols[dst][:, b:b + 1], cols[src][:, b:b + 1], 1.0 / n, EPS, ALU.mult, ALU.add)\
             .then_inc(s[sig], 1)

        def add_mix(b):
            if b == 0:
                dve.wait_ge(s["load_gain"], 32)
            dve.wait_ge(s["p_mr"], b + 1)
            link(v.scalar_tensor_tensor(MXS[:, :], MXS[:, :], cols["rsm"][:, b:b + 1], GPO[:, :], ALU.mult, ALU.mult))
            dve.wait_ge(load_xr[b % 2], 16 * (b // 2 + 1))
            v.tensor_tensor(XR[b % 2][:, :], XR[b % 2][:, :], MXS[:, :], ALU.add).then_inc(s["v_x1"], 1)

        def ffn_norm(b):
            dve.wait_ge(s["p_fr"], b + 1)
            if b >= 1:
                dve.wait_ge(s["t_tp"], tp_at[("ft", b - 1)] + 1)
            v.scalar_tensor_tensor(FN[:, :], XR[b % 2][:, :], cols["rsf"][:, b:b + 1], GPF[:, :], ALU.mult, ALU.mult)\
             .then_inc(s["v_fn"], 1)

        for t in range(STEPS + TAIL):
            if t < STEPS:
                mask_logits(t)
            if t == 3:
                ret_norm(NP - 1, 1)
            if at_half(t, 3) is not None:
                read_head_values(at_half(t, 3))
            if at_block(t, 6) is not None:
                variance("vm", "ssm", at_block(t, 6), D, "a_mss", "v_mv")
            if at_block(t, ADD_LAG) is not None:
                add_mix(at_block(t, ADD_LAG))
            if at_block(t, FV_LAG) is not None:
                variance("vf", "ssf", at_block(t, FV_LAG), D, "a_fss", "v_fv")
            if at_block(t, FN_LAG) is not None:
                ffn_norm(at_block(t, FN_LAG))
            for _ in range(rounds_beside(t)):
                bb, n = beside.pop(0)
                pick_round(bb, n == 0)
                if n == ROUNDS - 1:
                    picked_mask(bb)
        assert not beside

        for k in range(KT):
            dve.wait_ge(s["a_fth"], k + 1)
            v.tensor_tensor(FTL[:, k, :], FTR[:, k, :], FTH[:, k, :].bitcast(F32), ALU.subtract)\
             .then_inc(s["v_ftl"], 1)
            if k == 0:
                dve.wait_ge(s["a_gh"], 1)
                v.tensor_tensor(WL[0][:, :, :, :], WR[0][:, :, :, :], WH[0][:, :, :, :].bitcast(F32), ALU.subtract)\
                 .then_inc(s["v_gl"], 1)

        def gate_lo(slot, f):
            dve.wait_ge(s["a_gh"], f + 1)
            v.tensor_tensor(WL[slot][:, :, :, :], WR[slot][:, :, :, :], WH[slot][:, :, :, :].bitcast(F32),
                            ALU.subtract).then_inc(s["v_gl"], 1)

        def hidden(slot, f, half):
            dve.wait_ge(s["a_sg"], f * 2 + (half + 1))
            v.tensor_tensor(HT[:, bass.ds(f, 1), half * 512:(half + 1) * 512], SG[half][:, :].unsqueeze(1),
                            bank(4 * slot + 2 * half + 1).unsqueeze(1), ALU.mult).then_inc(s["v_ht"], 1)

        gate_lo(1, 1)
        for half in range(2):
            hidden(0, 0, half)
        with dve.Fori(1, FT // 2) as i:
            gate_lo(0, i * 2)
            for half in range(2):
                hidden(1, i * 2 - 1, half)
            gate_lo(1, i * 2 + 1)
            for half in range(2):
                hidden(0, i * 2, half)
        for half in range(2):
            hidden(1, FT - 1, half)

        def down_lo(slot, n, f):
            dve.wait_ge(s["a_dwh"], n + 1)
            v.tensor_tensor(DL[slot][:, :], DR[slot][:, :], DH[slot][:, :].bitcast(F32), ALU.subtract)\
             .then_inc(s["v_dwl"], 1)
            dve.wait_ge(s["a_dhh"], n + 1)
            v.tensor_tensor(HTL[slot][:, :].unsqueeze(1), HT[:, bass.ds(f, 1), :],
                            HTH[slot][:, :].bitcast(F32).unsqueeze(1), ALU.subtract).then_inc(s["v_dhl"], 1)

        dve.wait_ge(s["v_ht"], 2 * FT)
        with dve.Fori(0, FT // 2) as i:
            for t in range(2):
                down_lo(t, i * 2 + t, i * 2 + t)
        for t in range(2):
            down_lo(t, FT + t, t)
        for r in range(1, RT, 2):
            dve.wait_ge(s["t_acc"], r + 1)
            v.tensor_copy(FO0[:, r, :], bank(r)).then_inc(s["v_fo"], 1)
        with dve.Fori(1, FT // 2) as i:
            for t in range(2):
                down_lo(t, i * 2 + (FT + t), i * 2 + t)
        for r in range(1, RT, 2):
            dve.wait_ge(s["t_acc"], RT + r + 1)
            v.tensor_copy(FO1[:, r, :], bank(r)).then_inc(s["v_fo"], 1)

        def ple_lo(n):
            dve.wait_ge(s["a_wgh"], n + 1)
            k, dh = divmod(n if n < 4 else n - 4, 2)
            hi, lo = (WUH, WUL) if n < 4 else (WGH, WGL)
            ds = slice(dh * 512, (dh + 1) * 512)
            v.tensor_tensor(lo[:, k, ds], WGR[n % 3][:, :], hi[:, k, ds].bitcast(F32), ALU.subtract)\
             .then_inc(s["v_wgl"], 1)

        def out_variance(r):
            dve.wait_ge(s["a_css"], 2 * r + 2)
            link(v.tensor_tensor(SMF[:, 2 * r:2 * r + 1], SMF[:, 2 * r:2 * r + 1], SMF[:, 2 * r + 1:2 * r + 2], ALU.add))
            v.tensor_scalar(SMF[:, 16 + r:17 + r], SMF[:, 2 * r:2 * r + 1], 1.0 / D, EPS, ALU.mult, ALU.add)\
             .then_inc(s["v_wv"], 1)

        def make_x2(r):
            dve.wait_ge(s["p_wr"], r + 1)
            dve.wait_ge(load_x2[r % 3], 16 * (r // 3 + 1))
            if r == 0:
                dve.wait_ge(s["load_gain2"], 32)
            for dh, fo in enumerate((FO0, FO1)):
                ds = slice(dh * 512, (dh + 1) * 512)
                ins = v.scalar_tensor_tensor(fo[:, r, :], fo[:, r, :], SMF[:, 24 + r:25 + r], GPF2[:, ds],
                                             ALU.mult, ALU.mult)
                link(ins)
                ins = v.tensor_tensor(X2[r % 3][:, ds], X2[r % 3][:, ds], fo[:, r, :], ALU.add)
            ins.then_inc(s["v_x2"], 1)

        def x2_lo(r):
            dve.wait_ge(s["a_x2h"], r + 1)
            v.tensor_tensor(X2L[r % 2][:, :, :], pair(r % 2).rearrange("p (k c) -> p k c", k=KT),
                            X2H[r % 2][:, :, :].bitcast(F32), ALU.subtract).then_inc(s["v_x2l"], 1)

        out_variance(0)
        for n in range(4):
            ple_lo(n)
        for k in range(2):
            dve.wait_ge(s["a_pth"], k + 1)
            v.tensor_tensor(PTL[:, k, :], pair(k), PTH[:, k, :].bitcast(F32), ALU.subtract).then_inc(s["v_ptl"], 1)
        make_x2(0)
        for n in range(4, 20):
            ple_lo(n)
            if n == 8:
                x2_lo(0)
            if n in (5, 11, 17):
                out_variance((n + 1) // 6)
        make_x2(1)
        for r in range(RT):
            if r + 1 < RT:
                x2_lo(r + 1)
            if r + 4 < RT and r >= 0:
                pass
            dve.wait_ge(s["a_sig"], r + 1)
            dve.wait_ge(s["t_em"], r + 1)
            if r >= 2:
                dve.wait_ge(st_out[r % 2], 16 * (r // 2))
            v.tensor_tensor(UU[r % 2][:, :], pair(3), SGG[:, :], ALU.mult).then_inc(s["v_u"], 1)
            if r + 2 < RT:
                make_x2(r + 2)
            dve.wait_ge(s["a_uss"], r + 1)
            v.tensor_scalar(SMF[:, 40 + r:41 + r], SMF[:, 32 + r:33 + r], 1.0 / D, EPS, ALU.mult, ALU.add)\
             .then_inc(s["v_uv"], 1)
            if r + 4 < RT:
                out_variance(r + 4)
            dve.wait_ge(s["p_ur"], r + 1)
            link(v.scalar_tensor_tensor(UU[r % 2][:, :], UU[r % 2][:, :], SMF[:, 48 + r:49 + r], GPL[:, :],
                                        ALU.mult, ALU.mult))
            v.tensor_tensor(UU[r % 2][:, :], UU[r % 2][:, :], X2[r % 3][:, :], ALU.add).then_inc(s["v_out"], 1)

    @block.gpsimd
    def _(pool):
        g_ = nc.gpsimd
        made = [0]

        def link(ins):
            made[0] += 1
            ins.then_inc(s["p_link"], 1)
            pool.wait_ge(s["p_link"], made[0])

        def rsqrt(dst, src):
            n = src.shape[1]
            return g_.tensor_tensor(dst, src, cols["half"][:, 0:n], ALU.pow)

        def w_lo(n):
            c, k = divmod(n, KT)
            w = width(c)
            pool.wait_ge(s["a_whi"], n + 1)
            g_.tensor_tensor(WBL[c % 2][:, k, 0:w], RAW[n % 4][:, 0:w], WBH[c % 2][:, k, 0:w].bitcast(F32),
                             ALU.subtract).then_inc(s["p_wlo"], 1)

        link(g_.memset(cols["half"], -0.5))
        for r in range(RT + 2):
            if r < RT:
                pool.wait_ge(s["v_var"], r + 1)
                rsqrt(cols["rs0"][:, r:r + 1], cols["v0"][:, r:r + 1]).then_inc(s["p_rs"], 1)
            if r >= 2:
                w_lo(r - 2)
        link(g_.memset(TRI[:, :], 0.0))
        g_.affine_select(out=TRI[:, P:2 * P], in_=TRI[:, P:2 * P], compare_op=ALU.is_ge, fill=MASKED, base=0,
                         pattern=[[-1, P]], channel_multiplier=1).then_inc(s["p_tri"], 1)
        for n in range(KT, 3 * KT):
            w_lo(n)
        pool.wait_ge(s["v_nrm"], 1)
        rsqrt(cols["rsn"], cols["vn"]).then_inc(s["p_nrs"], 1)
        pool.wait_ge(s["v_ac"], 1)
        for i in range(2):
            g_.memset(STG[i][:, RV:RG_], 0.0).then_inc(s["p_pad"], 1)

        def causal(b):
            pool.wait_ge(s["v_acc"], H * (b - B0 + 1))
            diag = SC[b - B0][:, b * P:(b + 1) * P]
            g_.affine_select(out=diag, in_=diag, compare_op=ALU.is_ge, fill=NONCAUSAL, base=0,
                             pattern=[[-1, P]], channel_multiplier=1).then_inc(s["p_caus"], 1)

        def rotate(n):
            r = n % RT
            st = STG[n % 2]
            pool.wait_ge(s["a_ev"], 2 * KT + n + 1)
            if n == 0:
                pool.wait_ge(s["a_trig"], 2)
            else:
                pool.wait_ge(s["p_rot"], n)
            x8 = st[:, 0:256].rearrange("p (g c) -> p g c", c=32)
            x4, a4, b4 = (a.rearrange("p (g a c) -> p g a c", a=2, c=32) for a in (st[:, 0:256], RT1[:, :], RT2[:, :]))
            cos8 = COS[:, r, :].unsqueeze(1).to_broadcast([P, 8, 32])
            sin4 = SIN[:, r, :].unsqueeze(1).to_broadcast([P, 4, 32])
            g_.tensor_tensor(RT1[:, :].rearrange("p (g c) -> p g c", c=32), x8, cos8, ALU.mult)
            g_.tensor_tensor(b4[:, :, 0, :], x4[:, :, 1, :], sin4, ALU.mult)
            link(g_.tensor_tensor(b4[:, :, 1, :], x4[:, :, 0, :], sin4, ALU.mult))
            g_.tensor_tensor(x4[:, :, 0, :], a4[:, :, 0, :], b4[:, :, 0, :], ALU.subtract)
            g_.tensor_tensor(x4[:, :, 1, :], a4[:, :, 1, :], b4[:, :, 1, :], ALU.add).then_inc(s["p_rot"], 1)

        for g in range(2 * KT, LAST):
            if g + KT < LAST:
                w_lo(g + KT)
            if g < 6 * KT:
                rotate(g - 2 * KT)
            for n in items(g):
                if n % H == H - 1:
                    causal(B0 + n // H)

        def next_state(n):
            hp, r = divmod(n, RT)
            pool.wait_ge(s["a_rb"], n + 1)
            if r == 0 and hp >= 2:
                pool.wait_ge(s["t_ro"], RT * (hp - 1))
            kv, rs = QKT[hp % 2][:, r, 2 * P:3 * P], RST[hp % 2]
            link(g_.tensor_tensor(rs[:, r + 1, :], rs[:, r, :], kv, ALU.add))
            ins = g_.tensor_tensor(rs[:, r + 1, :], rs[:, r + 1, :], CD[:, hp, :], ALU.mult)
            ins.then_inc(s["p_rst"], 1)
            pool.wait_ge(s["p_rst"], hp * (RT - 1) + r + 1)

        def causal_scores(n):
            pool.wait_ge(s["a_st"], n + 1)
            st = ST[n % 2][:, :].rearrange("p (h i) -> p h i", h=2)
            g_.affine_select(out=st, in_=st, compare_op=ALU.is_ge, fill=0.0, base=0,
                             pattern=[[0, 2], [1, P]], channel_multiplier=-1).then_inc(s["p_st"], 1)

        pool.wait_ge(s["t_unit"], LAST)
        for i in range(2):
            g_.memset(RST[i][:, :, :], 0.0).then_inc(s["p_zero"], 1)
        pool.wait_ge(s["p_zero"], 2)
        pool.wait_ge(s["load_cd"], 16)
        for n in range(SAHEAD):
            next_state(n)
        for n in range(NP * RT):
            hp, r = divmod(n, RT)
            m = n + SAHEAD
            if m < NP * RT and m % RT < RT - 1:
                next_state(m)
            causal_scores(n)
            if r == RT - 3 and hp >= 1:
                pool.wait_ge(s["v_lnv"], hp)
                rsqrt(cols["rsn"], cols["vn"]).then_inc(s["p_lnr"], 1)
            if n == (NP - 1) * RT + 1:
                pool.wait_ge(s["t_ro"], (NP - 1) * RT)
                g_.memset(WUK[:, :, :], 0.0).then_inc(s["p_wz"], 1)
                g_.memset(WUV[:, :, :], 0.0).then_inc(s["p_wz"], 1)
        pool.wait_ge(s["v_lnv"], NP)
        rsqrt(cols["rsn"], cols["vn"]).then_inc(s["p_lnr"], 1)

        for b in range(RT):
            pool.wait_ge(s["v_mv"], b + 1)
            rsqrt(cols["rsm"][:, b:b + 1], cols["vm"][:, b:b + 1]).then_inc(s["p_mr"], 1)
            pool.wait_ge(s["v_fv"], b + 1)
            rsqrt(cols["rsf"][:, b:b + 1], cols["vf"][:, b:b + 1]).then_inc(s["p_fr"], 1)

        def out_rsqrt(r):
            pool.wait_ge(s["v_wv"], r + 1)
            rsqrt(SMF[:, 24 + r:25 + r], SMF[:, 16 + r:17 + r]).then_inc(s["p_wr"], 1)

        for r in range(4):
            out_rsqrt(r)
        for r in range(RT):
            pool.wait_ge(s["v_uv"], r + 1)
            rsqrt(SMF[:, 48 + r:49 + r], SMF[:, 40 + r:41 + r]).then_inc(s["p_ur"], 1)
            if r + 4 < RT:
                out_rsqrt(r + 4)

    ctx.close()


_INS = ["x", "p", "positions", "pre_mix_g", "w_in", "ret_norm_g", "ret_norm_b", "kv_norm_g", "idx_k_norm_g",
        "idx_k_norm_b", "w_uk", "w_uv", "w_out", "post_mix_g", "pre_ffn_g", "w_ffn_gate", "w_ffn_up",
        "w_ffn_down", "post_ffn_g", "w_ple_up", "w_ple_gate", "ple_norm_g"]


def kernel(**inputs):
    import concourse.bacc as bacc
    from concourse.bass_utils import run_bass_kernel_spmd

    nc = bacc.Bacc("TRN2", target_bir_lowering=False, num_devices=1)
    arrays, args = {}, []
    inv_freq, small, decay = shape_tables()
    for name, a in [(n, inputs[n]) for n in _INS] + [("inv_freq", inv_freq), ("small_tab", small), ("decay_tab", decay)]:
        a = np.ascontiguousarray(a)
        arrays[f"in_{name}"] = a
        args.append(nc.dram_tensor(f"in_{name}", a.shape, mybir.dt.from_np(a.dtype), kind="ExternalInput").ap())
    args.append(nc.dram_tensor("out_0", (1, S, D), F32, kind="ExternalOutput").ap())
    args.append(nc.dram_tensor("x1_rows", (S, D), F32, kind="Internal").ap())
    args.append(nc.dram_tensor("ret_rows", (NP, S, RW), F32, kind="Internal").ap())
    build(nc, *args)
    r = run_bass_kernel_spmd(nc, [arrays], core_ids=[0])
    return r.results[0]["out_0"]
```

```python
from contextlib import ExitStack

import numpy as np

import concourse.bass as bass
from concourse import mybir

F32 = mybir.dt.float32
F32R = mybir.dt.float32r
I32 = mybir.dt.int32
ALU = mybir.AluOpType
ACT = mybir.ActivationFunctionType
AX = mybir.AxisListType

P = 128
S = 1024
D = 1024
RT = S // P
KT = D // P
H = 8
HD = 64
NP = H // 2
FF = 2816
FT = FF // P
PLE = 256
TOPK = 256
B0 = TOPK // P
C_RET, C_AQ, C_AC, C_IQ, C_IK, C_IW = 0, 2048, 2560, 2688, 3200, 3264
SMALL = P + HD + H
RW = 640
RV, RG_ = 2 * P, 4 * P
EPS = 1e-6
NONCAUSAL = -3.0e38
PICKED = -3.4e38
MASKED = -1.0e30
ROUNDS = TOPK // 8
UNROLL = 8
TWO_PI = 2.0 * np.pi
MAGIC = 12582912.0
PI_CAP = 3.1415925


def shape_tables():
    inv_freq = (1.0 / (10000.0 ** (np.arange(0, HD, 2, dtype=np.float64) / HD))).astype(np.float32)
    g = 1.0 - 2.0 ** (-5.0 - np.arange(H, dtype=np.float64))
    i = np.arange(P, dtype=np.float64)[:, None]
    q_scale = g[None, :] ** (i + 1.0)
    k_scale = g[None, :] ** (-(i + 1.0)) * HD ** -0.5
    small = np.concatenate([q_scale, k_scale, np.eye(P)], axis=1).astype(np.float32)
    same_head = np.kron(np.eye(2), np.ones((HD, HD)))
    chunk_decay = same_head[:, None, :] * np.repeat((g ** P).reshape(NP, 2), HD, axis=1)[None]
    return np.tile(inv_freq, (P, 1)), small, chunk_decay.astype(np.float32)


def cody_waite():
    c1 = 6.28125
    c2 = float(np.float32(TWO_PI - c1))
    c2 = float(np.float32(np.round(c2 * 2.0 ** 20) / 2.0 ** 20))
    return c1, c2, float(np.float32(TWO_PI - c1 - c2))


def build(nc, x, p, positions, pre_mix_g, w_in, ret_norm_g, ret_norm_b, kv_norm_g, idx_k_norm_g,
          idx_k_norm_b, w_uk, w_uv, w_out, post_mix_g, pre_ffn_g, w_ffn_gate, w_ffn_up, w_ffn_down,
          post_ffn_g, w_ple_up, w_ple_gate, ple_norm_g, inv_freq, small_tab, decay_tab, out, x1_dram, ret_dram):
    ctx = ExitStack()
    base = 16512
    kb = 1024

    def sb(name, shape, at, dt=F32):
        return nc.alloc_sbuf_tensor_at(name, shape, dt, offset=base + int(at * kb))

    def sem(name):
        return nc.alloc_semaphore(name)

    TAB = sb("tab", [P, 2 * H + P], 0)
    QSC, KSC, ID = TAB[:, 0:H], TAB[:, H:2 * H], TAB[:, 2 * H:]
    SML = sb("sml", [P, 256], 0.75)
    KVG = sb("kvg", [P, P], 1.75)
    IKG = sb("ikg", [P, HD], 2.25)
    IKB = sb("ikb", [P, HD], 2.5)
    INV = sb("inv", [P, 32], 2.75)
    COS = sb("cos", [P, RT, 32], 3)
    SIN = sb("sin", [P, RT, 32], 4)
    RT2 = sb("rt2", [P, 256], 5)
    TRI = sb("tri", [P, 2 * P], 6)
    WI = sb("wi", [P, RT, H], 7)
    M8 = sb("m8", [P, 8], 7.25)
    POSI = sb("posi", [P, RT], 7.3125, I32)

    cols = {}
    at = 0
    for name, n in (("ss0", 8), ("v0", 8), ("rs0", 8), ("half", 16), ("ssn", 16), ("vn", 16), ("rsn", 16),
                    ("mu", 8), ("pos", 8), ("sum", 16), ("rsum", 16), ("nmax", 4), ("ssm", 8), ("vm", 8),
                    ("rsm", 8), ("ssf", 8), ("vf", 8), ("rsf", 8)):
        cols[name] = SML[:, at:at + n]
        at += n
    assert at <= 256

    XTH = sb("xth", [P, KT, S], 12, F32R)
    XTL = sb("xtl", [P, KT, S], 44, F32R)
    WBH = [sb(f"wbh{i}", [P, KT, 512], 76 + 32 * i, F32R) for i in range(2)]
    WBL = [sb(f"wbl{i}", [P, KT, 512], 92 + 32 * i, F32R) for i in range(2)]
    XN = [sb(f"xn{r}", [P, D], 148 + 4 * r if r < RT - 1 else 8) for r in range(RT)]
    RAW = [sb(f"raw{i}", [P, 512], 140 + 2 * i if i < 4 else 184.5 + 2 * i) for i in range(8)]
    QW = S - B0 * P
    QS = sb("qs", [P, H, QW], 148, F32R)
    AQ = sb("aq", [P, NP, S], 148)
    CKVT = sb("ckvt", [P, S], 164)
    CKV = sb("ckv", [P, RT, P], 8)
    sc_off = [sum(range(B0 + 1, b + 1)) * P for b in range(B0, RT)]
    SC = [sb(f"sc{b}", [P, (b + 1) * P], 176 + sc_off[b - B0] * 4 / kb) for b in range(B0, RT)]
    GIN = sb("gin", [P, D], 176)
    ANG = sb("ang", [P, RT, 32], 180)
    ANK = sb("ank", [P, RT, 32], 181)
    ANR = sb("anr", [P, RT, 32], 182)
    NTMP = sb("ntmp", [P, RT, P], 176)
    NXM = sb("nxm", [P, RT, HD], 184)
    KN = sb("kn", [P, RT, P], 186)
    KH = sb("kh", [P, S], 192.5, F32R)
    KL = sb("kl", [P, S], 196.5, F32R)
    AC = sb("ac", [P, RT, SMALL], 200.5)
    STG = [sb(f"stg{i}", [P, RW], 200.5 + 2.5 * i) for i in range(2)]
    RT1 = sb("rt1", [P, 256], 205.5)

    RP = [sb(f"rp{i}", [P, RT, RW], 108 + 20 * i) for i in range(2)]
    QKT = [sb("qkt0", [P, RT, 384], 60), sb("qkt1", [P, RT, 384], 24)]
    ST = [sb(f"st{i}", [P, 256], 36 + i) for i in range(2)]
    RST = [sb("rst0", [P, RT, P], 72), sb("rst1", [P, RT, P], 54)]
    CD = sb("cd", [P, NP, P], 38)
    O = [sb(f"o{i}", [P, RT, P], 42 + 4 * i) for i in range(2)]
    SGR = [sb("sgr0", [P, RT, P], 50), sb("sgr1", [P, RT, P], 172)]
    PT1 = sb("pt1", [P, RT, P], 20)
    Y = sb("y", [P, RT, P], 12)
    RG = sb("rg", [P, 512], 16)
    RB = sb("rb", [P, 512], 18)
    YRT = [sb(f"yrt{i}", [P, S], a) for i, a in enumerate((168, 192.5, 196.5, 200.5))]

    WO = sb("wo", [P, KT, D], 76)
    WUK = sb("wuk", [P, H, P], 64)
    WUV = sb("wuv", [P, H, P], 68)
    FTR = sb("ftr", [P, KT, S], 12)
    XR = [sb(f"xr{i}", [P, D], 44 + 4 * i) for i in range(2)]
    GPO = sb("gpo", [P, D], 52)
    GPF = sb("gpf", [P, D], 56)
    QL = [sb("ql0", [P, H, P], 108), sb("ql1", [P, H, P], 60)]
    LM = [sb(f"lm{i}", [P, S], 112 + 4 * i) for i in range(2)]
    PT = [sb(f"pt{i}", [P, S], 120 + 4 * i) for i in range(2)]
    OTS = [sb(f"ots{i}", [P, 512], 128 + 2 * i) for i in range(2)]
    YD = sb("yd", [P, 512], 132)
    YDT = sb("ydt", [P, NP, P], 134)
    MXS = sb("mxs", [P, D], 136)
    FN = sb("fn", [P, D], 140)
    JK = sb("jk", [P, D], 144)

    FTH = [sb(f"fth{i}", [P, KT, 512], a, F32R) for i, a in enumerate((148, 44))]
    FTL = sb("ftl", [P, KT, S], 12, F32R)
    HT = sb("ht", [P, FT, S], 60)
    WR0 = [sb(f"wrf{j}", [P, KT, P], a) for j, a in enumerate((72, 108))]
    WR = [sb("wr0", [P, 2, KT, P], 2), sb("wr1", [P, 2, KT, P], 164)]
    WH = [sb(f"wh{i}", [P, 2, KT, P], 172 + 16 * i, F32R) for i in range(2)]
    WL = [sb(f"wl{i}", [P, 2, KT, P], 180 + 16 * i, F32R) for i in range(2)]
    SG = [sb("sg0", [P, 512], 204), sb("sg1", [P, 512], 10)]
    HTH = [sb(f"hth{i}", [P, S], 164 + 8 * i, F32R) for i in range(2)]
    HTL = [sb(f"htl{i}", [P, S], 168 + 8 * i, F32R) for i in range(2)]
    DR = [sb(f"dr{i}", [P, 512], 180 + 2 * i) for i in range(2)]
    DH = [sb(f"dh{i}", [P, 512], 184 + 4 * i, F32R) for i in range(2)]
    DL = [sb(f"dl{i}", [P, 512], 186 + 4 * i, F32R) for i in range(2)]
    FO0 = sb("fo0", [P, RT, 512], 28)
    FO1 = sb("fo1", [P, RT, 512], 12)

    WG = sb("wg", [P, KT, 2, D], 60, F32R)
    WGR = [sb(f"wgr{i}", [P, D], 192 + 8 * i) for i in range(2)]
    WUH = sb("wuh", [P, 2, D], 148, F32R)
    WUL = sb("wul", [P, 2, D], 156, F32R)
    PN = sb("pn", [P, RT, PLE], 2)
    PTH = sb("pth", [P, 2, S], 44, F32R)
    PTL = sb("ptl", [P, 2, S], 52, F32R)
    X2 = [sb(f"x2{i}", [P, D], a) for i, a in enumerate((2, 6, 172, 176))]
    X2H = [sb(f"x2h{i}", [P, KT, P], 124 + 8 * i, F32R) for i in range(2)]
    X2L = [sb(f"x2l{i}", [P, KT, P], 128 + 8 * i, F32R) for i in range(2)]
    GPF2 = sb("gpf2", [P, D], 140)
    GPL = sb("gpl", [P, D], 144)
    UU = [sb("uu0", [P, D], 164), sb("uu1", [P, D], 184)]
    SGG = sb("sgg", [P, D], 168)
    JF = sb("jf", [P, D], 196)
    SMF = sb("smf", [P, 64], 206.25)

    PS = ctx.enter_context(nc.psum_tensor("ps", [P, 8 * 512], F32))

    def bank(i, n=512):
        return PS[:, 512 * i:512 * i + n]

    names = """a_sq v_var p_rs v_xn t_xt a_xh v_xl v_ang a_trig a_whi v_qlo a_kh v_kl p_pad p_wz p_wlo t_unit a_ev
        v_link p_link v_nrm p_nrs v_kn v_ac t_nt a_nt t_ix a_rl v_acc p_caus v_mask p_tri p_rot
        t_rb a_rb p_rst t_sc a_st p_st t_ro a_o a_silu p_zero v_lnv p_lnr v_y t_yr a_yrt
        t_lg v_lm a_ex t_tp a_tp t_pv a_ots t_ms a_ms v_ms a_mss v_mv p_mr v_x1 a_fss v_fv p_fr v_fn
        a_fth v_ftl a_gh v_gl t_gu a_sg v_ht a_dwh v_dwl a_dhh v_dhl t_dn t_acc a_fo v_fo
        a_wgh v_wgl t_pt a_pth v_ptl a_sqs v_wv p_wr v_x2 t_x2 a_x2h v_x2l t_gt t_em a_sig v_u v_uv p_ur
        v_out load_wf load_cd load_tab load_pos load_const load_gin load_gain load_wuk load_wo
        load_retg load_pn load_gain2 st_x1""".split()
    s = {n: sem(n) for n in names}
    load_x = [sem(f"load_x{i}") for i in range(RT)]
    load_raw = [sem(f"load_raw{i}") for i in range(8)]
    st_ret = [sem(f"st_ret{i}") for i in range(2)]
    st_out = [sem(f"st_out{i}") for i in range(2)]
    load_rp = [[sem(f"load_rp{i}{h}") for h in "ab"] for i in range(2)]
    load_xr = [sem(f"load_xr{i}") for i in range(2)]
    load_wr = [sem(f"load_wr{i}") for i in range(2)]
    load_dr = [sem(f"load_dr{i}") for i in range(2)]
    load_wg = [sem(f"load_wg{i}") for i in range(2)]
    load_x2 = [sem(f"load_x2{i}") for i in range(4)]

    NCH = 7
    block = ctx.enter_context(nc.Block())

    def pair(j, n=1024):
        return PS[:, 1024 * j:1024 * j + n]

    def raw_slot(n):
        return n if n < KT else n % 4

    def raw_count(n):
        return 32 + (16 * ((n - KT) // 4 + 1) if n >= KT else 0)

    def width(c):
        return SMALL if c == 0 else 512

    def unit_width(g):
        return 512 - B0 * P if KT <= g < KT + 4 else width(g // KT)

    IX0, ITEMS, PER = 2 * KT, (RT - B0) * H, 3

    def items(g):
        return range(max(0, (g - IX0) * PER), min(ITEMS, (g - IX0 + 1) * PER)) if g >= IX0 else range(0)

    EARLY, BETWEEN = 22, 2
    BESIDE = {0: 0, 1: 8, 2: 10, 3: 12, 4: 13, 5: 13, 6: 14}
    ROUND_HEADS = (3, 4, 3, 4, 3, 4, 4, 3, 0, 5, 7, 2, 1, 5)
    beside = [(RT - 3, n) for n in range(EARLY + 2 * BETWEEN, ROUNDS)]
    beside += [(b, n) for b in (RT - 2, RT - 1) for n in range(ROUNDS)]
    assert sum(BESIDE.values()) == len(beside)
    assert all(sum(BESIDE[i] for i in range(b)) >= sum(c[0] <= b for c in beside) for b in range(RT - 3, RT))

    def rounds_beside(t):
        b, h = divmod(t, H)
        return ROUND_HEADS[:BESIDE.get(b, 0)].count(h)

    HALF = (slice(0, HD), slice(HD, P))

    def query_cols(g):
        return slice(0, 512 - B0 * P) if g < KT + 4 else slice(512 - B0 * P, S - B0 * P)

    KEYS_AT = KT + 5
    LAST = NCH * KT
    YR_LAG = 3
    RAHEAD = 3
    SAHEAD = 2
    STEPS = RT * H
    ADD_LAG, SQ_LAG, FV_LAG, FN_LAG, FT_LAG = 7, 8, 9, 10, 11
    TAIL = FT_LAG + 1
    YR_STEP = {1: NP - 2, 9: NP - 1}

    def at_block(t, lag):
        b, h = divmod(t - lag, H)
        return b if h == H - 1 and 0 <= b < RT else None

    def ret_pair_due(n):
        hp, r = divmod(n - YR_LAG, RT)
        return hp - 2 if r == 0 and 2 <= hp < NP else None

    def at_half(t, lag):
        g, h = divmod(t - lag, 4)
        return g if h == 3 and 0 <= g < 2 * RT else None

    def ql_due(t):
        b, h = divmod(t + 4, H)
        return (b, h) if h < 2 and 1 <= b < RT else None

    tp_use, ms_use = [], [("ql", 0, 0), ("ql", 0, 1)]
    for t in range(STEPS + TAIL):
        if at_block(t, 5) is not None:
            tp_use.append(("mx", at_block(t, 5)))
        if 1 <= t <= STEPS:
            tp_use.append(("tr", t - 1))
        if t in YR_STEP:
            tp_use.append(("yr", YR_STEP[t]))
        if at_block(t, FT_LAG) is not None:
            tp_use.append(("ft", at_block(t, FT_LAG)))
        if ql_due(t) is not None:
            ms_use.append(("ql", *ql_due(t)))
        if at_half(t, 3) is not None:
            ms_use.append(("y", at_half(t, 3)))
        if at_block(t, 4) is not None:
            ms_use.append(("yt", at_block(t, 4)))
    tp_at = {u: n for n, u in enumerate(tp_use)}
    ms_at = {u: n for n, u in enumerate(ms_use)}

    def ms_read(n):
        v = sum(u[0] == "y" for u in ms_use[:n])
        return n - v, v

    squares = [("fo0", r) for r in range(RT)] + [("fo1", r) for r in range(4)]
    for r in range(RT):
        squares += [("fo1", r + 4)] if r + 4 < RT else []
        squares.append(("u", r))
    sq_at = {u: n + 1 for n, u in enumerate(squares)}
    DU = 4
    DFIRST, DLOOP = 2, 4
    assert DU * DLOOP // 2 == KT and DFIRST + DU * DLOOP + 4 == FT

    LEAD = 3
    PROLOGUE = ((0, 0), (1, 0), (0, 1), (1, 1))

    @block.sync
    def _(sp):
        x_t = x.rearrange("b (r p) d -> p (b r) d", p=P)

        def row_gain(dst, g, sm):
            sp.dma_start(dst[:, :], g[0:1, :].to_broadcast([P, g.shape[1]])).then_inc(s[sm], 16)

        def proj_weights(n):
            c, k = divmod(n, KT)
            if n >= KT:
                before = n - KT if n < KT + 4 else n - 4
                sp.wait_ge(s["a_whi"], before + 1)
                sp.wait_ge(s["p_wlo"], before + 1)
            dst, sm = RAW[raw_slot(n)], load_raw[raw_slot(n)]
            w = w_in[0, k * P:(k + 1) * P, :]
            if c == 1:
                sp.dma_start(dst[:, :], w[:, C_IQ:C_IQ + 512]).then_inc(sm, 16)
            elif c == 0:
                sp.dma_start(dst[:, 0:P], w[:, C_AC:C_AC + P]).then_inc(sm, 16)
                sp.dma_start(dst[:, P:SMALL], w[:, C_IK:C_IK + HD + H]).then_inc(sm, 16)
            elif c == 6:
                sp.dma_start(dst[:, :], w[:, C_AQ:C_AQ + 512]).then_inc(sm, 16)
            else:
                src = w[:, 0:4 * 512].rearrange("p (g c) -> p g c", g=4)[:, :, (c - 2) * P:(c - 1) * P]
                sp.dma_start(dst[:, :].rearrange("p (g c) -> p g c", g=4), src).then_inc(sm, 16)

        def store_retention(n):
            hp, r = divmod(n, RT)
            sp.wait_ge(s["p_rot"], n + 1)
            sp.dma_start(ret_dram[hp, r * P:(r + 1) * P, :], STG[n % 2][:, :]).then_inc(st_ret[n % 2], 16)

        sp.dma_start(XN[0][:, :], x_t[:, 0, :]).then_inc(load_x[0], 16)
        row_gain(GIN, pre_mix_g, "load_gin")
        sp.dma_start(TAB[:, :], small_tab).then_inc(s["load_tab"], 16)
        for n in range(4):
            proj_weights(n)
        sp.dma_start(XN[1][:, :], x_t[:, 1, :]).then_inc(load_x[1], 16)
        for n in range(4, KT):
            proj_weights(n)
        for r in range(2, 5):
            sp.dma_start(XN[r][:, :], x_t[:, r, :]).then_inc(load_x[r], 16)
        with nc.allow_non_contiguous_dma(reason="1024 positions, once"):
            sp.dma_start(POSI[:, :], positions[0].rearrange("(r p) -> p r", p=P)).then_inc(s["load_pos"], 16)
        sp.dma_start(INV[:, :], inv_freq).then_inc(s["load_pos"], 16)
        for r in range(5, RT):
            sp.dma_start(XN[r][:, :], x_t[:, r, :]).then_inc(load_x[r], 16)
        row_gain(KVG, kv_norm_g, "load_const")
        row_gain(IKG, idx_k_norm_g, "load_const")
        row_gain(IKB, idx_k_norm_b, "load_const")
        for g in range(-4, LAST):
            if g + 12 < LAST:
                proj_weights(g + 12)
            if 0 <= g - 17 < NP * RT:
                store_retention(g - 17)
        sp.wait_ge(s["t_unit"], 6 * RT)
        for hp in range(NP):
            for i in range(2):
                sp.wait_ge(st_ret[i], 16 * 4 * (hp + 1))
            if hp == 1:
                sp.wait_ge(s["t_unit"], LAST)
                sp.dma_start(CD[:, :, :], decay_tab).then_inc(s["load_cd"], 16)
            for half in range(2):
                rows = slice(half * RT // 2, (half + 1) * RT // 2)
                if hp >= 2:
                    sp.wait_ge(s["a_silu"], hp - 1)
                    sp.wait_ge(s["t_ro"], RT * (hp - 2) + (half + 1) * RT // 2)
                sp.dma_start(RP[hp % 2][:, rows, :], ret_dram[hp].rearrange("(r p) c -> p r c", p=P)[:, rows, :])\
                  .then_inc(load_rp[hp % 2][half], 16)
            if hp == 1:
                for dst, g in ((RG, ret_norm_g), (RB, ret_norm_b)):
                    sp.dma_start(dst[:, :], g[0:1].rearrange("a h d -> a (h d)").to_broadcast([P, 512]))\
                      .then_inc(s["load_retg"], 16)
                sp.dma_start(WO[:, :, :], w_out[0].rearrange("(k p) d -> p k d", p=P)).then_inc(s["load_wo"], 16)
        sp.wait_ge(s["p_wz"], 2)
        for h in range(H):
            j = HD * (h % 2)
            sp.dma_start(WUK[j:j + HD, h, :], w_uk[0, h]).then_inc(s["load_wuk"], 16)
            sp.dma_start(WUV[:, h, j:j + HD], w_uv[0, h]).then_inc(s["load_wuk"], 16)
        sp.wait_ge(s["v_y"], NP)
        row_gain(GPO, post_mix_g, "load_gain")
        row_gain(GPF, pre_ffn_g, "load_gain")
        for b in range(2):
            sp.dma_start(XR[b][:, :], x_t[:, b, :]).then_inc(load_xr[b], 16)
        def gate_up(slot, f):
            for j, w in enumerate((w_ffn_gate, w_ffn_up)):
                src = w[0].rearrange("(k p) f -> p k f", p=P)[:, :, bass.ds(f * P, P)]
                sp.dma_start(WR[slot][:, j, :, :], src).then_inc(load_wr[slot], 16)

        for b in range(RT):
            if b == RT - 2:
                sp.wait_ge(s["t_lg"], (RT - 1) * H)
                for j, w in enumerate((w_ffn_gate, w_ffn_up)):
                    sp.dma_start(WR0[j][:, :, :], w[0].rearrange("(k p) f -> p k f", p=P)[:, :, 0:P])\
                      .then_inc(s["load_wf"], 16)
            if b == RT - 1:
                sp.wait_ge(s["t_tp"], tp_at[("mx", b)] + 1)
                gate_up(1, 1)
            sp.wait_ge(s["v_x1"], b + 1)
            sp.dma_start(x1_dram[b * P:(b + 1) * P, :], XR[b % 2][:, :]).then_inc(s["st_x1"], 16)
            if b + 2 < RT:
                sp.wait_ge(s["st_x1"], 16 * (b + 1))
                sp.wait_ge(s["a_fss"], b + 1)
                sp.wait_ge(s["v_fn"], b + 1)
                sp.dma_start(XR[b % 2][:, :], x_t[:, b + 2, :]).then_inc(load_xr[b % 2], 16)

        sp.wait_ge(s["t_ms"], len(ms_use))
        sp.wait_ge(s["v_lm"], STEPS)
        sp.wait_ge(s["t_pv"], STEPS)
        with sp.Fori(1, FT // 2) as i:
            for t in range(2):
                sp.wait_ge(s["v_gl"], i * 2 + (t - 1))
                gate_up(t, i * 2 + t)

        def down(slot, f, dh):
            src = w_ffn_down[0, bass.ds(f * P, P), dh * 512:(dh + 1) * 512]
            sp.dma_start(DR[slot][:, :], src).then_inc(load_dr[slot], 16)

        sp.wait_ge(s["v_gl"], FT - 1)
        sp.dma_start(PN[:, :, :], p[0, 0].rearrange("(r q) c -> q r c", q=P)).then_inc(s["load_pn"], 16)
        sp.wait_ge(s["t_gu"], 2 * FT - 2)
        for t in range(2):
            down(t, t, 0)
        sp.wait_ge(s["t_gu"], 2 * FT)
        for k in range(2):
            sp.dma_start(WGR[k][:, :], w_ple_up[0, k * P:(k + 1) * P, :]).then_inc(load_wg[k], 16)
        with sp.Fori(1, FT // 2) as i:
            for t in range(2):
                sp.wait_ge(s["v_dwl"], i * 2 + (t - 1))
                down(t, i * 2 + t, 0)
        for f in range(DFIRST):
            sp.wait_ge(s["v_dwl"], FT + f - 1)
            down(f, f, 1)
        with sp.Fori(0, DLOOP) as i:
            for t in range(DU):
                sp.wait_ge(s["v_dwl"], i * DU + (FT + DFIRST + t - 1))
                down(t % 2, i * DU + (DFIRST + t), 1)
                if t % 2 == 1:
                    sp.wait_ge(s["v_wgl"], i * 2 + (t // 2 + 1))
                    sp.dma_start(WGR[t // 2][:, :], w_ple_gate[0, bass.ds((i * 2 + t // 2) * P, P), :])\
                      .then_inc(load_wg[t // 2], 16)
        for f in range(FT - 4, FT):
            sp.wait_ge(s["v_dwl"], FT + f - 1)
            down(f % 2, f, 1)

        def load_x1(r):
            sp.dma_start(X2[r % 4][:, :], x1_dram[r * P:(r + 1) * P, :]).then_inc(load_x2[r % 4], 16)

        sp.wait_ge(s["v_ptl"], 2)
        for r in range(2):
            load_x1(r)
        sp.wait_ge(s["a_dhh"], 2 * FT)
        sp.wait_ge(s["v_dhl"], 2 * FT)
        row_gain(GPF2, post_ffn_g, "load_gain2")
        row_gain(GPL, ple_norm_g, "load_gain2")
        sp.wait_ge(s["t_dn"], 2 * FT)
        for r in range(2, 4):
            load_x1(r)
        for r in range(RT):
            sp.wait_ge(s["v_out"], r + 1)
            sp.dma_start(out[0, r * P:(r + 1) * P, :], UU[r % 2][:, :]).then_inc(st_out[r % 2], 16)
            if r + 4 < RT:
                load_x1(r + 4)
        for i in range(2):
            sp.wait_ge(st_out[i], 16 * RT // 2)

    @block.tensor
    def _(pe):
        def mm3(o, ah, al, wh, wl, start, stop):
            pe.matmul(o, ah, wh, start=start, stop=False)
            pe.matmul(o, ah, wl, start=False, stop=False)
            return pe.matmul(o, al, wh, start=False, stop=stop)

        pe.wait_ge(s["load_tab"], 16)
        def row_transposes(r):
            pe.wait_ge(s["v_xn"], r + 1)
            if r >= 2:
                pe.wait_ge(s["v_xl"], r - 1)
            for k in range(KT):
                m = pe.transpose(pair(1 + r % 2)[:, k * P:(k + 1) * P], XN[r][:, k * P:(k + 1) * P], ID)
            m.then_inc(s["t_xt"], 1)

        def key_transposes():
            pe.wait_ge(s["v_kn"], 1)
            pe.wait_ge(s["v_xl"], RT)
            for r in range(RT):
                m = pe.transpose(pair(1)[:, r * P:(r + 1) * P], KN[:, r, :], ID)
            m.then_inc(s["t_nt"], 1)

        def indexer_scores(n):
            b, h = B0 + n // H, n % H
            if n == 0:
                pe.wait_ge(s["v_kl"], 1)
            if n >= 2:
                pe.wait_ge(s["v_acc"], n - 1)
            keys = (b + 1) * P
            for k0 in range(0, keys, 512):
                k1 = min(k0 + 512, keys)
                for key in (KH, KL):
                    m = pe.matmul(pair(1 + n % 2)[:, k0:k1], QS[:, h, (b - B0) * P:(b - B0 + 1) * P], key[:, k0:k1],
                                  start=(key is KH), stop=(key is KL))
            m.then_inc(s["t_ix"], 1)

        def unit(g):
            c, u = divmod(g, KT)
            if g >= 2:
                pe.wait_ge(s["a_ev"], g - 1)
                if g >= KT + 2:
                    pe.wait_ge(s["v_qlo"], min(g - 1 - KT, KT))
            pe.wait_ge(s["v_xl"], min(g + 1, RT))
            o = bank(g % 2, unit_width(g))
            hi, lo = WBH[c % 2], WBL[c % 2]
            todo = list(items(g))
            for k in range(KT):
                if todo and k in (1, 4, 7):
                    indexer_scores(todo.pop(0))
                if u == 0:
                    pe.wait_ge(s["p_wlo"], c * KT + k + 1)
                if c in (1, 6):
                    m, half = u % 4, u // 4
                    cs, rs = slice(m * P, (m + 1) * P), slice(half * 512 + 512 - unit_width(g), (half + 1) * 512)
                    last = mm3(o, hi[:, k, cs], lo[:, k, cs], XTH[:, k, rs], XTL[:, k, rs], k == 0, k == KT - 1)
                else:
                    rs = slice(u * P, (u + 1) * P)
                    last = mm3(o, XTH[:, k, rs], XTL[:, k, rs], hi[:, k, 0:width(c)], lo[:, k, 0:width(c)],
                               k == 0, k == KT - 1)
            last.then_inc(s["t_unit"], 1)

        for r in range(RT + 2):
            if r < RT:
                row_transposes(r)
            if r >= 2:
                unit(r - 2)
        for g in range(KT, LAST):
            unit(g)
            if g == KEYS_AT:
                key_transposes()

        def pair_bank(n):
            hp, r = divmod(n, RT)
            if r % (RT // 2) == 0:
                pe.wait_ge(load_rp[hp % 2][2 * r // RT], 16 * (hp // 2 + 1))
            if n == 0:
                pe.wait_ge(s["a_ev"], LAST)
            if n >= 2:
                pe.wait_ge(s["a_rb"], n - 1)
            if ret_pair_due(n - RAHEAD - 1) is not None:
                pe.wait_ge(s["a_yrt"], ret_pair_due(n - RAHEAD - 1) + 1)
            rp, o = RP[hp % 2], bank(n % 2)
            pe.transpose(o[:, 0:P], rp[:, r, 0:P], ID)
            m = pe.transpose(o[:, P:2 * P], rp[:, r, P:2 * P], ID)
            if r < RT - 1:
                v01 = rp[:, r, RV:RV + 384].rearrange("p (h c) -> p h c", h=2)[:, :, 0:HD]
                m = pe.matmul(o[:, 2 * P:3 * P], rp[:, r, P:2 * P], v01, start=True, stop=True)
            m.then_inc(s["t_rb"], 1)

        def scores(n):
            hp, r = divmod(n, RT)
            pe.wait_ge(s["a_rb"], n + 1)
            if n >= 2:
                pe.wait_ge(s["a_st"], n - 1)
            for h in range(2):
                j = slice(HD * h, HD * h + HD)
                qk = QKT[hp % 2]
                m = pe.matmul(bank(2 + 2 * (n % 2) + h, P), qk[j, r, P:2 * P], qk[j, r, 0:P],
                              start=True, stop=True)
            m.then_inc(s["t_sc"], 1)

        def ret_out(n):
            hp, r = divmod(n, RT)
            pe.wait_ge(s["p_st"], n + 1)
            if r > 0:
                pe.wait_ge(s["p_rst"], hp * (RT - 1) + r)
            else:
                pe.wait_ge(s["p_zero"], 2)
            if n >= 2:
                pe.wait_ge(s["a_o"], n - 1)
            o = bank(6 + n % 2, P)
            pe.matmul(o, QKT[hp % 2][:, r, 0:P], RST[hp % 2][:, r, :], start=True, stop=False)
            for h in range(2):
                m = pe.matmul(o, ST[n % 2][:, h * P:(h + 1) * P], RP[hp % 2][:, r, RV + h * P:RV + (h + 1) * P],
                              start=False, stop=(h == 1))
            m.then_inc(s["t_ro"], 1)

        def ret_transpose(hp):
            pe.wait_ge(s["v_y"], hp + 1)
            pe.wait_ge(s["a_rb"], min((hp + 2) * RT + YR_LAG + RAHEAD + 1, NP * RT))
            for r in range(RT):
                m = pe.transpose(pair(0)[:, r * P:(r + 1) * P], Y[:, r, :], ID)
            m.then_inc(s["t_yr"], 1)

        for n in range(RAHEAD):
            pair_bank(n)
        for n in range(NP * RT + 1):
            if n + RAHEAD < NP * RT:
                pair_bank(n + RAHEAD)
            if n < NP * RT:
                scores(n)
            if n >= 1:
                ret_out(n - 1)
            if ret_pair_due(n) is not None:
                ret_transpose(ret_pair_due(n))

        def tp_free(use):
            if tp_at[use] >= 1:
                pe.wait_ge(s["a_tp"], tp_at[use])

        def ms_free(use):
            a, v = ms_read(ms_at[use])
            if a:
                pe.wait_ge(s["a_ms"], a)
            if v:
                pe.wait_ge(s["v_ms"], v)

        def latent_queries(b, half):
            ms_free(("ql", b, half))
            for hh in range(4):
                h = 4 * half + hh
                m = pe.matmul(bank(7)[:, hh * P:(hh + 1) * P], WUK[:, h, :], AQ[:, h // 2, b * P:(b + 1) * P],
                              start=True, stop=True)
            m.then_inc(s["t_ms"], 1)

        def logits(t):
            b, h = divmod(t, H)
            if h == 0:
                pe.wait_ge(s["a_ms"], ms_read(ms_at[("ql", b, 1)])[0] + 1)
            if t == 0:
                pe.wait_ge(s["a_nt"], 1)
            if t >= 2:
                pe.wait_ge(s["v_lm"], t - 1)
            keys = (b + 1) * P
            for k0 in range(0, keys, 512):
                k1 = min(k0 + 512, keys)
                m = pe.matmul(pair(t % 2)[:, k0:k1], QL[b % 2][:, h, :], CKVT[:, k0:k1], start=True, stop=True)
            m.then_inc(s["t_lg"], 1)

        def prob_transposes(t):
            b = t // H
            tp_free(("tr", t))
            pe.wait_ge(s["a_ex"], t + 1)
            for j in range(b + 1):
                m = pe.transpose(pair(2)[:, j * P:(j + 1) * P], LM[t % 2][:, j * P:(j + 1) * P], ID)
            m.then_inc(s["t_tp"], 1)

        def prob_values(t):
            b, h = divmod(t, H)
            pe.wait_ge(s["a_tp"], tp_at[("tr", t)] + 1)
            if t % 4 == 0 and t >= 4:
                pe.wait_ge(s["a_ots"], t // 4)
            for j in range(b + 1):
                m = pe.matmul(bank(6)[:, (h % 4) * P:(h % 4 + 1) * P], CKV[:, j, :], PT[t % 2][:, j * P:(j + 1) * P],
                              start=(j == 0), stop=(j == b))
            m.then_inc(s["t_pv"], 1)

        def head_values(g):
            pe.wait_ge(s["a_ots"], g + 1)
            ms_free(("y", g))
            for hh in range(4):
                m = pe.matmul(bank(7)[:, hh // 2 * P:(hh // 2 + 1) * P], OTS[g % 2][:, hh * P:(hh + 1) * P],
                              WUV[:, 4 * (g % 2) + hh, :], start=(hh % 2 == 0), stop=(hh % 2 == 1))
            m.then_inc(s["t_ms"], 1)

        def y_transposes(b):
            ms_free(("yt", b))
            for k in range(NP):
                m = pe.transpose(bank(7)[:, k * P:(k + 1) * P], YD[:, k * P:(k + 1) * P], ID)
            m.then_inc(s["t_ms"], 1)

        def pair_outputs_transposes(hp):
            pe.wait_ge(s["v_y"], hp + 1)
            tp_free(("yr", hp))
            for r in range(RT):
                m = pe.transpose(pair(2)[:, r * P:(r + 1) * P], Y[:, r, :], ID)
            m.then_inc(s["t_tp"], 1)
            if hp < NP - 1:
                pe.wait_ge(s["t_tp"], tp_at[("yr", hp)] + 1)
                pe.sem_inc(s["t_yr"], 1)

        def out_projection(b, part):
            if part == 0:
                tp_free(("mx", b))
            else:
                pe.wait_ge(s["a_ms"], ms_read(ms_at[("yt", b)])[0] + 1)
            for k in range(part * NP, (part + 1) * NP):
                src = YRT[k][:, b * P:(b + 1) * P] if k < NP else YDT[:, k - NP, :]
                for dh in range(2):
                    m = pe.matmul(pair(2)[:, dh * 512:(dh + 1) * 512], src, WO[:, k, dh * 512:(dh + 1) * 512],
                                  start=(k == 0), stop=(k == KT - 1))
            if part == 1:
                m.then_inc(s["t_tp"], 1)

        def ffn_transposes(b):
            pe.wait_ge(s["v_fn"], b + 1)
            tp_free(("ft", b))
            for k in range(KT):
                m = pe.transpose(pair(2)[:, k * P:(k + 1) * P], FN[:, k * P:(k + 1) * P], ID)
            m.then_inc(s["t_tp"], 1)

        pe.wait_ge(s["a_yrt"], NP - 2)
        pe.wait_ge(s["a_rb"], NP * RT)
        for r in range(RT):
            m = pe.transpose(pair(0)[:, r * P:(r + 1) * P], CKV[:, r, :], ID)
        m.then_inc(s["t_nt"], 1)
        pe.wait_ge(s["load_wuk"], 16 * 2 * H)
        pe.wait_ge(s["load_wo"], 16)
        pe.wait_ge(s["a_o"], NP * RT)
        latent_queries(0, 0)
        latent_queries(0, 1)
        def gate_up_half(slot, half, first=False):
            for j in range(2):
                for k in range(KT):
                    if first and j == 0:
                        pe.wait_ge(s["v_ftl"], half * KT + k + 1)
                    m = mm3(bank(4 * slot + 2 * half + j), WH[slot][:, j, k, :], WL[slot][:, j, k, :],
                            FTH[half][:, k, :], FTL[:, k, half * 512:(half + 1) * 512], k == 0, k == KT - 1)
            m.then_inc(s["t_gu"], 1)

        def gate_up(slot, f):
            pe.wait_ge(s["v_gl"], f + 1)
            for half in range(2):
                pe.wait_ge(s["v_ht"], f * 2 + (half - 3))
                gate_up_half(slot, half)

        for t in range(STEPS + TAIL):
            if t < STEPS:
                logits(t)
            if at_block(t, 5) is not None:
                out_projection(at_block(t, 5), 1)
                if t <= STEPS + 1:
                    prob_values(t - 2)
            if 1 <= t <= STEPS:
                prob_transposes(t - 1)
            if 2 <= t <= STEPS + 1 and at_block(t, 5) is None:
                prob_values(t - 2)
            if ql_due(t) is not None:
                latent_queries(*ql_due(t))
            if at_half(t, 3) is not None:
                head_values(at_half(t, 3))
            if t in YR_STEP:
                pair_outputs_transposes(YR_STEP[t])
            if t == STEPS + 5:
                pe.wait_ge(s["v_lm"], STEPS)
                pe.wait_ge(s["v_gl"], 1)
                gate_up_half(0, 0, True)
            if at_block(t, FT_LAG) is not None:
                ffn_transposes(at_block(t, FT_LAG))
            if at_block(t, 4) is not None:
                y_transposes(at_block(t, 4))
                out_projection(at_block(t, 4), 0)

        pe.wait_ge(s["a_tp"], len(tp_use))
        for f, half in PROLOGUE[1:]:
            pe.wait_ge(s["v_gl"], f + 1)
            gate_up_half(f, half, (f, half) == (0, 1))
        pe.wait_ge(s["v_ht"], 3)
        with pe.Fori(1, FT // 2) as i:
            for t in range(2):
                gate_up(t, i * 2 + t)

        def row_product(slot, r, start, stop):
            rs = slice(r * P, (r + 1) * P)
            return mm3(bank(r), HTH[slot][:, rs], HTL[slot][:, rs], DH[slot][:, :], DL[slot][:, :], start, stop)

        def operands(n):
            pe.wait_ge(s["v_dwl"], n + 1)
            pe.wait_ge(s["v_dhl"], n + 1)

        def down(slot, n):
            operands(n)
            for r in range(RT):
                m = row_product(slot, r, False, False)
            m.then_inc(s["t_dn"], 1)

        def down_last_pair(n):
            operands(n)
            for r in range(RT + LEAD):
                if r < RT:
                    row_product(0, r, False, False)
                if r == LEAD:
                    operands(n + 1)
                if r >= LEAD:
                    row_product(1, r - LEAD, False, True).then_inc(s["t_acc"], 1)
            pe.wait_ge(s["t_acc"], 2 * RT)
            pe.sem_inc(s["t_dn"], 2)

        operands(0)
        for r in range(RT):
            if r in (0, RT // 2, RT * 3 // 4):
                pe.wait_ge(s["v_ht"], 2 * FT - (2, 1, 0)[(0, RT // 2, RT * 3 // 4).index(r)])
            m = row_product(0, r, True, False)
        m.then_inc(s["t_dn"], 1)
        down(1, 1)
        with pe.Fori(1, FT // 2 - 1) as i:
            for t in range(2):
                down(t, i * 2 + t)
        down(0, FT - 2)
        operands(FT - 1)
        for r in range(RT):
            row_product(1, r, False, True).then_inc(s["t_acc"], 1)
        pe.wait_ge(s["t_acc"], RT)
        pe.sem_inc(s["t_dn"], 1)

        pe.wait_ge(s["load_pn"], 16)
        for k in range(2):
            pe.wait_ge(s["a_fo"], k + 1)
            pe.wait_ge(s["v_fo"], k + 1)
            for r in range(RT):
                m = pe.transpose(pair(k)[:, r * P:(r + 1) * P], PN[:, r, k * P:(k + 1) * P], ID)
            m.then_inc(s["t_pt"], 1)
        operands(FT)
        for r in list(range(4, RT)) + list(range(4)):
            if r >= 4:
                pe.wait_ge(s["a_fo" if r % 2 == 0 else "v_fo"], r // 2 + 1)
            else:
                pe.wait_ge(s["v_ptl"], r // 2 + 1)
            m = row_product(0, r, True, False)
        m.then_inc(s["t_dn"], 1)
        down(1, FT + 1)
        with pe.Fori(1, FT // 2 - 1) as i:
            for t in range(2):
                down(t, i * 2 + (FT + t))
        down_last_pair(2 * FT - 2)

        def x2_transposes(r):
            pe.wait_ge(s["v_x2"], r + 1)
            if r < 2:
                pe.wait_ge(s["a_fo"], RT // 2 + r + 1)
                pe.wait_ge(s["v_fo"], RT // 2 + r + 1)
            else:
                pe.wait_ge(s["v_x2l"], r - 1)
            for k in range(KT):
                m = pe.transpose(pair(r % 2)[:, k * P:(k + 1) * P], X2[r % 4][:, k * P:(k + 1) * P], ID)
            m.then_inc(s["t_x2"], 1)

        def gate(r):
            if r == 0:
                pe.wait_ge(s["v_wgl"], 2 + KT)
                pe.wait_ge(s["a_fo"], RT)
                pe.wait_ge(s["v_fo"], RT)
            pe.wait_ge(s["v_x2l"], r + 1)
            if r >= 1:
                pe.wait_ge(s["a_sig"], r)
            for dh in range(2):
                ds = slice(dh * 512, (dh + 1) * 512)
                for k in range(KT):
                    m = mm3(pair(2)[:, ds], X2H[r % 2][:, k, :], X2L[r % 2][:, k, :], WG[:, k, 0, ds], WG[:, k, 1, ds],
                            k == 0, k == KT - 1)
            m.then_inc(s["t_gt"], 1)

        def embed(r):
            if r == 0:
                pe.wait_ge(s["v_wgl"], 2)
                pe.wait_ge(s["a_fo"], RT)
                pe.wait_ge(s["v_fo"], RT)
            else:
                pe.wait_ge(s["v_u"], r)
            rs = slice(r * P, (r + 1) * P)
            for dh in range(2):
                ds = slice(dh * 512, (dh + 1) * 512)
                for k in range(2):
                    m = mm3(pair(3)[:, ds], PTH[:, k, rs], PTL[:, k, rs], WUH[:, k, ds], WUL[:, k, ds], k == 0, k == 1)
            m.then_inc(s["t_em"], 1)

        x2_transposes(0)
        embed(0)
        x2_transposes(1)
        for r in range(RT):
            gate(r)
            if r:
                embed(r)
            if r + 2 < RT:
                x2_transposes(r + 2)

    @block.scalar
    def _(act):
        sc = nc.scalar

        def square(r):
            act.wait_ge(load_x[r], 16)
            if r:
                act.wait_ge(s["a_sq"], r)
            sc.activation(pair(3), XN[r][:, :], ACT.Square, accum_out=cols["ss0"][:, r:r + 1]).then_inc(s["a_sq"], 1)

        def x_hi(r):
            act.wait_ge(s["t_xt"], r + 1)
            sc.copy(XTH[:, :, r * P:(r + 1) * P], pair(1 + r % 2).rearrange("p (k c) -> p k c", k=KT))\
              .then_inc(s["a_xh"], 1)

        def w_hi(n):
            c, k = divmod(n, KT)
            act.wait_ge(load_raw[raw_slot(n)], raw_count(n))
            if k == 0 and c >= 2:
                act.wait_ge(s["t_unit"], KT * (c - 1))
            w = width(c)
            sc.copy(WBH[c % 2][:, k, 0:w], RAW[raw_slot(n)][:, 0:w]).then_inc(s["a_whi"], 1)

        def evacuate(g):
            c, u = divmod(g, KT)
            act.wait_ge(s["t_unit"], g + 1)
            o = bank(g % 2)
            m, half = u % 4, u // 4
            if c == 1:
                for h, j in enumerate(HALF):
                    ins = sc.copy(QS[j, 2 * m + h, query_cols(g)], bank(g % 2, unit_width(g))[j, :])
            elif c == 6:
                ins = sc.copy(AQ[:, m, half * 512:(half + 1) * 512], o)
            elif c == 0:
                ins = sc.copy(AC[:, u, :], o[:, 0:SMALL])
            else:
                n, hp = g - 2 * KT, c - 2
                if n == 0:
                    act.wait_ge(s["p_pad"], 2)
                if n >= 2:
                    act.wait_ge(st_ret[n % 2], 16 * (n // 2))
                for j in range(4):
                    col = (QSC if j < 2 else KSC)[:, 2 * hp + j % 2:2 * hp + j % 2 + 1]
                    sc.activation(STG[n % 2][:, j * HD:(j + 1) * HD], o[:, j * HD:(j + 1) * HD], ACT.Copy, scale=col)
                v01 = STG[n % 2][:, RV:RV + 384].rearrange("p (h c) -> p h c", h=2)[:, :, 0:HD]
                sc.copy(v01, o[:, 2 * P:3 * P].rearrange("p (h c) -> p h c", h=2))
                ins = sc.copy(STG[n % 2][:, RG_:RG_ + P], o[:, 3 * P:4 * P])
            ins.then_inc(s["a_ev"], 1)

        for r in range(RT + 5):
            if r < RT:
                square(r)
            if 2 <= r < RT + 2:
                x_hi(r - 2)
            if r < 4:
                w_hi(2 * r)
                w_hi(2 * r + 1)
            elif r < RT + 4:
                w_hi(r + 4)
            if r >= 5:
                evacuate(r - 5)
        act.wait_ge(s["v_ang"], 1)
        sc.activation(SIN[:, :, :], ANR[:, :, :], ACT.Sin).then_inc(s["a_trig"], 1)
        sc.activation(COS[:, :, :], ANK[:, :, :], ACT.Sin).then_inc(s["a_trig"], 1)
        for g in range(KT, 2 * KT):
            w_hi(g + KT)
            evacuate(g)
            if g == KEYS_AT:
                act.wait_ge(s["t_nt"], 1)
                sc.copy(KH[:, :], pair(1)).then_inc(s["a_kh"], 1)

        def relu_scores(n):
            o = pair(1 + n % 2, (B0 + n // H + 1) * P)
            act.wait_ge(s["t_ix"], n + 1)
            sc.activation(o, o, ACT.Relu).then_inc(s["a_rl"], 1)

        for g in range(2 * KT, LAST):
            for n in items(g):
                relu_scores(n)
            if g + KT < LAST:
                w_hi(g + KT)
            evacuate(g)

        def read_pair_bank(n):
            hp, r = divmod(n, RT)
            act.wait_ge(s["t_rb"], n + 1)
            w = 3 * P if r < RT - 1 else 2 * P
            sc.copy(QKT[hp % 2][:, r, 0:w], bank(n % 2, w)).then_inc(s["a_rb"], 1)

        def read_scores(n):
            act.wait_ge(s["t_sc"], n + 1)
            if n >= 2:
                act.wait_ge(s["t_ro"], n - 1)
            b0 = 1024 * (1 + n % 2)
            src = PS[:, b0:b0 + 1024].rearrange("p (h i) -> p h i", h=2)[:, :, 0:P]
            sc.copy(ST[n % 2][:, :].rearrange("p (h i) -> p h i", h=2), src).then_inc(s["a_st"], 1)

        def read_out(n):
            hp, r = divmod(n, RT)
            if r == 0 and hp >= 2:
                act.wait_ge(s["v_y"], hp - 1)
            act.wait_ge(s["t_ro"], n + 1)
            sc.copy(O[hp % 2][:, r, :], bank(6 + n % 2, P)).then_inc(s["a_o"], 1)

        def ret_gate(hp):
            for half in range(2):
                act.wait_ge(load_rp[hp % 2][half], 16 * (hp // 2 + 1))
            if hp >= 2:
                act.wait_ge(s["v_y"], hp - 1)
            sc.activation(SGR[hp % 2][:, :, :], RP[hp % 2][:, :, RG_:RG_ + P], ACT.Silu).then_inc(s["a_silu"], 1)

        def read_ret(hp):
            if hp == 0:
                for i in range(2):
                    act.wait_ge(st_ret[i], 16 * 4 * NP)
            act.wait_ge(s["t_yr"], hp + 1)
            sc.copy(YRT[hp][:, :], pair(0)).then_inc(s["a_yrt"], 1)

        for n in range(RAHEAD):
            read_pair_bank(n)
        for n in range(NP * RT + 1):
            if n + RAHEAD < NP * RT:
                read_pair_bank(n + RAHEAD)
            if n < NP * RT:
                read_scores(n)
            if n >= 1:
                read_out(n - 1)
            if n % RT == 2:
                ret_gate(n // RT)
            if ret_pair_due(n) is not None:
                read_ret(ret_pair_due(n))

        def read_queries(b, half):
            n = ms_at[("ql", b, half)]
            act.wait_ge(s["t_ms"], n + 1)
            if b >= 2:
                act.wait_ge(s["t_lg"], H * (b - 1))
            sc.mul(QL[b % 2][:, 4 * half:4 * half + 4, :], bank(7).rearrange("p (h c) -> p h c", h=4), HD ** -0.5)\
              .then_inc(s["a_ms"], 1)

        def exponent(t):
            b, h = divmod(t, H)
            keys = (b + 1) * P
            act.wait_ge(s["v_lm"], t + 1)
            if h == 0 and b >= 2:
                act.wait_ge(s["v_ms"], 2 * (b - 1))
            c = (b % 2) * H + h
            sc.activation(LM[t % 2][:, 0:keys], LM[t % 2][:, 0:keys], ACT.Exp, scale=-1.0,
                          bias=cols["nmax"][:, t % 4:t % 4 + 1], accum_out=cols["sum"][:, c:c + 1])\
              .then_inc(s["a_ex"], 1)

        def read_probs(t):
            keys = (t // H + 1) * P
            act.wait_ge(s["t_tp"], tp_at[("tr", t)] + 1)
            if t >= 2:
                act.wait_ge(s["t_pv"], t - 1)
            sc.copy(PT[t % 2][:, 0:keys], pair(2, keys)).then_inc(s["a_tp"], 1)

        def read_latent(g):
            act.wait_ge(s["t_pv"], 4 * (g + 1))
            if g >= 2:
                act.wait_ge(s["t_ms"], ms_at[("y", g - 2)] + 1)
            sc.copy(OTS[g % 2][:, :], bank(6)).then_inc(s["a_ots"], 1)

        def read_y(b):
            act.wait_ge(s["t_ms"], ms_at[("yt", b)] + 1)
            if b >= 1:
                act.wait_ge(s["t_tp"], tp_at[("mx", b - 1)] + 1)
            sc.copy(YDT[:, :, :], bank(7).rearrange("p (k c) -> p k c", k=NP)).then_inc(s["a_ms"], 1)

        def read_mix(b):
            act.wait_ge(s["t_tp"], tp_at[("mx", b)] + 1)
            if b >= 1:
                act.wait_ge(s["v_x1"], b)
            sc.copy(MXS[:, :], pair(2)).then_inc(s["a_tp"], 1)

        def mix_square(b):
            act.wait_ge(s["a_tp"], tp_at[("mx", b)] + 1)
            if b >= 1:
                act.wait_ge(s["a_fss"], b)
            sc.activation(JK[:, :], MXS[:, :], ACT.Square, accum_out=cols["ssm"][:, b:b + 1]).then_inc(s["a_mss"], 1)

        def ffn_square(b):
            act.wait_ge(s["v_x1"], b + 1)
            act.wait_ge(s["a_mss"], b + 1)
            sc.activation(JK[:, :], XR[b % 2][:, :], ACT.Square, accum_out=cols["ssf"][:, b:b + 1])\
              .then_inc(s["a_fss"], 1)

        def read_ffn_rows(b):
            act.wait_ge(s["t_tp"], tp_at[("ft", b)] + 1)
            sc.copy(FTR[:, :, b * P:(b + 1) * P], pair(2).rearrange("p (k c) -> p k c", k=KT)).then_inc(s["a_tp"], 1)

        def rows_hi(half, k):
            sc.copy(FTH[half][:, k, :], FTR[:, k, half * 512:(half + 1) * 512]).then_inc(s["a_fth"], 1)

        def gate_hi(slot, f):
            if isinstance(f, int) and f == 1:
                act.wait_ge(load_wr[1], 32)
                act.wait_ge(s["t_tp"], tp_at[("mx", RT - 1)] + 1)
                act.wait_ge(s["v_lm"], STEPS)
            else:
                act.wait_ge(load_wr[slot], (f - slot) * 16 + 32 * slot)
                act.wait_ge(s["t_gu"], f * 2 - (1 if isinstance(f, int) and f == 2 else 2))
            sc.copy(WH[slot][:, :, :, :], WR[slot][:, :, :, :]).then_inc(s["a_gh"], 1)

        def silu_gate(slot, f, half):
            n = PROLOGUE.index((f, half)) if isinstance(f, int) and f < 2 else f * 2 + half
            act.wait_ge(s["t_gu"], n + 1)
            if not (isinstance(f, int) and (f, half) in ((0, 0), (0, 1))):
                act.wait_ge(s["v_ht"], n if isinstance(f, int) and f < 2 else n - 1)
            sc.activation(SG[half][:, :], bank(4 * slot + 2 * half), ACT.Silu).then_inc(s["a_sg"], 1)

        def first_gate_hi(j):
            act.wait_ge(s["load_wf"], 32)
            ins = sc.copy(WH[0][:, j, :, :], WR0[j][:, :, :])
            if j == 1:
                ins.then_inc(s["a_gh"], 1)

        act.wait_ge(s["t_nt"], 2)
        sc.copy(CKVT[:, :], pair(0)).then_inc(s["a_nt"], 1)
        read_queries(0, 0)
        read_queries(0, 1)
        for t in range(STEPS + TAIL):
            if at_block(t, SQ_LAG) is not None:
                ffn_square(at_block(t, SQ_LAG))
            if t < STEPS:
                exponent(t)
            if at_block(t, 5) is not None:
                read_mix(at_block(t, 5))
            if 1 <= t <= STEPS:
                read_probs(t - 1)
            if at_block(t, 5) is not None:
                mix_square(at_block(t, 5))
            if at_half(t, 2) is not None:
                read_latent(at_half(t, 2))
            if ql_due(t) is not None:
                read_queries(*ql_due(t))
            if t in YR_STEP:
                act.wait_ge(s["t_tp"], tp_at[("yr", YR_STEP[t])] + 1)
                sc.copy(YRT[YR_STEP[t]][:, :], pair(2)).then_inc(s["a_tp"], 1)
            if at_block(t, FT_LAG) is not None:
                if t == STEPS + FT_LAG - 1:
                    gate_hi(1, 1)
                read_ffn_rows(at_block(t, FT_LAG))
                if t == STEPS + FT_LAG - 1:
                    silu_gate(0, 0, 0)
            if at_block(t, 4) is not None:
                read_y(at_block(t, 4))
            if STEPS - H <= t < STEPS:
                if t == STEPS - H:
                    act.wait_ge(s["a_tp"], tp_at[("ft", RT // 2 - 1)] + 1)
                    act.wait_ge(s["t_ms"], ms_at[("ql", RT - 1, 1)] + 1)
                rows_hi(0, t - (STEPS - H))
                if t >= STEPS - 2:
                    first_gate_hi(t - (STEPS - 2))

        for k in range(KT):
            if k == 0:
                act.wait_ge(s["st_x1"], 16 * RT)
                act.wait_ge(s["v_fn"], RT)
                act.wait_ge(s["a_tp"], len(tp_use))
            rows_hi(1, k)
        for f, half in PROLOGUE[1:3]:
            silu_gate(f, f, half)
        gate_hi(0, 2)
        silu_gate(1, 1, 1)
        gate_hi(1, 3)
        for half in range(2):
            silu_gate(0, 2, half)
        with act.Fori(2, FT // 2) as i:
            gate_hi(0, i * 2)
            for half in range(2):
                silu_gate(1, i * 2 - 1, half)
            gate_hi(1, i * 2 + 1)
            for half in range(2):
                silu_gate(0, i * 2, half)
        def hidden_hi(slot, f):
            sc.copy(HTH[slot][:, :], HT[:, bass.ds(f, 1), :]).then_inc(s["a_dhh"], 1)

        def down_hi(slot, n, f):
            act.wait_ge(load_dr[slot], (n - slot) * 8 + 16)
            act.wait_ge(s["t_dn"], n - 1)
            sc.copy(DH[slot][:, :], DR[slot][:, :]).then_inc(s["a_dwh"], 1)
            hidden_hi(slot, f)

        def evacuate_even(dst, r, n):
            act.wait_ge(s["t_acc"], n + r + 1)
            sc.copy(dst[:, r, :], bank(r)).then_inc(s["a_fo"], 1)

        def square_into(use, src, col):
            if sq_at[use] >= 2:
                act.wait_ge(s["a_sqs"], sq_at[use] - 1)
            sc.activation(JF[:, 0:src.shape[1]], src, ACT.Square, accum_out=SMF[:, col:col + 1]).then_inc(s["a_sqs"], 1)

        def ffn_out_square(r):
            act.wait_ge(s["a_fo" if r % 2 == 0 else "v_fo"], RT // 2 + r // 2 + 1)
            square_into(("fo1", r), FO1[:, r, :], 2 * r + 1)

        def up_hi(k):
            act.wait_ge(load_wg[k], 16)
            sc.copy(WUH[:, k, :], WGR[k][:, :]).then_inc(s["a_wgh"], 1)

        def ple_gate_hi(slot, k, i):
            act.wait_ge(load_wg[slot], i * 16 + 32)
            act.wait_ge(s["v_dhl"], k * 2 + (FT + 2))
            sc.copy(WG[:, bass.ds(k, 1), 0, :], WGR[slot][:, :].unsqueeze(1)).then_inc(s["a_wgh"], 1)

        silu_gate(1, FT - 1, 0)
        act.wait_ge(s["v_gl"], FT)
        act.wait_ge(s["v_ht"], 4)
        hidden_hi(0, 0)
        act.wait_ge(load_dr[0], 16)
        act.wait_ge(s["t_gu"], 2 * FT - 2)
        sc.copy(DH[0][:, :], DR[0][:, :]).then_inc(s["a_dwh"], 1)
        hidden_hi(1, 1)
        silu_gate(1, FT - 1, 1)
        act.wait_ge(load_dr[1], 16)
        sc.copy(DH[1][:, :], DR[1][:, :]).then_inc(s["a_dwh"], 1)
        act.wait_ge(s["v_ht"], 2 * FT)
        with act.Fori(1, FT // 2) as i:
            for t in range(2):
                down_hi(t, i * 2 + t, i * 2 + t)
        for k in range(2):
            up_hi(k)
        down_hi(0, FT, 0)
        for r in range(0, RT, 2):
            evacuate_even(FO0, r, 0)
        for k in range(2):
            act.wait_ge(s["t_pt"], k + 1)
            sc.copy(PTH[:, k, :], pair(k)).then_inc(s["a_pth"], 1)
        down_hi(1, FT + 1, 1)
        for r in range(RT):
            act.wait_ge(s["a_fo" if r % 2 == 0 else "v_fo"], r // 2 + 1)
            square_into(("fo0", r), FO0[:, r, :], 2 * r)
        with act.Fori(0, DLOOP) as i:
            for t in range(DU):
                down_hi(t % 2, i * DU + (FT + DFIRST + t), i * DU + (DFIRST + t))
                if t % 2 == 1:
                    ple_gate_hi(t // 2, i * 2 + t // 2, i)
        for f in range(FT - 4, FT):
            down_hi(f % 2, FT + f, f)

        def x2_hi(r):
            act.wait_ge(s["t_x2"], r + 1)
            if r >= 2:
                act.wait_ge(s["t_gt"], r - 1)
            sc.copy(X2H[r % 2][:, :, :], pair(r % 2).rearrange("p (k c) -> p k c", k=KT)).then_inc(s["a_x2h"], 1)

        for r in range(0, RT, 2):
            evacuate_even(FO1, r, RT)
            if r < 4:
                ffn_out_square(r // 2)
        x2_hi(0)
        ffn_out_square(2)
        x2_hi(1)
        ffn_out_square(3)
        for r in range(RT):
            if r + 4 < RT:
                ffn_out_square(r + 4)
            act.wait_ge(s["t_gt"], r + 1)
            if r >= 1:
                act.wait_ge(s["v_u"], r)
            sc.activation(SGG[:, :], pair(2), ACT.Sigmoid).then_inc(s["a_sig"], 1)
            if r + 2 < RT:
                x2_hi(r + 2)
            act.wait_ge(s["v_u"], r + 1)
            square_into(("u", r), UU[r % 2][:, :], 32 + r)

    @block.vector
    def _(dve):
        v = nc.vector
        made = [0]

        def link(ins):
            made[0] += 1
            ins.then_inc(s["v_link"], 1)
            dve.wait_ge(s["v_link"], made[0])

        def norm_x(r):
            if r == 0:
                dve.wait_ge(s["load_gin"], 16)
            dve.wait_ge(s["p_rs"], r + 1)
            v.scalar_tensor_tensor(XN[r][:, :], XN[r][:, :], cols["rs0"][:, r:r + 1], GIN[:, :], ALU.mult, ALU.mult)\
             .then_inc(s["v_xn"], 1)

        def x_lo(r):
            dve.wait_ge(s["a_xh"], r + 1)
            rs = slice(r * P, (r + 1) * P)
            v.tensor_tensor(XTL[:, :, rs], pair(1 + r % 2).rearrange("p (k c) -> p k c", k=KT),
                            XTH[:, :, rs].bitcast(F32), ALU.subtract).then_inc(s["v_xl"], 1)

        def query_lo(g):
            dve.wait_ge(s["a_ev"], g + 1)
            for h, (j, i) in enumerate(zip(HALF, HALF[::-1])):
                q = QS[:, 2 * (g % 4) + h, query_cols(g)]
                ins = v.tensor_tensor(q[i, :], bank(g % 2, unit_width(g))[j, :], q[j, :].bitcast(F32), ALU.subtract)
            ins.then_inc(s["v_qlo"], 1)

        def rotation_angles():
            c1, c2, c3 = cody_waite()
            dve.wait_ge(s["load_pos"], 32)
            link(v.tensor_copy(cols["pos"], POSI[:, :]))
            inv_b = INV[:, :].unsqueeze(1).to_broadcast([P, RT, 32])
            link(v.tensor_tensor(ANG[:, :, :], cols["pos"].unsqueeze(2).to_broadcast([P, RT, 32]), inv_b, ALU.mult))
            link(v.tensor_scalar(ANK[:, :, :], ANG[:, :, :], 1.0 / TWO_PI, MAGIC, ALU.mult, ALU.add))
            link(v.tensor_scalar(ANK[:, :, :], ANK[:, :, :], MAGIC, None, ALU.subtract))
            flat = [a[:, :, :].rearrange("p r c -> p (r c)") for a in (ANG, ANK, ANR)]
            link(v.scalar_tensor_tensor(flat[2], flat[1], -c1, flat[0], ALU.mult, ALU.add))
            link(v.scalar_tensor_tensor(flat[2], flat[1], -c2, flat[2], ALU.mult, ALU.add))
            link(v.scalar_tensor_tensor(flat[2], flat[1], -c3, flat[2], ALU.mult, ALU.add))
            link(v.tensor_scalar(flat[0], flat[2], np.pi / 2, None, ALU.add))
            link(v.tensor_scalar(flat[1], flat[0], np.pi, TWO_PI, ALU.is_gt, ALU.mult))
            link(v.tensor_tensor(flat[1], flat[0], flat[1], ALU.subtract))
            link(v.tensor_scalar(flat[1], flat[1], PI_CAP, -PI_CAP, ALU.min, ALU.max))
            v.tensor_scalar(flat[2], flat[2], PI_CAP, -PI_CAP, ALU.min, ALU.max).then_inc(s["v_ang"], 1)

        for r in range(RT + 2):
            if r < RT:
                dve.wait_ge(s["a_sq"], r + 1)
                v.tensor_scalar(cols["v0"][:, r:r + 1], cols["ss0"][:, r:r + 1], 1.0 / D, EPS, ALU.mult, ALU.add)\
                 .then_inc(s["v_var"], 1)
            if 1 <= r <= RT:
                norm_x(r - 1)
            if r >= 2:
                x_lo(r - 2)
            if r == RT:
                rotation_angles()
        def over(col, n):
            return col.unsqueeze(2).to_broadcast([P, RT, n])

        def rows(g, n):
            return g[:, :].unsqueeze(1).to_broadcast([P, RT, n])

        ac, ak = AC[:, :, 0:P], AC[:, :, P:P + HD]

        def key_norms(step):
            if step == 0:
                dve.wait_ge(s["a_ev"], KT)
                dve.wait_ge(s["a_trig"], 2)
                dve.wait_ge(s["load_const"], 48)
                link(v.tensor_reduce(cols["mu"], ak, AX.X, ALU.add))
                link(v.tensor_scalar(cols["mu"], cols["mu"], 1.0 / HD, None, ALU.mult))
                link(v.tensor_tensor(NXM[:, :, :], ak, over(cols["mu"], HD), ALU.subtract))
            elif step == 1:
                link(v.tensor_tensor(NTMP[:, :, 0:HD], NXM[:, :, :], NXM[:, :, :], ALU.mult))
                link(v.tensor_reduce(cols["ssn"][:, 8:16], NTMP[:, :, 0:HD], AX.X, ALU.add))
                link(v.tensor_tensor(NTMP[:, :, :], ac, ac, ALU.mult))
            elif step == 2:
                link(v.tensor_reduce(cols["ssn"][:, 0:8], NTMP[:, :, :], AX.X, ALU.add))
                v.tensor_scalar(cols["vn"][:, 0:8], cols["ssn"][:, 0:8], 1.0 / P, EPS, ALU.mult, ALU.add)
                v.tensor_scalar(cols["vn"][:, 8:16], cols["ssn"][:, 8:16], 1.0 / HD, EPS, ALU.mult, ALU.add)\
                 .then_inc(s["v_nrm"], 1)
                link(v.tensor_scalar(WI[:, :, :], AC[:, :, P + HD:SMALL], H ** -0.5 * HD ** -0.5, None, ALU.mult))
            elif step == 3:
                dve.wait_ge(s["p_nrs"], 1)
                link(v.tensor_tensor(NXM[:, :, :], NXM[:, :, :], over(cols["rsn"][:, 8:16], HD), ALU.mult))
                link(v.tensor_tensor(NXM[:, :, :], NXM[:, :, :], rows(IKG, HD), ALU.mult))
            elif step == 4:
                v.tensor_tensor(KN[:, :, 0:HD], NXM[:, :, :], rows(IKB, HD), ALU.add)
                v.tensor_tensor(KN[:, :, HD:P], NXM[:, :, :], rows(IKB, HD), ALU.add).then_inc(s["v_kn"], 1)
            elif step == 5:
                link(v.tensor_tensor(CKV[:, :, :], ac, over(cols["rsn"][:, 0:8], P), ALU.mult))
                v.tensor_tensor(CKV[:, :, :], CKV[:, :, :], rows(KVG, P), ALU.mult).then_inc(s["v_ac"], 1)
            elif step == 6:
                dve.wait_ge(s["a_kh"], 1)
                v.tensor_tensor(KL[:, :], pair(1), KH[:, :].bitcast(F32), ALU.subtract).then_inc(s["v_kl"], 1)

        for g in range(KT, 2 * KT):
            query_lo(g)
            key_norms(g - KT)

        def add_head(n):
            b, h = B0 + n // H, n % H
            o, sc_b = pair(1 + n % 2, (b + 1) * P), SC[b - B0][:, :]
            dve.wait_ge(s["a_rl"], n + 1)
            if h:
                dve.wait_ge(s["v_acc"], n)
                ins = v.scalar_tensor_tensor(sc_b, o, WI[:, b, h:h + 1], sc_b, ALU.mult, ALU.add)
            else:
                ins = v.tensor_scalar(sc_b, o, WI[:, b, h:h + 1], None, ALU.mult)
            ins.then_inc(s["v_acc"], 1)

        def pick_round(b, first=False):
            sc_b = SC[b - B0][:, :]
            if first:
                dve.wait_ge(s["p_caus"], b - B0 + 1)
            v.max(M8[:, :], sc_b)
            dve.drain()
            v.match_replace(sc_b, M8[:, :], sc_b, PICKED)
            dve.drain()

        def picked_mask(b):
            sc_b = SC[b - B0][:, :]
            v.tensor_scalar(sc_b, sc_b, (NONCAUSAL + PICKED) / 2, MASKED, ALU.is_gt, ALU.mult).then_inc(s["v_mask"], 1)

        def pick_rounds(b, rounds, unroll=UNROLL):
            assert rounds % unroll == 0
            with dve.Fori(0, rounds // unroll):
                for _ in range(unroll):
                    pick_round(b)

        done = 0
        for g in range(IX0, IX0 + ITEMS // PER):
            for j, n in enumerate(items(g)):
                add_head(n)
                if g > IX0 + (H - 1) // PER and done < ROUNDS + UNROLL:
                    for _ in range((1, 1, 2)[j]):
                        pick_round(B0 + done // ROUNDS, done % ROUNDS == 0)
                        done += 1
                        if done % ROUNDS == 0:
                            picked_mask(B0 + done // ROUNDS - 1)
        b = B0 + done // ROUNDS
        pick_rounds(b, ROUNDS - done % ROUNDS)
        picked_mask(b)
        dve.wait_ge(s["p_caus"], b + 1 - B0 + 1)
        pick_rounds(b + 1, ROUNDS)
        picked_mask(b + 1)

        def ret_center(hp):
            o16 = O[hp % 2][:, :, :].rearrange("p r (h e) -> p (r h) e", h=2)
            t16 = PT1[:, :, :].rearrange("p r (h e) -> p (r h) e", h=2)
            if hp == 0:
                dve.wait_ge(s["load_retg"], 32)
            dve.wait_ge(s["a_o"], RT * (hp + 1))
            link(v.tensor_reduce(cols["ssn"], o16, AX.X, ALU.add))
            link(v.tensor_scalar(cols["ssn"], cols["ssn"], 1.0 / HD, None, ALU.mult))
            link(v.tensor_tensor(o16, o16, cols["ssn"].unsqueeze(2).to_broadcast([P, 2 * RT, HD]), ALU.subtract))
            link(v.tensor_tensor(t16, o16, o16, ALU.mult))
            link(v.tensor_reduce(cols["ssn"], t16, AX.X, ALU.add))
            v.tensor_scalar(cols["vn"], cols["ssn"], 1.0 / HD, EPS, ALU.mult, ALU.add).then_inc(s["v_lnv"], 1)

        def ret_scale(hp, step):
            o = O[hp % 2][:, :, :]
            gain = (RG, RB)[step == 2][:, hp * P:(hp + 1) * P].unsqueeze(1).to_broadcast([P, RT, P])
            if step == 0:
                dve.wait_ge(s["p_lnr"], hp + 1)
                o16 = o.rearrange("p r (h e) -> p (r h) e", h=2)
                link(v.tensor_tensor(o16, o16, cols["rsn"].unsqueeze(2).to_broadcast([P, 2 * RT, HD]), ALU.mult))
            elif step < 3:
                link(v.tensor_tensor(o, o, gain, ALU.mult if step == 1 else ALU.add))
            else:
                dve.wait_ge(s["a_silu"], hp + 1)
                if hp >= 1:
                    dve.wait_ge(s["t_yr"], hp)
                v.tensor_tensor(Y[:, :, :], o, SGR[hp % 2][:, :, :], ALU.mult).then_inc(s["v_y"], 1)

        def ret_norm(hp):
            ret_center(hp)
            for step in range(4):
                ret_scale(hp, step)

        dve.wait_ge(s["p_caus"], RT - 3 - B0 + 1)
        pick_rounds(RT - 3, EARLY, EARLY // 2)
        for hp in range(NP - 1):
            ret_norm(hp)
            if hp < NP - 2:
                for _ in range(BETWEEN):
                    pick_round(RT - 3)
        def mask_logits(t):
            b, h = divmod(t, H)
            keys = (b + 1) * P
            if h == 0:
                if b == 0:
                    dve.wait_ge(s["p_tri"], 1)
                elif b >= B0:
                    dve.wait_ge(s["v_mask"], b - B0 + 1)
            mask = SC[b - B0][:, :] if b >= B0 else TRI[:, 2 * P - keys:2 * P]
            dve.wait_ge(s["t_lg"], t + 1)
            if t >= 2:
                dve.wait_ge(s["t_tp"], tp_at[("tr", t - 2)] + 1)
            v.tensor_tensor_reduce(LM[t % 2][:, 0:keys], pair(t % 2, keys), mask, -1.0, 3.0e38, ALU.add, ALU.min,
                                   cols["nmax"][:, t % 4:t % 4 + 1]).then_inc(s["v_lm"], 1)

        def read_head_values(g):
            b, half = divmod(g, 2)
            c = (b % 2) * H + 4 * half
            dve.wait_ge(s["a_ex"], 4 * (g + 1))
            link(v.reciprocal(cols["rsum"][:, c:c + 4], cols["sum"][:, c:c + 4]))
            dve.wait_ge(s["t_ms"], ms_at[("y", g)] + 1)
            if half == 0 and b >= 1:
                dve.wait_ge(s["t_ms"], ms_at[("yt", b - 1)] + 1)
            v.tensor_tensor(YD[:, half * 256:(half + 1) * 256].rearrange("p (h e) -> p h e", h=4),
                            bank(7, 256).rearrange("p (h e) -> p h e", h=4),
                            cols["rsum"][:, c:c + 4].unsqueeze(2).to_broadcast([P, 4, HD]), ALU.mult)\
             .then_inc(s["v_ms"], 1)

        def variance(dst, src, b, n, after, sig):
            dve.wait_ge(s[after], b + 1)
            v.tensor_scalar(cols[dst][:, b:b + 1], cols[src][:, b:b + 1], 1.0 / n, EPS, ALU.mult, ALU.add)\
             .then_inc(s[sig], 1)

        def scale_mix(b):
            if b == 0:
                dve.wait_ge(s["load_gain"], 32)
            dve.wait_ge(s["p_mr"], b + 1)
            link(v.scalar_tensor_tensor(MXS[:, :], MXS[:, :], cols["rsm"][:, b:b + 1], GPO[:, :], ALU.mult, ALU.mult))

        def add_mix(b):
            dve.wait_ge(load_xr[b % 2], 16 * (b // 2 + 1))
            v.tensor_tensor(XR[b % 2][:, :], XR[b % 2][:, :], MXS[:, :], ALU.add).then_inc(s["v_x1"], 1)

        def ffn_norm(b):
            dve.wait_ge(s["p_fr"], b + 1)
            if b >= 1:
                dve.wait_ge(s["t_tp"], tp_at[("ft", b - 1)] + 1)
            v.scalar_tensor_tensor(FN[:, :], XR[b % 2][:, :], cols["rsf"][:, b:b + 1], GPF[:, :], ALU.mult, ALU.mult)\
             .then_inc(s["v_fn"], 1)

        def rows_lo(half, k):
            rs = slice(half * 512, (half + 1) * 512)
            dve.wait_ge(s["a_fth"], half * KT + k + 1)
            v.tensor_tensor(FTL[:, k, rs], FTR[:, k, rs], FTH[half][:, k, :].bitcast(F32), ALU.subtract)\
             .then_inc(s["v_ftl"], 1)

        def gate_lo(slot, f):
            dve.wait_ge(s["a_gh"], f + 1)
            v.tensor_tensor(WL[slot][:, :, :, :], WR[slot][:, :, :, :], WH[slot][:, :, :, :].bitcast(F32),
                            ALU.subtract).then_inc(s["v_gl"], 1)

        def first_gate_lo():
            dve.wait_ge(s["a_gh"], 1)
            for j in range(2):
                ins = v.tensor_tensor(WL[0][:, j, :, :], WR0[j][:, :, :], WH[0][:, j, :, :].bitcast(F32), ALU.subtract)
            ins.then_inc(s["v_gl"], 1)

        def hidden(slot, f, half):
            n = PROLOGUE.index((f, half)) if isinstance(f, int) and f < 2 else f * 2 + half
            dve.wait_ge(s["a_sg"], n + 1)
            v.tensor_tensor(HT[:, bass.ds(f, 1), half * 512:(half + 1) * 512], SG[half][:, :].unsqueeze(1),
                            bank(4 * slot + 2 * half + 1).unsqueeze(1), ALU.mult).then_inc(s["v_ht"], 1)

        for t in range(STEPS + TAIL):
            if t < STEPS:
                mask_logits(t)
            if t == 1:
                ret_center(NP - 1)
            if 3 <= t < 7:
                ret_scale(NP - 1, t - 3)
            if at_block(t, 6) is not None:
                variance("vm", "ssm", at_block(t, 6), D, "a_mss", "v_mv")
            if at_block(t, ADD_LAG) is not None:
                scale_mix(at_block(t, ADD_LAG))
                add_mix(at_block(t, ADD_LAG))
            if at_half(t, 3) is not None:
                read_head_values(at_half(t, 3))
            if at_block(t, FV_LAG) is not None:
                variance("vf", "ssf", at_block(t, FV_LAG), D, "a_fss", "v_fv")
            if at_block(t, FN_LAG) is not None:
                ffn_norm(at_block(t, FN_LAG))
            if STEPS - H <= t < STEPS:
                rows_lo(0, t - (STEPS - H))
            if t == STEPS:
                first_gate_lo()
            if t == STEPS + FT_LAG - 1:
                gate_lo(1, 1)
                hidden(0, 0, 0)
            for _ in range(rounds_beside(t)):
                bb, n = beside.pop(0)
                pick_round(bb, n == 0)
                if n == ROUNDS - 1:
                    picked_mask(bb)
        assert not beside

        for k in range(KT):
            rows_lo(1, k)
        for f, half in PROLOGUE[1:3]:
            hidden(f, f, half)
        gate_lo(0, 2)
        hidden(1, 1, 1)
        gate_lo(1, 3)
        for half in range(2):
            hidden(0, 2, half)
        with dve.Fori(2, FT // 2) as i:
            gate_lo(0, i * 2)
            for half in range(2):
                hidden(1, i * 2 - 1, half)
            gate_lo(1, i * 2 + 1)
            for half in range(2):
                hidden(0, i * 2, half)
        def hidden_lo(slot, n, f):
            dve.wait_ge(s["a_dhh"], n + 1)
            v.tensor_tensor(HTL[slot][:, :].unsqueeze(1), HT[:, bass.ds(f, 1), :],
                            HTH[slot][:, :].bitcast(F32).unsqueeze(1), ALU.subtract).then_inc(s["v_dhl"], 1)

        def weights_lo(slot, n):
            dve.wait_ge(s["a_dwh"], n + 1)
            v.tensor_tensor(DL[slot][:, :], DR[slot][:, :], DH[slot][:, :].bitcast(F32), ALU.subtract)\
             .then_inc(s["v_dwl"], 1)

        def down_lo(slot, n, f):
            weights_lo(slot, n)
            hidden_lo(slot, n, f)

        def evacuate_odd(dst, r, n):
            dve.wait_ge(s["t_acc"], n + r + 1)
            v.tensor_copy(dst[:, r, :], bank(r)).then_inc(s["v_fo"], 1)

        def ple_gate_lo(slot, k):
            dve.wait_ge(s["a_wgh"], k + 3)
            v.tensor_tensor(WG[:, bass.ds(k, 1), 1, :], WGR[slot][:, :].unsqueeze(1),
                            WG[:, bass.ds(k, 1), 0, :].bitcast(F32), ALU.subtract).then_inc(s["v_wgl"], 1)

        hidden(1, FT - 1, 0)
        hidden_lo(0, 0, 0)
        weights_lo(0, 0)
        hidden_lo(1, 1, 1)
        hidden(1, FT - 1, 1)
        weights_lo(1, 1)
        dve.wait_ge(s["v_ht"], 2 * FT)
        with dve.Fori(1, FT // 2) as i:
            for t in range(2):
                down_lo(t, i * 2 + t, i * 2 + t)
        for k in range(2):
            dve.wait_ge(s["a_wgh"], k + 1)
            v.tensor_tensor(WUL[:, k, :], WGR[k][:, :], WUH[:, k, :].bitcast(F32), ALU.subtract).then_inc(s["v_wgl"], 1)
        down_lo(0, FT, 0)
        for r in range(1, RT, 2):
            evacuate_odd(FO0, r, 0)
        for k in range(2):
            dve.wait_ge(s["a_pth"], k + 1)
            v.tensor_tensor(PTL[:, k, :], pair(k), PTH[:, k, :].bitcast(F32), ALU.subtract).then_inc(s["v_ptl"], 1)
        down_lo(1, FT + 1, 1)
        with dve.Fori(0, DLOOP) as i:
            for t in range(DU):
                down_lo(t % 2, i * DU + (FT + DFIRST + t), i * DU + (DFIRST + t))
                if t % 2 == 1:
                    ple_gate_lo(t // 2, i * 2 + t // 2)
        for f in range(FT - 4, FT):
            down_lo(f % 2, FT + f, f)

        def out_variance(r):
            dve.wait_ge(s["a_sqs"], sq_at[("fo1", r)])
            link(v.tensor_tensor(SMF[:, 2 * r:2 * r + 1], SMF[:, 2 * r:2 * r + 1], SMF[:, 2 * r + 1:2 * r + 2], ALU.add))
            v.tensor_scalar(SMF[:, 16 + r:17 + r], SMF[:, 2 * r:2 * r + 1], 1.0 / D, EPS, ALU.mult, ALU.add)\
             .then_inc(s["v_wv"], 1)

        def make_x2(r):
            dve.wait_ge(s["p_wr"], r + 1)
            dve.wait_ge(load_x2[r % 4], 16 * (r // 4 + 1))
            if r == 0:
                dve.wait_ge(s["load_gain2"], 32)
            for dh, fo in enumerate((FO0, FO1)):
                ds = slice(dh * 512, (dh + 1) * 512)
                ins = v.scalar_tensor_tensor(fo[:, r, :], fo[:, r, :], SMF[:, 24 + r:25 + r], GPF2[:, ds],
                                             ALU.mult, ALU.mult)
                link(ins)
                ins = v.tensor_tensor(X2[r % 4][:, ds], X2[r % 4][:, ds], fo[:, r, :], ALU.add)
            ins.then_inc(s["v_x2"], 1)

        def x2_lo(r):
            dve.wait_ge(s["a_x2h"], r + 1)
            v.tensor_tensor(X2L[r % 2][:, :, :], pair(r % 2).rearrange("p (k c) -> p k c", k=KT),
                            X2H[r % 2][:, :, :].bitcast(F32), ALU.subtract).then_inc(s["v_x2l"], 1)

        evacuate_odd(FO1, 1, RT)
        out_variance(0)
        evacuate_odd(FO1, 3, RT)
        out_variance(1)
        evacuate_odd(FO1, 5, RT)
        make_x2(0)
        evacuate_odd(FO1, 7, RT)
        make_x2(1)
        x2_lo(0)
        out_variance(2)
        x2_lo(1)
        make_x2(2)
        out_variance(3)
        for r in range(RT):
            if r + 3 < RT:
                make_x2(r + 3)
            dve.wait_ge(s["a_sig"], r + 1)
            dve.wait_ge(s["t_em"], r + 1)
            if r >= 2:
                dve.wait_ge(st_out[r % 2], 16 * (r // 2))
            v.tensor_tensor(UU[r % 2][:, :], pair(3), SGG[:, :], ALU.mult).then_inc(s["v_u"], 1)
            if r + 2 < RT:
                x2_lo(r + 2)
            dve.wait_ge(s["a_sqs"], sq_at[("u", r)])
            v.tensor_scalar(SMF[:, 40 + r:41 + r], SMF[:, 32 + r:33 + r], 1.0 / D, EPS, ALU.mult, ALU.add)\
             .then_inc(s["v_uv"], 1)
            if r + 4 < RT:
                out_variance(r + 4)
            dve.wait_ge(s["p_ur"], r + 1)
            link(v.scalar_tensor_tensor(UU[r % 2][:, :], UU[r % 2][:, :], SMF[:, 48 + r:49 + r], GPL[:, :],
                                        ALU.mult, ALU.mult))
            v.tensor_tensor(UU[r % 2][:, :], UU[r % 2][:, :], X2[r % 4][:, :], ALU.add).then_inc(s["v_out"], 1)

    @block.gpsimd
    def _(pool):
        g_ = nc.gpsimd
        made = [0]

        def link(ins):
            made[0] += 1
            ins.then_inc(s["p_link"], 1)
            pool.wait_ge(s["p_link"], made[0])

        def rsqrt(dst, src):
            n = src.shape[1]
            return g_.tensor_tensor(dst, src, cols["half"][:, 0:n], ALU.pow)

        def w_lo(n):
            c, k = divmod(n, KT)
            w = width(c)
            pool.wait_ge(s["a_whi"], n + 1)
            g_.tensor_tensor(WBL[c % 2][:, k, 0:w], RAW[raw_slot(n)][:, 0:w], WBH[c % 2][:, k, 0:w].bitcast(F32),
                             ALU.subtract).then_inc(s["p_wlo"], 1)

        link(g_.memset(cols["half"], -0.5))
        for r in range(RT):
            pool.wait_ge(s["v_var"], r + 1)
            rsqrt(cols["rs0"][:, r:r + 1], cols["v0"][:, r:r + 1]).then_inc(s["p_rs"], 1)
            if r < 4:
                w_lo(2 * r)
                w_lo(2 * r + 1)
            else:
                w_lo(r + 4)
        link(g_.memset(TRI[:, :], 0.0))
        g_.affine_select(out=TRI[:, P:2 * P], in_=TRI[:, P:2 * P], compare_op=ALU.is_ge, fill=MASKED, base=0,
                         pattern=[[-1, P]], channel_multiplier=1).then_inc(s["p_tri"], 1)
        for n in range(KT + 4, 3 * KT):
            if n == 2 * KT + 3:
                pool.wait_ge(s["v_nrm"], 1)
                rsqrt(cols["rsn"], cols["vn"]).then_inc(s["p_nrs"], 1)
            w_lo(n)
        pool.wait_ge(s["v_ac"], 1)
        for i in range(2):
            g_.memset(STG[i][:, RV:RG_], 0.0).then_inc(s["p_pad"], 1)

        def causal(b):
            pool.wait_ge(s["v_acc"], H * (b - B0 + 1))
            diag = SC[b - B0][:, b * P:(b + 1) * P]
            g_.affine_select(out=diag, in_=diag, compare_op=ALU.is_ge, fill=NONCAUSAL, base=0,
                             pattern=[[-1, P]], channel_multiplier=1).then_inc(s["p_caus"], 1)

        def rotate(n):
            r = n % RT
            st = STG[n % 2]
            pool.wait_ge(s["a_ev"], 2 * KT + n + 1)
            if n == 0:
                pool.wait_ge(s["a_trig"], 2)
            else:
                pool.wait_ge(s["p_rot"], n)
            x8 = st[:, 0:256].rearrange("p (g c) -> p g c", c=32)
            x4, a4, b4 = (a.rearrange("p (g a c) -> p g a c", a=2, c=32) for a in (st[:, 0:256], RT1[:, :], RT2[:, :]))
            cos8 = COS[:, r, :].unsqueeze(1).to_broadcast([P, 8, 32])
            sin4 = SIN[:, r, :].unsqueeze(1).to_broadcast([P, 4, 32])
            g_.tensor_tensor(RT1[:, :].rearrange("p (g c) -> p g c", c=32), x8, cos8, ALU.mult)
            g_.tensor_tensor(b4[:, :, 0, :], x4[:, :, 1, :], sin4, ALU.mult)
            link(g_.tensor_tensor(b4[:, :, 1, :], x4[:, :, 0, :], sin4, ALU.mult))
            g_.tensor_tensor(x4[:, :, 0, :], a4[:, :, 0, :], b4[:, :, 0, :], ALU.subtract)
            g_.tensor_tensor(x4[:, :, 1, :], a4[:, :, 1, :], b4[:, :, 1, :], ALU.add).then_inc(s["p_rot"], 1)

        for g in range(2 * KT, LAST):
            if g + KT < LAST:
                w_lo(g + KT)
            if g < 6 * KT:
                rotate(g - 2 * KT)
            for n in items(g):
                if n % H == H - 1:
                    causal(B0 + n // H)

        def next_state(n):
            hp, r = divmod(n, RT)
            pool.wait_ge(s["a_rb"], n + 1)
            if r == 0 and hp >= 2:
                pool.wait_ge(s["t_ro"], RT * (hp - 1))
            kv, rs = QKT[hp % 2][:, r, 2 * P:3 * P], RST[hp % 2]
            link(g_.tensor_tensor(rs[:, r + 1, :], rs[:, r, :], kv, ALU.add))
            ins = g_.tensor_tensor(rs[:, r + 1, :], rs[:, r + 1, :], CD[:, hp, :], ALU.mult)
            ins.then_inc(s["p_rst"], 1)
            pool.wait_ge(s["p_rst"], hp * (RT - 1) + r + 1)

        def causal_scores(n):
            pool.wait_ge(s["a_st"], n + 1)
            st = ST[n % 2][:, :].rearrange("p (h i) -> p h i", h=2)
            g_.affine_select(out=st, in_=st, compare_op=ALU.is_ge, fill=0.0, base=0,
                             pattern=[[0, 2], [1, P]], channel_multiplier=-1).then_inc(s["p_st"], 1)

        pool.wait_ge(s["t_unit"], LAST)
        for i in range(2):
            g_.memset(RST[i][:, :, :], 0.0).then_inc(s["p_zero"], 1)
        pool.wait_ge(s["p_zero"], 2)
        pool.wait_ge(s["load_cd"], 16)
        for n in range(SAHEAD):
            next_state(n)
        for n in range(NP * RT):
            hp, r = divmod(n, RT)
            m = n + SAHEAD
            if m < NP * RT and m % RT < RT - 1:
                next_state(m)
            causal_scores(n)
            if r == RT - 2 and hp >= 1:
                pool.wait_ge(s["v_lnv"], hp)
                rsqrt(cols["rsn"], cols["vn"]).then_inc(s["p_lnr"], 1)
            if n == (NP - 1) * RT + 1:
                pool.wait_ge(s["t_ro"], (NP - 1) * RT)
                g_.memset(WUK[:, :, :], 0.0).then_inc(s["p_wz"], 1)
                g_.memset(WUV[:, :, :], 0.0).then_inc(s["p_wz"], 1)
        pool.wait_ge(s["v_lnv"], NP)
        rsqrt(cols["rsn"], cols["vn"]).then_inc(s["p_lnr"], 1)

        for b in range(RT):
            pool.wait_ge(s["v_mv"], b + 1)
            rsqrt(cols["rsm"][:, b:b + 1], cols["vm"][:, b:b + 1]).then_inc(s["p_mr"], 1)
            pool.wait_ge(s["v_fv"], b + 1)
            rsqrt(cols["rsf"][:, b:b + 1], cols["vf"][:, b:b + 1]).then_inc(s["p_fr"], 1)

        def out_rsqrt(r):
            pool.wait_ge(s["v_wv"], r + 1)
            rsqrt(SMF[:, 24 + r:25 + r], SMF[:, 16 + r:17 + r]).then_inc(s["p_wr"], 1)

        for r in range(4):
            out_rsqrt(r)
        for r in range(RT):
            pool.wait_ge(s["v_uv"], r + 1)
            rsqrt(SMF[:, 48 + r:49 + r], SMF[:, 40 + r:41 + r]).then_inc(s["p_ur"], 1)
            if r + 4 < RT:
                out_rsqrt(r + 4)

    ctx.close()


_INS = ["x", "p", "positions", "pre_mix_g", "w_in", "ret_norm_g", "ret_norm_b", "kv_norm_g", "idx_k_norm_g",
        "idx_k_norm_b", "w_uk", "w_uv", "w_out", "post_mix_g", "pre_ffn_g", "w_ffn_gate", "w_ffn_up",
        "w_ffn_down", "post_ffn_g", "w_ple_up", "w_ple_gate", "ple_norm_g"]


def kernel(**inputs):
    import concourse.bacc as bacc
    from concourse.bass_utils import run_bass_kernel_spmd

    nc = bacc.Bacc("TRN2", target_bir_lowering=False, num_devices=1)
    arrays, args = {}, []
    inv_freq, small, decay = shape_tables()
    for name, a in [(n, inputs[n]) for n in _INS] + [("inv_freq", inv_freq), ("small_tab", small), ("decay_tab", decay)]:
        a = np.ascontiguousarray(a)
        arrays[f"in_{name}"] = a
        args.append(nc.dram_tensor(f"in_{name}", a.shape, mybir.dt.from_np(a.dtype), kind="ExternalInput").ap())
    args.append(nc.dram_tensor("out_0", (1, S, D), F32, kind="ExternalOutput").ap())
    args.append(nc.dram_tensor("x1_rows", (S, D), F32, kind="Internal").ap())
    args.append(nc.dram_tensor("ret_rows", (NP, S, RW), F32, kind="Internal").ap())
    build(nc, *args)
    r = run_bass_kernel_spmd(nc, [arrays], core_ids=[0])
    return r.results[0]["out_0"]
```
